# Optimizing a Trainium2 kernel written in Bass

```python
import math
import jax
import jax.numpy as jnp
from jax import lax
import numpy as np

D_MODEL = 1024
BATCH = 1
SEQ = 512
DEPTH = 2
DEC_BATCH = 8
DEC_SEQ = 16
PAST_LEN = 512

CHUNK = 64
N_EVEN = (DEPTH + 1) // 2
N_ODD = DEPTH // 2
HEAD_DIM = 64
MIX_WIDTH = D_MODEL
FOX_WIDTH = MIX_WIDTH // 2
FOX_HEADS = FOX_WIDTH // HEAD_DIM
RW_WIDTH = MIX_WIDTH - FOX_WIDTH
RW_HEADS = RW_WIDTH // HEAD_DIM
W_LORA = 64
A_LORA = 64
G_LORA = 128
FOX_COLS = 3 * FOX_WIDTH + FOX_HEADS
RW_OFF_W = 3 * RW_WIDTH
RW_OFF_A = RW_OFF_W + W_LORA
RW_OFF_G = RW_OFF_A + A_LORA
RW_COLS = RW_OFF_G + G_LORA
EVEN_IN = FOX_COLS + RW_COLS
Q_BLOCK = 128
GM_CHUNK = 128
GM_GROUPS = 8
GM_WIDTH = D_MODEL
GM_GDIM = GM_WIDTH // GM_GROUPS
D_FF = 2816
FFN_RES_SCALE = 0.5
RMS_EPS = 1e-6
LN_EPS = 1e-5
GN_EPS = 64e-5

kernel_name = 'fox_rwkv7_gmlp_streaming_step'

def rms_norm(x, g):
    xf = x.astype(jnp.float32)
    y = xf * lax.rsqrt(jnp.mean(xf * xf, axis=-1, keepdims=True) + RMS_EPS)
    return (y * g.astype(jnp.float32)).astype(x.dtype)

def layer_norm(x, g, b):
    xf = x.astype(jnp.float32)
    m = jnp.mean(xf, axis=-1, keepdims=True)
    var = jnp.mean(jnp.square(xf - m), axis=-1, keepdims=True)
    y = (xf - m) * lax.rsqrt(var + LN_EPS)
    return (y * g.astype(jnp.float32) + b.astype(jnp.float32)).astype(x.dtype)

def swiglu(h, w_in, w_out):
    gate, up = jnp.split(h @ w_in, 2, axis=-1)
    return (jax.nn.silu(gate) * up) @ w_out

def macaron_half(x, g_pre, g_post, w_in, w_out):
    return x + FFN_RES_SCALE * rms_norm(swiglu(rms_norm(x, g_pre), w_in, w_out), g_post)

def fox_block(q, k, v, cq, ck, qpos, kpos):
    s = jnp.einsum('bqhd,bkhd->bhqk', q, k).astype(jnp.float32) * (HEAD_DIM ** -0.5)
    bias = jnp.swapaxes(cq, 1, 2)[..., :, None] - jnp.swapaxes(ck, 1, 2)[..., None, :]
    mask = kpos[None, :] <= qpos[:, None]
    p = jax.nn.softmax(jnp.where(mask, s + bias, -jnp.inf), axis=-1)
    return jnp.einsum('bhqk,bkhd->bqhd', p.astype(v.dtype), v)

def fox_prompt(q, k, v, logf):
    t_len = q.shape[1]
    c = jnp.cumsum(logf, axis=1)
    pos = jnp.arange(t_len)
    outs = []
    for i in range(t_len // Q_BLOCK):
        lo, hi = i * Q_BLOCK, (i + 1) * Q_BLOCK
        outs.append(fox_block(q[:, lo:hi], k[:, :hi], v[:, :hi], c[:, lo:hi], c[:, :hi], pos[lo:hi], pos[:hi]))
    return jnp.concatenate(outs, axis=1)

def fox_sample(q, k, v, logf, ck, cv, clogf):
    p_len = ck.shape[1]
    t_len = q.shape[1]
    k_all = jnp.concatenate([ck.astype(k.dtype), k], axis=1)
    v_all = jnp.concatenate([cv.astype(v.dtype), v], axis=1)
    c = jnp.cumsum(jnp.concatenate([clogf.astype(jnp.float32), logf], axis=1), axis=1)
    pos = jnp.arange(p_len + t_len)
    return fox_block(q, k_all, v_all, c[:, p_len:], c, pos[p_len:], pos)

def rwkv7_scan(s0, r, w, k, v, a_, b_):
    def step(s, inp):
        r_t, w_t, k_t, v_t, a_t, b_t = inp
        sa = jnp.einsum('bhij,bhj->bhi', s, a_t)
        s = s * w_t[:, :, None, :] + sa[..., :, None] * b_t[:, :, None, :] + v_t[..., :, None] * k_t[:, :, None, :]
        return s, jnp.einsum('bhij,bhj->bhi', s, r_t)
    xs = tuple(jnp.swapaxes(t, 0, 1) for t in (r, w, k, v, a_, b_))
    s_fin, ys = lax.scan(step, s0, xs)
    return s_fin, jnp.swapaxes(ys, 0, 1)

def even_mixer(h, w_in, fox_bf, rw_mu, rw_w0, rw_w2, rw_a0, rw_a2, rw_g2, rw_kk, rw_ka, rw_rk,
               rw_ln_g, rw_ln_b, w_out, past):
    f32 = jnp.float32
    bsz, t_len, _ = h.shape
    proj = h @ w_in
    pf = proj[..., :FOX_COLS]
    pr = proj[..., FOX_COLS:]
    fh = lambda t: t.reshape(bsz, t_len, FOX_HEADS, HEAD_DIM)
    q = fh(pf[..., :FOX_WIDTH])
    k = fh(pf[..., FOX_WIDTH:2 * FOX_WIDTH])
    v = fh(pf[..., 2 * FOX_WIDTH:3 * FOX_WIDTH])
    logf = jax.nn.log_sigmoid(pf[..., 3 * FOX_WIDTH:].astype(f32) + fox_bf.astype(f32))
    if past is None:
        o_fox = fox_prompt(q, k, v, logf)
        prev = jnp.zeros((bsz, 1, RW_COLS), pr.dtype)
        s0 = jnp.zeros((bsz, RW_HEADS, HEAD_DIM, HEAD_DIM), f32)
    else:
        ck, cv, clogf, s_in, prev = past
        o_fox = fox_sample(q, k, v, logf, ck, cv, clogf)
        s0 = s_in.astype(f32)
    prev_seq = jnp.concatenate([prev.astype(pr.dtype), pr[:, :-1]], axis=1)
    xm = pr + (prev_seq - pr) * rw_mu
    r = xm[..., :RW_WIDTH].astype(f32)
    kx = xm[..., RW_WIDTH:2 * RW_WIDTH].astype(f32)
    vx = xm[..., 2 * RW_WIDTH:RW_OFF_W].astype(f32)
    dw = xm[..., RW_OFF_W:RW_OFF_A]
    da = xm[..., RW_OFF_A:RW_OFF_G]
    dg = xm[..., RW_OFF_G:]
    w_log = -jax.nn.softplus(-(rw_w0 + jnp.tanh(dw) @ rw_w2).astype(f32)) - 0.5
    decay = jnp.exp(-jnp.exp(w_log))
    a = jax.nn.sigmoid((rw_a0 + da @ rw_a2).astype(f32))
    g = (jax.nn.sigmoid(dg) @ rw_g2).astype(f32)
    rh = lambda t: t.reshape(bsz, t_len, RW_HEADS, HEAD_DIM)
    kk = rh(kx * rw_kk.astype(f32))
    kk = kk / jnp.maximum(jnp.linalg.norm(kk, axis=-1, keepdims=True), 1e-12)
    k_mod = rh(kx * (1.0 + (a - 1.0) * rw_ka.astype(f32)))
    r_h = rh(r)
    v_h = rh(vx)
    s_fin, y = rwkv7_scan(s0, r_h, rh(decay), k_mod, v_h, -kk, kk * rh(a))
    ym = jnp.mean(y, axis=-1, keepdims=True)
    yv = jnp.mean(jnp.square(y - ym), axis=-1, keepdims=True)
    y = ((y - ym) * lax.rsqrt(yv + GN_EPS)).reshape(bsz, t_len, RW_WIDTH)
    y = y * rw_ln_g.astype(f32) + rw_ln_b.astype(f32)
    bonus = jnp.sum(r_h * k_mod * rw_rk.astype(f32), axis=-1, keepdims=True) * v_h
    y = (y + bonus.reshape(bsz, t_len, RW_WIDTH)) * g
    mixed = jnp.concatenate([o_fox.reshape(bsz, t_len, FOX_WIDTH), y.astype(h.dtype)], axis=-1)
    out = mixed @ w_out
    new_state = (k, v, logf.astype(h.dtype), s_fin.astype(h.dtype), pr[:, -1:])
    return out, new_state

def odd_mixer(h, w_in, ln_g, ln_b, w_s, b_s, w_out, is_prompt):
    bsz, t_len, _ = h.shape
    u, v = jnp.split(jax.nn.gelu(h @ w_in, approximate=False), 2, axis=-1)
    v = layer_norm(v, ln_g, ln_b)
    cpos = jnp.arange(GM_CHUNK) // CHUNK
    wm = jnp.where(cpos[None, :] <= cpos[:, None], w_s, 0.0).astype(v.dtype)
    if is_prompt:
        vg = v.reshape(bsz, t_len // GM_CHUNK, GM_CHUNK, GM_GROUPS, GM_GDIM)
        sp = jnp.einsum('gts,bnsgc->bntgc', wm, vg) + b_s.T[None, None, :, :, None]
    else:
        vg = v.reshape(bsz, t_len, GM_GROUPS, GM_GDIM)
        sp = jnp.einsum('gts,bsgc->btgc', wm[:, :t_len, :t_len], vg) + b_s[:, :t_len].T[None, :, :, None]
    sp = sp.reshape(bsz, t_len, GM_WIDTH).astype(u.dtype)
    return (u * sp) @ w_out, v

def setup_inputs(seed: int = 0) -> dict:
    key = jax.random.key(seed)
    ks = jax.random.split(key, 32)
    f32 = jnp.float32
    nrm = lambda i, shape, scale: jax.random.normal(ks[i], shape, f32) * scale
    return {
        'x_prompt': nrm(0, (BATCH, SEQ, D_MODEL), 1.0),
        'x_sample': nrm(1, (DEC_BATCH, DEC_SEQ, D_MODEL), 1.0),
        'cache_fox_k': nrm(2, (N_EVEN, DEC_BATCH, PAST_LEN, FOX_HEADS, HEAD_DIM), 1.0),
        'cache_fox_v': nrm(3, (N_EVEN, DEC_BATCH, PAST_LEN, FOX_HEADS, HEAD_DIM), 1.0),
        'cache_fox_logf': jax.nn.log_sigmoid(nrm(4, (N_EVEN, DEC_BATCH, PAST_LEN, FOX_HEADS), 1.0) + 2.0),
        'state_rwkv': nrm(5, (N_EVEN, DEC_BATCH, RW_HEADS, HEAD_DIM, HEAD_DIM), 1.0),
        'state_rwkv_shift': nrm(6, (N_EVEN, DEC_BATCH, 1, RW_COLS), 1.0),
        'norm_g': 1.0 + nrm(7, (DEPTH, 6, D_MODEL), 0.05),
        'ffn_w_in': nrm(8, (DEPTH, 2, D_MODEL, 2 * D_FF), D_MODEL ** -0.5),
        'ffn_w_out': nrm(9, (DEPTH, 2, D_FF, D_MODEL), D_FF ** -0.5),
        'even_w_in': nrm(10, (N_EVEN, D_MODEL, EVEN_IN), D_MODEL ** -0.5),
        'fox_bf': 2.0 + nrm(11, (N_EVEN, FOX_HEADS), 0.5),
        'rw_mu': jax.random.uniform(ks[12], (N_EVEN, RW_COLS), f32, 0.0, 1.0),
        'rw_w0': jax.random.uniform(ks[13], (N_EVEN, RW_WIDTH), f32, -6.0, -1.0),
        'rw_w2': nrm(14, (N_EVEN, W_LORA, RW_WIDTH), W_LORA ** -0.5),
        'rw_a0': nrm(15, (N_EVEN, RW_WIDTH), 0.1),
        'rw_a2': nrm(16, (N_EVEN, A_LORA, RW_WIDTH), A_LORA ** -0.5),
        'rw_g2': nrm(17, (N_EVEN, G_LORA, RW_WIDTH), G_LORA ** -0.5),
        'rw_kk': 0.85 + nrm(18, (N_EVEN, RW_WIDTH), 0.05),
        'rw_ka': 1.0 + nrm(19, (N_EVEN, RW_WIDTH), 0.05),
        'rw_rk': nrm(20, (N_EVEN, RW_HEADS, HEAD_DIM), 0.1),
        'rw_ln_g': 1.0 + nrm(21, (N_EVEN, RW_WIDTH), 0.05),
        'rw_ln_b': nrm(22, (N_EVEN, RW_WIDTH), 0.02),
        'even_w_out': nrm(23, (N_EVEN, MIX_WIDTH, D_MODEL), MIX_WIDTH ** -0.5),
        'gm_w_in': nrm(24, (N_ODD, D_MODEL, 2 * GM_WIDTH), D_MODEL ** -0.5),
        'gm_ln_g': 1.0 + nrm(25, (N_ODD, GM_WIDTH), 0.05),
        'gm_ln_b': nrm(26, (N_ODD, GM_WIDTH), 0.02),
        'gm_w_s': nrm(27, (N_ODD, GM_GROUPS, GM_CHUNK, GM_CHUNK), GM_CHUNK ** -0.5),
        'gm_b_s': 1.0 + nrm(28, (N_ODD, GM_GROUPS, GM_CHUNK), 0.1),
        'gm_w_out': nrm(29, (N_ODD, GM_WIDTH, D_MODEL), GM_WIDTH ** -0.5),
    }

def reference(x_prompt, x_sample, cache_fox_k, cache_fox_v, cache_fox_logf, state_rwkv, state_rwkv_shift,
              norm_g, ffn_w_in, ffn_w_out, even_w_in, fox_bf, rw_mu, rw_w0, rw_w2, rw_a0, rw_a2, rw_g2,
              rw_kk, rw_ka, rw_rk, rw_ln_g, rw_ln_b, even_w_out, gm_w_in, gm_ln_g, gm_ln_b, gm_w_s,
              gm_b_s, gm_w_out):
    xp, xs = x_prompt, x_sample
    fk_p, fv_p, fl_p, rs_p, rsh_p = [], [], [], [], []
    fk_s, fv_s, fl_s, rs_s, rsh_s = [], [], [], [], []
    gv_s = []
    for layer in range(DEPTH):
        j = layer // 2
        ng = norm_g[layer]
        xp = macaron_half(xp, ng[0], ng[1], ffn_w_in[layer, 0], ffn_w_out[layer, 0])
        xs = macaron_half(xs, ng[0], ng[1], ffn_w_in[layer, 0], ffn_w_out[layer, 0])
        if layer % 2 == 0:
            ew = (even_w_in[j], fox_bf[j], rw_mu[j], rw_w0[j], rw_w2[j], rw_a0[j], rw_a2[j], rw_g2[j],
                  rw_kk[j], rw_ka[j], rw_rk[j], rw_ln_g[j], rw_ln_b[j], even_w_out[j])
            mp, stp = even_mixer(rms_norm(xp, ng[2]), *ew, None)
            ms, sts = even_mixer(rms_norm(xs, ng[2]), *ew,
                                 (cache_fox_k[j], cache_fox_v[j], cache_fox_logf[j], state_rwkv[j], state_rwkv_shift[j]))
            for lst, val in zip((fk_p, fv_p, fl_p, rs_p, rsh_p), stp):
                lst.append(val)
            for lst, val in zip((fk_s, fv_s, fl_s, rs_s, rsh_s), sts):
                lst.append(val)
        else:
            ow = (gm_w_in[j], gm_ln_g[j], gm_ln_b[j], gm_w_s[j], gm_b_s[j], gm_w_out[j])
            mp, _ = odd_mixer(rms_norm(xp, ng[2]), *ow, True)
            ms, v_new = odd_mixer(rms_norm(xs, ng[2]), *ow, False)
            gv_s.append(v_new)
        xp = xp + rms_norm(mp, ng[3])
        xs = xs + rms_norm(ms, ng[3])
        xp = macaron_half(xp, ng[4], ng[5], ffn_w_in[layer, 1], ffn_w_out[layer, 1])
        xs = macaron_half(xs, ng[4], ng[5], ffn_w_in[layer, 1], ffn_w_out[layer, 1])
    return (xp, xs,
            jnp.stack(fk_p), jnp.stack(fv_p), jnp.stack(fl_p), jnp.stack(rs_p), jnp.stack(rsh_p),
            jnp.stack(fk_s), jnp.stack(fv_s), jnp.stack(fl_s), jnp.stack(rs_s), jnp.stack(rsh_s),
            jnp.stack(gv_s))


_drawn_inputs = setup_inputs


def setup_inputs(seed=0):
    import zlib

    import numpy as np

    out = dict(_drawn_inputs(seed))
    spreads = {}
    factors = {'rw_ln_b': 4.055, 'gm_ln_b': 2.805}
    for name, (base, spread) in spreads.items():
        noise = np.random.default_rng([zlib.crc32(name.encode()), seed]).standard_normal(out[name].shape)
        drawn = base * np.exp(spread * noise) if base else spread * noise
        out[name] = jnp.asarray(drawn.astype(out[name].dtype))
    for name, factor in factors.items():
        out[name] = (out[name] * factor).astype(out[name].dtype)
    return out
```

```python
import math
from contextlib import ExitStack

import concourse.bass as bass
from concourse import mybir

F32 = mybir.dt.float32
F32R = mybir.dt.float32r
ALU = mybir.AluOpType
ACT = mybir.ActivationFunctionType
AX = mybir.AxisListType.X

P = 128
D = 1024
KD = D // P
SEQ = 512
NSEQ, NEW = 8, 16
TT = SEQ // P + NSEQ * NEW // P
TOK = TT * P
HALF = TOK // 2
D_FF = 2816
FF_CHUNKS = 2
FF_K = D_FF // P // FF_CHUNKS
OUT_N = D // 512
FOXH, HEAD = 8, 64
FOXW = FOXH * HEAD
FOXC = 3 * FOXW + FOXH
RMS_EPS = 1e-6
LN_EPS = 1e-5
GN_EPS = 64e-5

EVEN_BANKS = (4, 5, 6, 7, 0)
ODD_BANKS = (1, 2, 3, 4, 5)
NORM_BANKS = (6, 4)

FFN = (FF_CHUNKS * FF_K, FF_CHUNKS * OUT_N * FF_K, FF_CHUNKS * OUT_N)
STAGES = {"ffn0": FFN, "even_in": (11, KD, 1), "even_out": (0, OUT_N * KD, OUT_N), "ffn1": FFN, "ffn2": FFN,
          "gm_in": (KD // 2, OUT_N * KD, OUT_N), "gm_out": (0, OUT_N * KD, OUT_N), "ffn3": FFN, "end": (0, 0, 0)}

ATT = {"tri_ones": 512, "tri_streams": P, "causal": P, "sel8": FOXH, "minus_ones": P,
       "minus_heads": P}


def columns(table):
    at, out = 0, {}
    for name, n in table.items():
        out[name] = slice(at, at + n)
        at += n
    return out, at


ATT_AT, ATT_N = columns(ATT)


RW_DVE = {
    "prompt": """
        diff mix xm kkr sig_g e scan eex a ka kmod rk rkr floor inverse kk abar kka rbar khat bhat
        bonus p_end0 p_end1 gram0 gram1 gram2 gram3 gram4 gram5 gram6 gram7 q_first q_unit tn2 qn2
        tn3 qn3 tn4 qn4 tn5 qn5 qn6 sadd0 s0 sadd1 s1 yc y_inverse yn y_gain y_shift y_bonus y_gate
        lo
    """.split(),
    "streams": """
        diff diff0 mix xm clear kkr sig_g e scan eex a ka kmod rk rkr floor inverse kk abar kka rbar
        khat bhat bonus p_end gram0 gram1 gram2 gram3 gram4 gram5 gram6 gram7 q_first q_unit tn2 qn2
        tn3 qn3 qn4 yt0 yt1 yc y_inverse yn y_gain y_shift y_bonus y_gate lo sadd0 s0 sadd1 s1 sadd2
        s2 sadd3 s3 sadd4 s4 sadd5 s5 sadd6 s6 sadd7 s7
    """.split(),
}
RW_ACT = {
    "prompt": """
        tanh_w tanh_g sig_w sig_a gate kk_sq p p_inv p_ex root b_tok k_tok v_tok t_first y1_2 y1_3
        y1_4 y1_5 y1_6 r0 u0 r1 u1 yt0 yt1 y_sq y_root hi
    """.split(),
    "streams": """
        prompt_state tanh_w tanh_g sig_w sig_a gate kk_sq p p_inv p_ex root b_tok k_tok v_tok
        t_first y1_2 y1_3 y1_4 turn0 turn1 turn2 turn3 turn4 turn5 turn6 turn7 r1t y0 r u y_sq
        y_root hi out0 out1 out2 out3 out4 out5 out6 out7
    """.split(),
}
RW_PE = {
    "prompt": """
        lora norm bonus turn gram0 gram1 gram2 gram3 gram4 gram5 gram6 gram7 q_turn y1_2 tn2 qn2
        y1_3 tn3 qn3 y1_4 tn4 qn4 y1_5 tn5 qn5 y1_6 qn6 r0 u0 s0 r1 u1 y s1 mean var
    """.split(),
    "streams": """
        prompt_state lora norm bonus turn gram0 gram1 gram2 gram3 gram4 gram5 gram6 gram7 q_turn
        y1_2 tn2 qn2 y1_3 tn3 qn3 y1_4 qn4 turn0 turn1 turn2 turn3 turn4 turn5 turn6 turn7 ra r u y
        mean var s0 s1 s2 s3 s4 s5 s6 s7 out0 out1 out2 out3 out4 out5 out6 out7
    """.split(),
}
RW_POOL = {
    "prompt": """
        lt2 lt3 lt4 lt5 lt6
    """.split(),
    "streams": """
        lt2 lt3 lt4 spread0_0 spread0_1 spread1_0 spread1_1 spread2_0 spread2_1 spread3_0 spread3_1
        spread4_0 spread4_1 spread5_0 spread5_1 spread6_0 spread6_1 spread7_0 spread7_1
    """.split(),
}

RWC = {"tril_p": 2 * P, "tril_s": 2 * P, "levels": 6 * P, "two_heads": P, "reset_p": 512, "reset_s": 512,
       "stream_rows": NSEQ}
RWC_AT, RWC_N = columns(RWC)


def before(stage, what):
    total = 0
    for name, counts in STAGES.items():
        if name == stage:
            return total
        total += counts[what]
    raise KeyError(stage)


def build(nc, io):
    ctx = ExitStack()
    with ctx:
        def sb(name, shape, dt=F32):
            return ctx.enter_context(nc.sbuf_tensor(name, shape, dt))

        def sem(name):
            return ctx.enter_context(nc.semaphore(name))

        x = sb("x", [P, TT, D])
        y = sb("y", [P, TT, D])
        act_hi = sb("act_hi", [P, KD, TOK], F32R)
        act_lo = sb("act_lo", [P, KD, TOK], F32R)
        pair_raw = [sb(f"pair_raw{i}", [P, KD, P]) for i in range(2)]
        pair_hi = [sb(f"pair_hi{i}", [P, KD, P], F32R) for i in range(2)]
        pair_lo = [sb(f"pair_lo{i}", [P, KD, P], F32R) for i in range(2)]
        row_raw = [sb(f"row_raw{i}", [P, 512]) for i in range(2)]
        row_hi = [sb(f"row_hi{i}", [P, 512], F32R) for i in range(2)]
        row_lo = [sb(f"row_lo{i}", [P, 512], F32R) for i in range(2)]
        norm_buf = sb("norm_buf", [P, 4 * D])
        g_post, g_pre = norm_buf[:, 0:D], norm_buf[:, D:2 * D]
        squares = [norm_buf[:, 2 * D:3 * D], norm_buf[:, 3 * D:4 * D]]
        xn_buf = sb("xn_buf", [P, 2 * D])
        xn = [xn_buf[:, 0:D], xn_buf[:, D:2 * D]]
        stat = sb("stat", [P, 6, TT])
        ident = sb("ident", [P, P])
        ones = sb("ones", [P, P])
        eps = sb("eps", [P, 4])
        with ExitStack() as ffn:
            hid_hi = ffn.enter_context(nc.sbuf_tensor("hid_hi", [P, FF_K, TOK], F32R))
            hid_lo = ffn.enter_context(nc.sbuf_tensor("hid_lo", [P, FF_K, TOK], F32R))
            silu = ffn.enter_context(nc.sbuf_tensor("silu", [P, 2, HALF], F32))
            hid = ffn.enter_context(nc.sbuf_tensor("hid", [P, 2, HALF], F32))
        with ExitStack() as even:
            def eb(name, shape, dt=F32):
                return even.enter_context(nc.sbuf_tensor(name, shape, dt))

            rw = eb("rw", [P, 14, 1 + TOK])
            last_cols = eb("last_cols", [P, 14, 9])
            logf = eb("logf", [P, TT, FOXH])
            with ExitStack() as fox:
                def fb(name, shape, dt=F32):
                    return fox.enter_context(nc.sbuf_tensor(name, shape, dt))

                qk = fb("qk", [P, 8, TOK])
                vtok = fb("vtok", [P, TT, FOXW])
                att_const = fb("att_const", [P, ATT_N])
                rmax, nmax = fb("rmax", [P, 8]), fb("nmax", [P, 8])
                esum, rsum = fb("esum", [P, 8]), fb("rsum", [P, 8])
                f_raw = fb("f_raw", [P, KD, FOXH])
                f_hi = fb("f_hi", [P, KD, FOXH], F32R)
                f_lo = fb("f_lo", [P, KD, FOXH], F32R)
                f_tmp = fb("f_tmp", [P, TT, FOXH])
                bf_all = fb("bf_all", [P, FOXH])
                v_pair = fb("v_pair", [P, 4, P])
                k_pair = fb("k_pair", [P, 1, SEQ])
                f_cache = [fb(f"f_cache{i}", [P, 4, FOXH]) for i in range(2)]
                q_rows = fb("q_rows", [P, 656])
            with ExitStack() as wkv:
                def wb(name, shape, dt=F32):
                    return wkv.enter_context(nc.sbuf_tensor(name, shape, dt))

                rw_const = wb("rw_const", [P, RWC_N])
                par = wb("par", [P, 34])
                shift = wb("shift", [P, NSEQ * 14])
                lora_wa, lora_g = wb("lora_wa", [P, 512]), wb("lora_g", [P, 512])
                bias_rows = wb("bias_rows", [33, 512])
                xm = wb("xm", [P, 14, P])
                tanh_w, sig_g = wb("tanh_w", [P, P]), wb("sig_g", [P, P])
                gate, bonus_buf = wb("gate", [P, 512]), wb("bonus", [P, 512])
                state = [wb(f"state{i}", [P, 512]) for i in range(2)]
                decay_mask = [wb(f"decay_mask{i}", [P, 512]) for i in range(2)]
                yc, ysq = wb("yc", [P, 512]), wb("ysq", [P, 512])
                prompt_state = wb("prompt_state", [P, 512])
                p_end = wb("p_end", [P, 4 * NSEQ])
        with ExitStack() as odd:
            def ob(name, shape):
                return odd.enter_context(nc.sbuf_tensor(name, shape, F32))

            u_cols = ob("u_cols", [P, KD, TOK])
            ws, ws_t = ob("ws", [P, KD, P]), ob("ws_t", [P, KD, P])
            ws_new, ws_new_t = ob("ws_new", [P, KD, P]), ob("ws_new_t", [P, KD, P])
            ln_g, ln_b = ob("ln_g", [P, D]), ob("ln_b", [P, D])
            bs, bs_new = ob("bs", [1, KD, P]), ob("bs_new", [1, KD, P])
            ln_stat = ob("ln_stat", [P, 6, TT])
        gated = [xn[i].rearrange("p (g t) -> p g t", t=P) for i in range(2)]
        att = {n: att_const[:, ATT_AT[n]] for n in ATT}
        tri_ones, tri_streams, causal, sel8 = (att[n] for n in ("tri_ones", "tri_streams", "causal", "sel8"))
        sel8 = sel8[0:FOXH]
        minus_ones, minus_heads = att["minus_ones"], att["minus_heads"][0:FOXH]
        yflat = y[:, :, :].rearrange("p t d -> p (t d)")
        ktok = yflat[:, 0:TT * FOXW].rearrange("p (t c) -> p t c", c=FOXW)
        last_rows = yflat[0:9, 2560:2560 + 14 * P]
        q_pair = yflat[:, 4352:4864]
        c_heads = norm_buf[0:FOXH, :].rearrange("p (h c) -> p h c", c=SEQ)
        prob = [xn_buf[:, 1024 * i:1024 * i + 512] for i in range(2)]
        prob_t = [xn_buf[:, 1024 * i + 512:1024 * i + 1024] for i in range(2)]
        v_cache = [yflat[:, 2048 * i:2048 * i + 2048].rearrange("p (a c) -> p a c", c=FOXW) for i in range(2)]
        k_cache = [norm_buf[:, 2048 * i:2048 * i + 2048].rearrange("p (a c) -> p a c", c=FOXW) for i in range(2)]
        new_mask = yflat[:, 4096:5120].rearrange("p (b c) -> p b c", c=P)
        kt_cache = [pair_raw[i][:, :, :].rearrange("p (a k) c -> p a (k c)", a=2) for i in range(2)]
        prob2, prob_t2 = xn_buf[:, 0:TOK], xn_buf[:, TOK:2 * TOK]
        c_stream = xn_buf[0:FOXH, 2 * TOK:3 * TOK]

        rwc = {n: rw_const[:, RWC_AT[n]] for n in RWC}
        tril_p, tril_s, two_heads, reset_p, reset_s, stream_rows = (rwc[n] for n in (
            "tril_p", "tril_s", "two_heads", "reset_p", "reset_s", "stream_rows"))

        def level_mask(lv):
            return rwc["levels"][:, (lv - 1) * P:lv * P]

        par_rows, shift_rows = yflat[0:34, 0:P], yflat[0:NSEQ * 14, P:2 * P]
        t0, t1, t2, t3, t4, t5, t6, t7, t8, t9 = (yflat[:, 512 * i:512 * i + 512] for i in range(10))
        gram = yflat[:, 0:4096].rearrange("p (h c) -> p h c", h=8)
        t_inv = yflat[:, 4096:5120]
        q_inv, y1, lt_m = (norm_buf[:, D * i:D * i + D] for i in range(3))
        ar = norm_buf[:, 3 * D:4 * D].rearrange("p (k a c) -> p k a c", k=4, a=2)
        bT, kT, b_tok, k_tok = (xn_buf[:, 512 * i:512 * i + 512] for i in range(4))
        raw0, raw1 = (pair_raw[i][:, :, :].rearrange("p k c -> p (k c)") for i in range(2))
        r1, u_tok, v_tok, y_t = raw0[:, 0:512], raw0[:, 512:1024], raw1[:, 0:512], raw1[:, 512:1024]
        r1t, y0_t = decay_mask[0][:, :], decay_mask[1][:, :]
        bonus = bonus_buf[:, :]
        rwflat = rw[:, :, :].rearrange("p i c -> p (i c)")
        streams_state = rwflat[:, 0:4096].rearrange("p (s k c) -> p s k c", s=NSEQ, k=4)
        state_raw = rwflat[:, 4096:8192].rearrange("p (n c) -> p n c", c=P)
        spread = [[yflat[:, 512 * (2 * j + i):512 * (2 * j + i) + 512].rearrange("p (s v) -> p s v", s=NSEQ)
                   for i in range(2)] for j in range(2)]

        ps = ctx.enter_context(nc.psum_tensor("ps", [P, 8, 512], F32))

        s_x = sem("x_loaded")
        s_const = sem("constants_set")
        s_pair_raw = [sem("gate_raw"), sem("up_raw")]
        s_pair_hi = [sem("gate_hi"), sem("up_hi")]
        s_pair_lo = [sem("gate_lo"), sem("up_lo")]
        s_pair_mm = [sem("gate_products"), sem("up_products")]
        s_pair_read = [sem("gate_read"), sem("up_read")]
        s_hid_hi = sem("hid_hi_written")
        s_hid_lo = sem("hid_lo_written")
        s_row_raw = [sem("row_raw0"), sem("row_raw1")]
        s_row_hi = sem("row_hi_written")
        s_row_lo = sem("row_lo_written")
        s_row_mm = sem("row_products")
        s_out = sem("outputs_summed")
        s_evict = sem("outputs_read")
        s_y0 = sem("y_cleared")
        s_gpost = sem("g_post_loaded")
        s_gpre = sem("g_pre_loaded")
        s_sq = [sem("post_squares"), sem("pre_squares")]
        s_rt = [sem("post_root"), sem("pre_root")]
        s_rc = [sem("post_reciprocal"), sem("pre_reciprocal")]
        s_post = sem("y_normalised")
        s_xnew = sem("x_updated")
        s_xn = sem("xn_written")
        s_tr = sem("xn_transposed")
        s_ahi = sem("act_hi_written")
        s_alo = sem("act_lo_written")
        s_store = sem("y_stored")
        s_f_raw, s_f_hi, s_f_split, s_f_mm = (sem(n) for n in ("f_raw_loaded", "f_hi_written", "f_split", "f_products"))
        s_att_const, s_z, s_fa, s_logf = (sem(n) for n in ("att_const_loaded", "f_logits", "f_functions", "logf_done"))
        s_rw0, s_last, s_kt, s_kt_read = (sem(n) for n in ("rw_zeroed", "last_cols_copied", "k_turned", "k_read"))
        s_c, s_ch, s_qrow0 = sem("c_summed"), sem("c_by_head"), sem("q_rows_cleared")
        s_qp, s_vp, s_mx, s_rs = (sem(n) for n in ("q_pair_set", "v_pair_set", "row_max", "row_sum_inverse"))
        s_sc, s_nm, s_ex, s_pm = (sem(n) for n in ("scores", "minus_max", "exponentials", "probabilities"))
        s_pt, s_ptr, s_o, s_oh, s_ol = (sem(n) for n in ("prob_turned", "prob_t_read", "fox_out", "fox_hi", "fox_lo"))
        s_rwc, s_par, s_st = sem("rw_loaded"), sem("rw_parameters"), sem("states_loaded")
        s_rwd, s_rwa, s_rwe, s_rwp = (sem(f"rw_{n}_steps") for n in ("dve", "act", "pe", "pool"))
        s_gm, s_ws0, s_wt, s_wt_read = (sem(n) for n in (
            "spatial_loaded", "ws_new_cleared", "spatial_turned", "spatial_read"))
        s_mean, s_vsq, s_vroot, s_vinv, s_vgain, s_v, s_new_v = (sem(n) for n in (
            "v_mean", "v_squares", "v_root", "v_inverse", "v_times_gain", "v_normalised", "new_v_stored"))
        s_spatial, s_gated, s_ghi, s_glo = (sem(n) for n in ("spatial_products", "gated", "gated_hi", "gated_lo"))
        s_kc = [sem(f"k_cache{i}_loaded") for i in range(2)]
        s_vc = [sem(f"v_cache{i}_loaded") for i in range(2)]
        s_fc = [sem(f"f_cache{i}_loaded") for i in range(2)]
        s_mx2, s_rs2 = sem("row_max2"), sem("row_sum_inverse2")
        s_tk, s_c2, s_kta, s_ktd, s_cs, s_q2 = (sem(n) for n in (
            "cache_turned", "c2_summed", "kt01_read", "kt23_read", "c2_read", "q_rows_set"))
        s_sc2, s_nm2, s_ex2, s_pm2, s_pt2, s_ptr2, s_o2, s_oh2, s_ol2 = (sem(n + "2") for n in (
            "scores", "minus_max", "exponentials", "probabilities", "prob_turned", "prob_t_read", "fox_out", "fox_hi",
            "fox_lo"))
        block = ctx.enter_context(nc.Block())

        def wide(b):
            return ps[:, b:b + 2, 0:HALF]

        def halves(buf, k):
            if isinstance(k, int):
                return buf[:, k, :].rearrange("p (a b) -> p a b", a=2)
            return buf[:, bass.ds(k, 1), :].rearrange("p o (a b) -> p (o a) b", a=2)


        def sp_pair(sp, n, src_of):
            for c in range(2):
                sp.wait_ge(s_pair_lo[c], n + 1)
                sp.dma_start(pair_raw[c][:, :, :], src_of(c)).then_inc(s_pair_raw[c], 16)

        def sp_row(sp, i, base, half_base, src):
            sp.wait_ge(s_row_lo, base + i + 1)
            sp.dma_start(row_raw[i % 2][:, :], src).then_inc(s_row_raw[i % 2], 16)

        def act_split_pair(act, c, n):
            act.wait_ge(s_pair_raw[c], (n + 1) * 16)
            act.wait_ge(s_pair_mm[c], n + 1)
            act.activation(pair_hi[c][:, :, :], pair_raw[c][:, :, :], ACT.Copy).then_inc(s_pair_hi[c], 1)

        def dve_split_pair(dve, c, n):
            dve.wait_ge(s_pair_hi[c], n + 1)
            dve.tensor_tensor(pair_lo[c][:, :, :], pair_raw[c][:, :, :], pair_hi[c][:, :, :].bitcast(F32),
                              ALU.subtract).then_inc(s_pair_lo[c], 1)

        def act_split_row(act, i, base, half_base):
            act.wait_ge(s_row_raw[i % 2], (half_base + i // 2 + 1) * 16)
            act.wait_ge(s_row_mm, base + i + 1)
            act.activation(row_hi[i % 2][:, :], row_raw[i % 2][:, :], ACT.Copy).then_inc(s_row_hi, 1)

        def dve_split_row(dve, i, base):
            dve.wait_ge(s_row_hi, base + i + 1)
            dve.tensor_tensor(row_lo[i % 2][:, :], row_raw[i % 2][:, :], row_hi[i % 2][:, :].bitcast(F32),
                              ALU.subtract).then_inc(s_row_lo, 1)

        def pe_pair(pe, n):
            for c in range(2):
                pe.wait_ge(s_pair_lo[c], n + 2)
                pe.wait_ge(s_pair_read[c], n + 1)
                for k in range(KD):
                    for w, a in ((pair_hi, act_hi), (pair_hi, act_lo), (pair_lo, act_hi)):
                        for h in range(2):
                            mm = pe.matmul(ps[:, 2 * c + h, 0:HALF], w[c][:, k, :],
                                           a[:, k, h * HALF:(h + 1) * HALF],
                                           start=(k == 0 and w is pair_hi and a is act_hi),
                                           stop=(k == KD - 1 and w is pair_lo))
                mm.then_inc(s_pair_mm[c], 1)

        def pe_rows(pe, kt, groups, base, group_base, left_hi, left_lo, left_ready):
            for g in range(groups):
                banks = ODD_BANKS if g % 2 else EVEN_BANKS
                for k in range(kt):
                    i = g * kt + k
                    pe.wait_ge(s_row_lo, base + i + 3)
                    if g == 0:
                        left_ready(k)
                    for t in range(TT):
                        if k == 0 and g % 2 == 0 and t == 0:
                            pe.wait_ge(s_evict, (group_base + g) * TT + 1)
                        if k == 0 and g % 2 == 1 and t == 3:
                            pe.wait_ge(s_evict, (group_base + g - 1) * TT + 3)
                        for w, a in ((row_hi, left_hi), (row_hi, left_lo), (row_lo, left_hi)):
                            mm = pe.matmul(ps[:, banks[t], :], a[:, k, t * P:(t + 1) * P],
                                           w[i % 2][:, :],
                                           start=(k == 0 and w is row_hi and a is left_hi),
                                           stop=(k == kt - 1 and w is row_lo))
                        if t == TT - 1:
                            mm.then_inc(s_row_mm, 1)
                        elif k == kt - 1:
                            mm.then_inc(s_out, 1)

        def wait_output(eng, g, t, kt, base, group_base):
            if t < TT - 1:
                eng.wait_ge(s_out, (group_base + g) * (TT - 1) + t + 1)
            else:
                eng.wait_ge(s_row_mm, base + (g + 1) * kt + 2)

        def splits_and_outputs(kt, groups, split, evict):
            done = 0
            for g in range(groups):
                until = min((g + 1) * kt + 2, groups * kt)
                for i in range(done, until):
                    split(i)
                done = until
                for t in range(TT):
                    evict(g, t)

        def ffn_counts(stage, c):
            return (before(stage, 0) + c * FF_K, before(stage, 1) + c * (OUT_N * FF_K),
                    before(stage, 1) // 2 + c * (OUT_N * FF_K // 2), before(stage, 2) + c * OUT_N)

        def sp_ffn(sp, f):
            w_in = io["ffn_w_in"][f // 2, f % 2].rearrange("(k p) n -> p k n", p=P)
            w_out = io["ffn_w_out"][f // 2, f % 2]
            with sp.Fori(0, FF_CHUNKS) as c:
                n0, r0, h0, _ = ffn_counts(f"ffn{f}", c)
                with sp.Fori(0, FF_K) as j:
                    sp_pair(sp, n0 + j, lambda half: w_in[:, :, bass.ds((c * FF_K + j) * P + half * D_FF, P)])
                for i in range(OUT_N * FF_K):
                    n, k = i // FF_K, i % FF_K
                    sp_row(sp, i, r0, h0, w_out[bass.ds((c * FF_K + k) * P, P), n * 512:(n + 1) * 512])

        def pe_ffn(pe, f):
            with pe.Fori(0, FF_CHUNKS) as c:
                n0, r0, _, g0 = ffn_counts(f"ffn{f}", c)
                with pe.Fori(0, FF_K) as j:
                    pe.wait_ge(s_evict, g0 * TT + 1)
                    pe_pair(pe, n0 + j)
                for h in range(2):
                    pe.wait_ge(s_pair_read[h], n0 + FF_K + 1)

                def hidden_ready(k):
                    pe.wait_ge(s_hid_lo, hid_base(f, c) + k + 2)

                pe_rows(pe, FF_K, OUT_N, r0, g0, hid_hi, hid_lo, hidden_ready)

        def hid_base(f, c):
            return (f * FF_CHUNKS + c) * FF_K

        def act_ffn(act, f):
            with act.Fori(0, FF_CHUNKS) as c:
                n0, r0, h0, _ = ffn_counts(f"ffn{f}", c)
                hb = hid_base(f, c)

                def tile(j, last):
                    act.wait_ge(s_pair_mm[0], n0 + j + 2)
                    act.wait_ge(s_pair_read[1], n0 + j + 1)
                    act.activation(silu[:, :, :], wide(0), ACT.Silu).then_inc(s_pair_read[0], 1)
                    if not last:
                        act_split_pair(act, 0, n0 + j + 1)
                    act.wait_ge(s_pair_read[1], n0 + j + 2)
                    act.activation(halves(hid_hi, j), hid[:, :, :], ACT.Copy).then_inc(s_hid_hi, 1)
                    if not last:
                        act_split_pair(act, 1, n0 + j + 1)

                act_split_pair(act, 0, n0)
                act_split_pair(act, 1, n0)
                with act.Fori(0, FF_K - 1) as j:
                    tile(j, False)
                act_split_row(act, 0, r0, h0)
                act_split_row(act, 1, r0, h0)
                tile(FF_K - 1, True)
                for i in range(2, OUT_N * FF_K):
                    act_split_row(act, i, r0, h0)

        def dve_ffn(dve, f):
            with dve.Fori(0, FF_CHUNKS) as c:
                n0, r0, h0, g0 = ffn_counts(f"ffn{f}", c)
                hb = hid_base(f, c)

                def tile(j, last):
                    if not last:
                        dve_split_pair(dve, 0, n0 + j + 1)
                    dve.wait_ge(s_pair_mm[1], n0 + j + 2)
                    dve.wait_ge(s_pair_read[0], n0 + j + 2)
                    dve.wait_ge(s_hid_lo, hb + j + 1)
                    dve.tensor_tensor(hid[:, :, :], silu[:, :, :], wide(2), ALU.mult).then_inc(s_pair_read[1], 1)
                    dve.wait_ge(s_hid_hi, hb + j + 1)
                    dve.tensor_tensor(halves(hid_lo, j), hid[:, :, :], halves(hid_hi, j).bitcast(F32),
                                      ALU.subtract).then_inc(s_hid_lo, 1)
                    if not last:
                        dve_split_pair(dve, 1, n0 + j + 1)

                dve_split_pair(dve, 0, n0)
                dve_split_pair(dve, 1, n0)
                with dve.Fori(0, FF_K - 1) as j:
                    tile(j, False)
                dve_split_row(dve, 0, r0)
                dve_split_row(dve, 1, r0)
                tile(FF_K - 1, True)

                def split(i):
                    if i > 1:
                        dve_split_row(dve, i, r0)

                def evict(g, t):
                    wait_output(dve, g, t, FF_K, r0, g0)
                    bank = (ODD_BANKS if g % 2 else EVEN_BANKS)[t]
                    dve.wait_ge(s_evict, g0 * TT + 1)
                    dve.wait_ge(s_y0, (f + 1) * TT)
                    dst = y[:, t, g * 512:(g + 1) * 512]
                    dve.tensor_tensor(dst, dst, ps[:, bank, :], ALU.add).then_inc(s_evict, 1)

                splits_and_outputs(FF_K, OUT_N, split, evict)

        NORMS = 6

        def roots(act, t, which, n, src, scale):
            if n:
                act.wait_ge(s_sq[which], n)
            act.activation(squares[which][:, :], src, ACT.Square,
                           accum_out=stat[:, 3 * which, t:t + 1]).then_inc(s_sq[which], 1)
            act.wait_ge(s_sq[which], n + 1)
            act.activation(stat[:, 3 * which + 1, t:t + 1], stat[:, 3 * which, t:t + 1], ACT.Sqrt,
                           bias=eps[:, 0:1] if scale == 1 else eps[:, 1:2],
                           scale=1 / D / scale ** 2).then_inc(s_rt[which], 1)

        def act_norm(act, m, scale, groups):
            if m == 0:
                act.wait_ge(s_const, 4)
                act.wait_ge(s_x, 32)
            for s in range(TT + 2):
                if m and s < TT:
                    act.wait_ge(s_evict, groups * TT - TT + s + 2)
                    roots(act, s, 0, 5 * (m - 1) + s, y[:, s, :], scale)
                if 0 <= s - 1 < TT and m < NORMS:
                    t = s - 1
                    if m:
                        act.wait_ge(s_xnew, 5 * (m - 1) + t + 1)
                    roots(act, t, 1, 5 * m + t, x[:, t, :], 1)
                if 0 <= s - 2 < TT and m < NORMS:
                    t = s - 2
                    act.wait_ge(s_tr, 5 * m + t + 1)
                    b = NORM_BANKS[t % 2]
                    act.activation(act_hi[:, :, t * P:(t + 1) * P],
                                   ps[:, b:b + 2, :].rearrange("p a (k c) -> p (a k) c", c=P),
                                   ACT.Copy).then_inc(s_ahi, 1)

        def dve_norm(dve, m):
            for s in range(TT + 2):
                if m and s < TT:
                    n = 5 * (m - 1) + s
                    dve.wait_ge(s_rt[0], n + 1)
                    dve.reciprocal(stat[:, 2, s:s + 1], stat[:, 1, s:s + 1]).then_inc(s_rc[0], 1)
                    dve.wait_ge(s_rc[0], n + 1)
                    dve.wait_ge(s_gpost, 16 * m)
                    dve.scalar_tensor_tensor(out=y[:, s, :], in0=y[:, s, :], scalar=stat[:, 2, s:s + 1],
                                             in1=g_post[:, :], op0=ALU.mult, op1=ALU.mult).then_inc(s_post, 1)
                if 0 <= s - 1 < TT and m < NORMS:
                    t, n = s - 1, 5 * m + s - 1
                    dve.wait_ge(s_rt[1], n + 1)
                    dve.reciprocal(stat[:, 5, t:t + 1], stat[:, 4, t:t + 1]).then_inc(s_rc[1], 1)
                    dve.wait_ge(s_rc[1], n + 1)
                    dve.wait_ge(s_gpre, 16 * (m + 1))
                    if n >= 2:
                        dve.wait_ge(s_tr, n - 1)
                    dve.scalar_tensor_tensor(out=xn[t % 2][:, :], in0=x[:, t, :], scalar=stat[:, 5, t:t + 1],
                                             in1=g_pre[:, :], op0=ALU.mult, op1=ALU.mult).then_inc(s_xn, 1)
                if 0 <= s - 2 < TT and m < NORMS:
                    t = s - 2
                    dve.wait_ge(s_ahi, 5 * m + t + 1)
                    b = NORM_BANKS[t % 2]
                    cols = slice(t * P, (t + 1) * P)
                    dve.tensor_tensor(act_lo[:, :, cols],
                                      ps[:, b:b + 2, :].rearrange("p a (k c) -> p (a k) c", c=P),
                                      act_hi[:, :, cols].bitcast(F32), ALU.subtract).then_inc(s_alo, 1)

        CLEARING = (0, 2, 3, 5)

        def pool_norm(pool, m):
            for t in range(TT):
                n = 5 * (m - 1) + t
                if m:
                    pool.wait_ge(s_post, n + 1)
                    pool.tensor_tensor(x[:, t, :], x[:, t, :], y[:, t, :], ALU.add).then_inc(s_xnew, 1)
                if m in CLEARING:
                    if m:
                        pool.wait_ge(s_xnew, n + 1)
                    pool.memset(y[:, t, :], 0.0).then_inc(s_y0, 1)

        def pe_norm(pe, m, groups):
            if m == 0:
                pe.wait_ge(s_const, 4)
            else:
                pe.wait_ge(s_evict, groups * TT + 1)
            for t in range(TT):
                n = 5 * m + t
                pe.wait_ge(s_xn, n + 1)
                if n >= 2:
                    pe.wait_ge(s_alo, n - 1)
                b = NORM_BANKS[t % 2]
                for k in range(KD):
                    mm = pe.transpose(ps[:, b + k // 4, k % 4 * P:(k % 4 + 1) * P],
                                      xn[t % 2][:, k * P:(k + 1) * P], ident[:, :])
                mm.then_inc(s_tr, 1)

        def sp_norm_gains(sp, m):
            layer, i = divmod(m, 3)
            if m:
                pl, pi = divmod(m - 1, 3)
                if m > 1:
                    sp.wait_ge(s_post, 5 * (m - 1))
                sp.dma_start(g_post[:, :], io["norm_g"][pl, 2 * pi + 1:2 * pi + 2, :].broadcast_to([P, D]))\
                  .then_inc(s_gpost, 16)
            if m < NORMS:
                if m:
                    sp.wait_ge(s_xn, 5 * m)
                sp.dma_start(g_pre[:, :], io["norm_g"][layer, 2 * i:2 * i + 1, :].broadcast_to([P, D]))\
                  .then_inc(s_gpre, 16)

        NQK, NRW = 4, 7
        ew_in = io["even_w_in"][0].rearrange("(k p) n -> p k n", p=P)

        def sp_even_in(sp):
            n0, r0, h0 = before("even_in", 0), before("even_in", 1), before("even_in", 1) // 2
            sp.dma_start(f_raw[:, :, :], ew_in[:, :, 3 * FOXW:3 * FOXW + FOXH]).then_inc(s_f_raw, 16)
            sp.dma_start(bf_all[:, :], io["fox_bf"].broadcast_to([P, FOXH])).then_inc(s_f_raw, 16)
            sp.dma_start(att_const[:, :], io["att_const"]).then_inc(s_att_const, 16)
            with sp.Fori(0, NQK) as j:
                sp_pair(sp, n0 + j, lambda c: ew_in[:, :, bass.ds(j * 256 + c * P, P)])
            with sp.Fori(0, NRW) as j:
                sp_pair(sp, n0 + NQK + j, lambda c: ew_in[:, :, bass.ds(j * 256 + c * P + FOXC, P)])
            for k in range(KD):
                sp_row(sp, k, r0, h0, io["even_w_in"][0, k * P:(k + 1) * P, 2 * FOXW:3 * FOXW])

        def pe_even_in(pe):
            n0, r0, g0 = (before("even_in", i) for i in range(3))
            pe.wait_ge(s_f_split, 1)
            for t in range(TT):
                for k in range(KD):
                    for a, w in ((act_hi, f_hi), (act_lo, f_hi), (act_hi, f_lo)):
                        mm = pe.matmul(ps[:, 6, t * FOXH:(t + 1) * FOXH], a[:, k, t * P:(t + 1) * P],
                                       w[:, k, :], start=(k == 0 and a is act_hi and w is f_hi),
                                       stop=(k == KD - 1 and w is f_lo))
            mm.then_inc(s_f_mm, 1)
            with pe.Fori(0, NQK + NRW) as j:
                pe.wait_ge(s_evict, g0 * TT + 1)
                pe_pair(pe, n0 + j)
            for h in range(2):
                pe.wait_ge(s_pair_read[h], n0 + NQK + NRW + 1)
            pe.wait_ge(s_z, 1)
            pe_rows(pe, KD, 1, r0, g0, act_hi, act_lo, lambda k: None)

        def rw_cols(i):
            return rw[:, bass.ds(i, 1), 1:1 + TOK].rearrange("p o (a b) -> p (o a) b", a=2)

        def act_even_in(act):
            n0, r0, h0 = before("even_in", 0), before("even_in", 1), before("even_in", 1) // 2
            act.wait_ge(s_f_raw, 32)
            act.activation(f_hi[:, :, :], f_raw[:, :, :], ACT.Copy).then_inc(s_f_hi, 1)

            def tile(n, dst, last):
                act.wait_ge(s_pair_mm[0], n + 2)
                act.activation(dst, wide(0), ACT.Copy).then_inc(s_pair_read[0], 1)
                if not last:
                    act_split_pair(act, 0, n + 1)
                    act_split_pair(act, 1, n + 1)

            act_split_pair(act, 0, n0)
            act_split_pair(act, 1, n0)
            with act.Fori(0, NQK) as j:
                tile(n0 + j, halves(qk, 2 * j), False)
            with act.Fori(0, NRW - 1) as j:
                tile(n0 + NQK + j, rw_cols(2 * j), False)
            act_split_row(act, 0, r0, h0)
            act_split_row(act, 1, r0, h0)
            tile(n0 + NQK + NRW - 1, rw_cols(2 * NRW - 2), True)
            for k in range(2, KD):
                act_split_row(act, k, r0, h0)
            act.wait_ge(s_z, 1)
            act.activation(f_tmp[:, :, :], logf[:, :, :], ACT.Abs).then_inc(s_fa, 1)
            act.wait_ge(s_fa, 1)
            act.activation(f_tmp[:, :, :], f_tmp[:, :, :], ACT.Exp, scale=-1.0).then_inc(s_fa, 1)
            act.wait_ge(s_fa, 2)
            act.activation(f_tmp[:, :, :], f_tmp[:, :, :], ACT.Ln, bias=1.0).then_inc(s_fa, 1)

        def dve_even_in(dve):
            n0, r0, g0 = (before("even_in", i) for i in range(3))
            dve.wait_ge(s_f_hi, 1)
            dve.tensor_tensor(f_lo[:, :, :], f_raw[:, :, :], f_hi[:, :, :].bitcast(F32), ALU.subtract)\
               .then_inc(s_f_split, 1)
            dve.memset(rw[:, :, 0:1], 0.0).then_inc(s_rw0, 1)

            def tile(n, dst, last):
                if not last:
                    dve_split_pair(dve, 0, n + 1)
                dve.wait_ge(s_pair_mm[1], n + 2)
                dve.tensor_copy(dst, wide(2)).then_inc(s_pair_read[1], 1)
                if not last:
                    dve_split_pair(dve, 1, n + 1)

            dve_split_pair(dve, 0, n0)
            dve_split_pair(dve, 1, n0)
            dve.wait_ge(s_f_mm, 1)
            dve.tensor_tensor(logf[:, :, :], ps[:, 6, 0:TT * FOXH].rearrange("p (t h) -> p t h", h=FOXH),
                              bf_all[:, :].rearrange("p (o h) -> p o h", o=1).broadcast_to([P, TT, FOXH]),
                              ALU.add).then_inc(s_z, 1)
            with dve.Fori(0, NQK) as j:
                tile(n0 + j, halves(qk, 2 * j + 1), False)
            with dve.Fori(0, NRW - 1) as j:
                tile(n0 + NQK + j, rw_cols(2 * j + 1), False)
            dve_split_row(dve, 0, r0)
            dve_split_row(dve, 1, r0)
            tile(n0 + NQK + NRW - 1, rw_cols(2 * NRW - 1), True)
            for k in range(2, KD):
                dve_split_row(dve, k, r0)
            for t in range(TT):
                wait_output(dve, 0, t, KD, r0, g0)
                dve.tensor_copy(vtok[:, t, :], ps[:, EVEN_BANKS[t], :]).then_inc(s_evict, 1)
            dve.wait_ge(s_fa, 3)
            dve.wait_ge(s_z, 1)
            dve.scalar_tensor_tensor(out=logf[:, :, :], in0=logf[:, :, :], scalar=0.0, in1=f_tmp[:, :, :],
                                     op0=ALU.min, op1=ALU.subtract).then_inc(s_logf, 1)

        def pe_even_outputs(pe):
            e0 = before("even_in", 2)
            pe.wait_ge(s_evict, (e0 + 1) * TT + 1)
            pe.wait_ge(s_z, 1)
            for t in range(TT):
                for p in range(4):
                    mm = pe.transpose(ps[:, t, p * P:(p + 1) * P], qk[:, 4 + p, t * P:(t + 1) * P], ident[:, :])
                mm.then_inc(s_kt, 1)
            for i in range(2 * NRW):
                if i == 12:
                    pe.wait_ge(s_kt_read, 1)
                mm = pe.transpose(ps[0:9, (5, 6, 7, 0)[i // 4], i % 4 * P:(i % 4 + 1) * P],
                                  last_cols[:, i, :], ident[:, :])
            mm.then_inc(s_kt, 1)

        def dve_even_outputs(dve):
            dve.wait_ge(s_pair_read[0], before("even_in", 0) + NQK + NRW + 1)
            dve.wait_ge(s_pair_read[1], before("even_in", 0) + NQK + NRW + 1)
            dve.tensor_copy(last_cols[:, :, 0:1], rw[:, :, SEQ:SEQ + 1]).then_inc(s_last, 1)
            dve.tensor_copy(last_cols[:, :, 1:9],
                            rw[:, :, 1 + SEQ:1 + TOK].rearrange("p i (s t) -> p i s t", t=NEW)[:, :, :, NEW - 1])\
               .then_inc(s_last, 1)
            for t in range(TT):
                dve.wait_ge(s_kt, t + 1)
                dve.tensor_copy(ktok[:, t, :], ps[:, t, :]).then_inc(s_kt_read, 1)
            dve.wait_ge(s_kt, TT + 1)
            dve.tensor_copy(last_rows[:, 0:12 * P].rearrange("p (b c) -> p b c", b=3), ps[0:9, 5:8, :])\
               .then_inc(s_kt_read, 1)
            dve.tensor_copy(last_rows[:, 12 * P:14 * P], ps[0:9, 0, 0:2 * P]).then_inc(s_kt_read, 1)

        def sp_even_outputs(sp):
            sp.wait_ge(s_evict, (before("even_in", 2) + 1) * TT + 1)
            store(sp, io["fv_p"][0, 0].rearrange("(t p) h d -> p t (h d)", p=P), vtok[:, 0:4, :])
            store(sp, io["fv_s"][0].rearrange("s t h d -> (s t) (h d)"), vtok[:, 4, :])
            sp.wait_ge(s_kt_read, TT)
            store(sp, io["fk_p"][0, 0].rearrange("(t p) h d -> p t (h d)", p=P), ktok[:, 0:4, :])
            store(sp, io["fk_s"][0].rearrange("s t h d -> (s t) (h d)"), ktok[:, 4, :])
            sp.wait_ge(s_kt_read, TT + 2)
            store(sp, io["rsh_p"][0, 0], last_rows[0:1, :])
            store(sp, io["rsh_s"][0].rearrange("s o c -> (s o) c"), last_rows[1:9, :])
            sp.wait_ge(s_logf, 1)
            store(sp, io["fl_p"][0, 0].rearrange("(t p) h -> p t h", p=P), logf[:, 0:4, :])
            store(sp, io["fl_s"][0].rearrange("s t h -> (s t) h"), logf[:, 4, :])

        def pe_prompt_c(pe):
            pe.wait_ge(s_att_const, 16)
            pe.wait_ge(s_logf, 1)
            pe.wait_ge(s_kt_read, TT + 2)
            for t in range(4):
                mm = pe.matmul(ps[0:FOXH, 1, t * P:SEQ], logf[:, t, :], tri_ones[:, 0:SEQ - t * P],
                               start=(t == 0), stop=(t == 3))
            mm.then_inc(s_c, 1)

        def dve_prompt_c(dve):
            dve.wait_ge(s_c, 1)
            dve.tensor_tensor(c_heads[:, :, :],
                              ps[0:FOXH, 1:2, :].broadcast_to([FOXH, FOXH, SEQ]),
                              sel8.rearrange("p (h o) -> p h o", o=1).broadcast_to([FOXH, FOXH, SEQ]),
                              ALU.mult).then_inc(s_ch, 1)

        UNITS = 8

        def unit(u):
            h, qt = u // 4, u % 4
            return h, qt, (qt + 1) * P, slice(64 * h, 64 * h + 64)

        def after(n, lag=0):
            return n + (3 - lag)

        def act_prompt(act):
            act.wait_ge(s_kt_read, TT + 2)
            with act.Fori(0, 4) as p:
                act.wait_ge(s_sc, UNITS * p + 2)
                act.activation(q_pair[:, :].rearrange("p (o c) -> p o c", o=1), qk[:, bass.ds(p, 1), 0:SEQ],
                               ACT.Copy, scale=HEAD ** -0.5).then_inc(s_qp, 1)
                for s in range(UNITS + 2):
                    if s < UNITS:
                        u, n = s, UNITS * p + s
                        kl = unit(u)[2]
                        act.wait_ge(s_nm, after(n))
                        act.wait_ge(s_pt, after(n, 2))
                        act.activation(prob[u % 2][:, 0:kl], ps[:, u % 2, 0:kl], ACT.Exp, bias=nmax[:, u:u + 1],
                                       accum_out=esum[:, u:u + 1]).then_inc(s_ex, 1)
                    if 0 <= s - 1 < UNITS:
                        u, n = s - 1, UNITS * p + (s - 1)
                        kl = unit(u)[2]
                        act.wait_ge(s_pt, after(n))
                        act.wait_ge(s_o, after(n, 2))
                        act.activation(prob_t[u % 2][:, 0:kl], ps[:, 2 + u % 2, 0:kl], ACT.Copy).then_inc(s_ptr, 1)
                    if 0 <= s - 2 < UNITS:
                        u, n = s - 2, UNITS * p + (s - 2)
                        _, qt, _, rows = unit(u)
                        act.wait_ge(s_o, after(n))
                        act.activation(act_hi[rows, bass.ds(p, 1), qt * P:(qt + 1) * P],
                                       ps[rows, 4 + u % 2, 0:P].rearrange("p (o c) -> p o c", o=1),
                                       ACT.Copy).then_inc(s_oh, 1)

        def dve_prompt(dve):
            with dve.Fori(0, 4) as p:
                for s in range(UNITS + 2):
                    if s < UNITS:
                        u, n = s, UNITS * p + s
                        kl = unit(u)[2]
                        dve.wait_ge(s_sc, after(n))
                        dve.tensor_reduce(rmax[:, u:u + 1], ps[:, u % 2, 0:kl], AX, ALU.max).then_inc(s_mx, 1)
                        dve.wait_ge(s_mx, n + 1)
                        dve.tensor_scalar(nmax[:, u:u + 1], rmax[:, u:u + 1], -1.0, None, ALU.mult)\
                           .then_inc(s_nm, 1)
                        dve.wait_ge(s_ex, after(n))
                        dve.wait_ge(s_pm, after(n, 2))
                        dve.reciprocal(rsum[:, u:u + 1], esum[:, u:u + 1]).then_inc(s_rs, 1)
                    if 0 <= s - 2 < UNITS:
                        u, n = s - 2, UNITS * p + (s - 2)
                        _, qt, _, rows = unit(u)
                        dve.wait_ge(s_oh, after(n))
                        cols = slice(qt * P, (qt + 1) * P)
                        dve.tensor_tensor(act_lo[rows, bass.ds(p, 1), cols],
                                          ps[rows, 4 + u % 2, 0:P].rearrange("p (o c) -> p o c", o=1),
                                          act_hi[rows, bass.ds(p, 1), cols].bitcast(F32),
                                          ALU.subtract).then_inc(s_ol, 1)

        def pool_prompt(pool):
            pool.wait_ge(s_kt_read, TT + 2)
            with pool.Fori(0, 4) as p:
                pool.wait_ge(s_o, UNITS * p + 2)
                pool.tensor_copy(k_pair[:, :, :], qk[:, bass.ds(p + 4, 1), 0:SEQ])
                pool.tensor_copy(v_pair[:, :, :], vtok[:, 0:4, bass.ds(p * P, P)]).then_inc(s_vp, 1)
                for u in range(UNITS):
                    n = UNITS * p + u
                    kl = unit(u)[2]
                    pool.wait_ge(s_rs, n + 1)
                    pool.tensor_tensor(prob[u % 2][:, 0:kl], prob[u % 2][:, 0:kl],
                                       rsum[:, u:u + 1].broadcast_to([P, kl]), ALU.mult).then_inc(s_pm, 1)

        def pe_prompt(pe):
            def scores(p, u):
                h, qt, kl, rows = unit(u)
                pe.wait_ge(s_ex, after(UNITS * p + u, 2))
                out = ps[:, u % 2, 0:kl]
                pe.matmul(out, q_pair[rows, qt * P:(qt + 1) * P],
                          k_pair[rows, 0, 0:kl], start=True, stop=False)
                pe.matmul(out, minus_ones[0:FOXH, :],
                          c_heads[:, bass.ds(2 * p + h, 1), 0:kl].rearrange("p o c -> p (o c)"),
                          start=False, stop=False)
                pe.matmul(ps[:, u % 2, qt * P:kl], ident[:, :], causal, start=False, stop=True)\
                  .then_inc(s_sc, 1)

            pe.wait_ge(s_ch, 1)
            with pe.Fori(0, 4) as p:
                pe.wait_ge(s_qp, p + 1)
                pe.wait_ge(s_vp, p + 1)
                scores(p, 0)
                for u in range(UNITS):
                    n = UNITS * p + u
                    qt = unit(u)[1]
                    if u + 1 < UNITS:
                        scores(p, u + 1)
                    pe.wait_ge(s_pm, after(n))
                    pe.wait_ge(s_ptr, after(n, 2))
                    for k in range(qt + 1):
                        mm = pe.transpose(ps[:, 2 + u % 2, k * P:(k + 1) * P],
                                          prob[u % 2][:, k * P:(k + 1) * P], ident[:, :])
                    mm.then_inc(s_pt, 1)
                    pe.wait_ge(s_ptr, after(n))
                    pe.wait_ge(s_ol, after(n, 2))
                    for k in range(qt + 1):
                        mm = pe.matmul(ps[:, 4 + u % 2, 0:P], v_pair[:, k, :], prob_t[u % 2][:, k * P:(k + 1) * P],
                                       start=(k == 0), stop=(k == qt))
                    mm.then_inc(s_o, 1)

        flat = ps[:, :, :].rearrange("p b c -> p (b c)")

        def sp_streams(sp):
            sp.wait_ge(s_store, sum(stores))
            sp.wait_ge(s_ol, UNITS * 4 + 2)
            sp.dma_start(new_mask, io["new_mask"].rearrange("p (b c) -> p b c", c=P)).then_inc(s_att_const, 16)
            with sp.Fori(0, NSEQ // 2) as i:
                for slot in range(2):
                    b = 2 * i + slot
                    one = lambda a: a[0, bass.ds(b, 1)]
                    sp.wait_ge(s_tk, after(b, 2))
                    sp.dma_start(k_cache[slot][:, :, :],
                                 one(io["cache_fox_k"]).rearrange("o (t p) h d -> p (o t) (h d)", p=P))\
                      .then_inc(s_kc[slot], 16)
                    sp.wait_ge(s_c2, after(b, 2))
                    sp.dma_start(f_cache[slot][:, :, :],
                                 one(io["cache_fox_logf"]).rearrange("o (t p) h -> p (o t) h", p=P))\
                      .then_inc(s_fc[slot], 16)
                    sp.wait_ge(s_o2, after(b, 2))
                    sp.dma_start(v_cache[slot][:, :, :],
                                 one(io["cache_fox_v"]).rearrange("o (t p) h d -> p (o t) (h d)", p=P))\
                      .then_inc(s_vc[slot], 16)

        def pe_streams(pe):
            def keys(i, slot):
                b = 2 * i + slot
                pe.wait_ge(s_kc[slot], 16 * i + 16)
                pe.wait_ge(s_kta, after(b, 1))
                pe.wait_ge(s_ktd, after(b, 1))
                for p in range(4):
                    for k in range(4):
                        mm = pe.transpose(ps[:, p, k * P:(k + 1) * P], k_cache[slot][:, k, p * P:(p + 1) * P],
                                          ident[:, :])
                mm.then_inc(s_tk, 1)
                pe.wait_ge(s_fc[slot], 16 * i + 16)
                pe.wait_ge(s_ptr2, after(b, 1 + slot))
                for k in range(4):
                    pe.matmul(ps[0:FOXH, 6, k * P:SEQ], f_cache[slot][:, k, :], tri_ones[:, 0:SEQ - k * P],
                              start=(k == 0), stop=(k == 3))
                for k in range(4):
                    pe.matmul(ps[0:FOXH, 7, 0:P], f_cache[slot][:, k, :], tri_ones[:, P:2 * P],
                              start=(k == 0), stop=False)
                pe.matmul(ps[0:FOXH, 7, 0:P], logf[:, 4, :], tri_streams, start=False, stop=True)\
                  .then_inc(s_c2, 1)

            def scores(b):
                pe.wait_ge(s_kta, after(b))
                pe.wait_ge(s_ktd, after(b))
                pe.wait_ge(s_q2, after(b))
                pe.wait_ge(s_ol2, after(b, 1))
                for p in range(4):
                    pe.matmul(ps[:, 4, :], q_rows[:, p * P:(p + 1) * P], kt_cache[p // 2][:, p % 2, :], start=(p == 0), stop=False)
                pe.matmul(ps[:, 4, :], minus_heads, c_stream[0:FOXH, 0:SEQ], start=False, stop=True)
                for p in range(4):
                    pe.matmul(ps[:, 5, 0:P], q_rows[:, p * P:(p + 1) * P], qk[:, 4 + p, SEQ:TOK],
                              start=(p == 0), stop=False)
                pe.matmul(ps[:, 5, 0:P], minus_heads, c_stream[0:FOXH, SEQ:TOK], start=False, stop=False)
                pe.matmul(ps[:, 5, 0:P], ident[:, :], new_mask[:, bass.ds(b, 1), :].rearrange("p o c -> p (o c)"),
                          start=False, stop=True).then_inc(s_sc2, 1)

            def outputs(i, slot):
                b = 2 * i + slot
                pe.wait_ge(s_pm2, after(b))
                pe.wait_ge(s_cs, after(b, slot - 1))
                for k in range(5):
                    mm = pe.transpose(flat[:, 6 * 512 + k * P:6 * 512 + (k + 1) * P], prob2[:, k * P:(k + 1) * P],
                                      ident[:, :])
                mm.then_inc(s_pt2, 1)
                pe.wait_ge(s_ptr2, after(b))
                pe.wait_ge(s_vc[slot], 16 * i + 16)
                for p in range(4):
                    for k in range(5):
                        v = v_cache[slot][:, k, p * P:(p + 1) * P] if k < 4 else vtok[:, 4, p * P:(p + 1) * P]
                        mm = pe.matmul(ps[:, 4, p * 32:p * 32 + 32], v, prob_t2[:, k * P + p * 32:k * P + p * 32 + 32],
                                       start=(k == 0), stop=(k == 4))
                mm.then_inc(s_o2, 1)

            pe.wait_ge(s_ol, UNITS * 4 + 2)
            pe.wait_ge(s_att_const, 32)
            with pe.Fori(0, NSEQ // 2) as i:
                keys(i, 0)
                scores(2 * i)
                keys(i, 1)
                outputs(i, 0)
                scores(2 * i + 1)
                outputs(i, 1)

        def diagonal(buf, h, b):
            return buf[64 * h:64 * h + 64, 0:4, bass.ds(SEQ + NEW * b, NEW)]

        def products(h):
            return ps[64 * h:64 * h + 64, 4, 0:P].rearrange("p (a c) -> p a c", c=32)[:, :, NEW * h:NEW * h + NEW]

        def act_streams(act):
            def keys(b):
                act.wait_ge(s_sc2, after(b, 1))
                act.wait_ge(s_tk, after(b))
                act.activation(kt_cache[0], ps[:, 0:2, :], ACT.Copy).then_inc(s_kta, 1)
                act.wait_ge(s_c2, after(b))
                act.activation(c_stream[0:FOXH, :], flat[0:FOXH, 6 * 512:6 * 512 + TOK], ACT.Copy).then_inc(s_cs, 1)
                for h in range(2):
                    rows = slice(64 * h, 64 * h + 64)
                    ins = act.activation(
                        q_rows[rows, NEW * h:NEW * h + 640].rearrange("p (a c) -> p a c", c=160)[:, :, 0:NEW],
                        qk[rows, 0:4, bass.ds(SEQ + NEW * b, NEW)], ACT.Copy, scale=HEAD ** -0.5)
                ins.then_inc(s_q2, 1)

            def soft(b):
                act.wait_ge(s_nm2, after(b))
                act.wait_ge(s_pt2, after(b, 1))
                act.activation(prob2[:, :], flat[:, 4 * 512:4 * 512 + TOK], ACT.Exp, bias=nmax[:, 0:1],
                               accum_out=esum[:, 0:1]).then_inc(s_ex2, 1)

            def outputs(b):
                act.wait_ge(s_pt2, after(b))
                act.wait_ge(s_o2, after(b, 1))
                act.activation(prob_t2[:, :], flat[:, 6 * 512:6 * 512 + TOK], ACT.Copy).then_inc(s_ptr2, 1)
                act.wait_ge(s_o2, after(b))
                act.activation(diagonal(act_hi, 0, b), products(0), ACT.Copy)
                act.activation(diagonal(act_hi, 1, b), products(1), ACT.Copy).then_inc(s_oh2, 1)

            act.wait_ge(s_qrow0, 1)
            act.wait_ge(s_ol, UNITS * 4 + 2)
            with act.Fori(0, NSEQ // 2) as i:
                keys(2 * i)
                soft(2 * i)
                keys(2 * i + 1)
                outputs(2 * i)
                soft(2 * i + 1)
                outputs(2 * i + 1)

        def dve_streams(dve):
            def keys(b):
                dve.wait_ge(s_sc2, after(b, 1))
                dve.wait_ge(s_tk, after(b))
                dve.tensor_copy(kt_cache[1], ps[:, 2:4, :]).then_inc(s_ktd, 1)

            def soft(b):
                dve.wait_ge(s_sc2, after(b))
                dve.tensor_reduce(rmax[:, 0:1], flat[:, 4 * 512:4 * 512 + TOK], AX, ALU.max).then_inc(s_mx2, 1)
                dve.wait_ge(s_mx2, b + 1)
                dve.tensor_scalar(nmax[:, 0:1], rmax[:, 0:1], -1.0, None, ALU.mult).then_inc(s_nm2, 1)

            def total(b):
                dve.wait_ge(s_ex2, after(b))
                dve.wait_ge(s_pm2, after(b, 1))
                dve.reciprocal(rsum[:, 0:1], esum[:, 0:1]).then_inc(s_rs2, 1)

            def outputs(b):
                dve.wait_ge(s_oh2, after(b))
                for h in range(2):
                    ins = dve.tensor_tensor(diagonal(act_lo, h, b), products(h), diagonal(act_hi, h, b).bitcast(F32),
                                            ALU.subtract)
                ins.then_inc(s_ol2, 1)

            dve.memset(q_rows[:, :], 0.0).then_inc(s_qrow0, 1)
            with dve.Fori(0, NSEQ // 2) as i:
                keys(2 * i)
                soft(2 * i)
                total(2 * i)
                keys(2 * i + 1)
                outputs(2 * i)
                soft(2 * i + 1)
                total(2 * i + 1)
                outputs(2 * i + 1)

        def pool_streams(pool):
            with pool.Fori(0, NSEQ) as b:
                pool.wait_ge(s_rs2, b + 1)
                pool.tensor_tensor(prob2[:, :], prob2[:, :], rsum[:, 0:1].broadcast_to([P, TOK]), ALU.mult)\
                    .then_inc(s_pm2, 1)

        F4 = lambda a: a.rearrange("p (k c) -> p k c", k=4)
        H8 = lambda a: a.rearrange("p (h c) -> p h c", h=8)

        def stretch(v, n, c):
            return v.rearrange("p (k o) -> p k o", o=1).broadcast_to([P, n, c])

        def same(v, n):
            return v.rearrange("p (o c) -> p o c", o=1).broadcast_to([P, n, v.shape[-1]])

        def tile_counts(tile, streams):
            def of(steps):
                def at(name, before=False):
                    if streams:
                        return len(steps["prompt"]) * 4 + steps["streams"].index(name) + 2
                    return tile * len(steps["prompt"]) + (steps["prompt"].index(name) + 2)
                return at
            return of(RW_DVE), of(RW_ACT), of(RW_PE), of(RW_POOL)

        def tile_start(steps, tile, streams):
            return len(steps["prompt"]) * 4 + 1 if streams else tile * len(steps["prompt"]) + 1

        def ticker(steps, streams):
            names = iter(steps["streams" if streams else "prompt"])

            def did(name):
                want = next(names)
                assert name == want, (name, want)
                return 1
            return did

        DECAY = 0.5 * math.exp(-0.5)

        def sp_rwkv(sp):
            sp.wait_ge(s_ol2, NSEQ + 2)
            sp.dma_start(rw_const[:, :], io["rw_const"]).then_inc(s_rwc, 16)
            sp.dma_start(par_rows[0:14, :], io["rw_mu"][0].rearrange("(i c) -> i c", c=P)).then_inc(s_rwc, 16)
            for n, name in enumerate(("rw_kk", "rw_ka", "rw_rk", "rw_ln_g", "rw_ln_b")):
                src = io[name][0]
                if name == "rw_rk":
                    src = src.rearrange("h d -> (h d)")
                sp.dma_start(par_rows[14 + 4 * n:18 + 4 * n, :], src.rearrange("(i c) -> i c", c=P))\
                  .then_inc(s_rwc, 16)
            sp.dma_start(shift_rows[:, :], io["state_rwkv_shift"][0].rearrange("s o (i c) -> (s o i) c", c=P))\
              .then_inc(s_rwc, 16)
            sp.dma_start(lora_wa[0:64, :], io["rw_w2"][0]).then_inc(s_rwc, 16)
            sp.dma_start(lora_wa[64:128, :], io["rw_a2"][0]).then_inc(s_rwc, 16)
            sp.dma_start(lora_g[:, :], io["rw_g2"][0]).then_inc(s_rwc, 16)
            sp.dma_start(bias_rows[0:1, :], io["rw_w0"]).then_inc(s_rwc, 16)
            sp.dma_start(bias_rows[32:33, :], io["rw_a0"]).then_inc(s_rwc, 16)
            at = tile_counts(0, True)
            sp.wait_ge(s_rwd, at[0]("clear"))
            for h in range(2):
                sp.dma_start(state_raw[64 * h:64 * h + 64, :, 64 * h:64 * h + 64],
                             io["state_rwkv"][0].rearrange("s (p h) v k -> h v (s p) k", h=2)[h]).then_inc(s_st, 16)
            sp.wait_ge(s_rwa, at[1]("prompt_state"))
            for h in range(2):
                store(sp, io["rs_p"][0, 0].rearrange("(p h) v k -> h v p k", h=2)[h],
                      F4(prompt_state[64 * h:64 * h + 64, :])[:, :, 64 * h:64 * h + 64])
            sp.wait_ge(s_rwa, at[1]("out7"))
            for h in range(2):
                store(sp, io["rs_s"][0].rearrange("s (p h) v k -> h v (s p) k", h=2)[h],
                      state_raw[64 * h:64 * h + 64, :, 64 * h:64 * h + 64])

        def pe_rwkv_setup(pe):
            pe.wait_ge(s_rwc, 16 * 13)
            pe.wait_ge(s_ol2, NSEQ + 2)
            pe.transpose(ps[:, 0, 0:34], par_rows[0:34, :], ident[0:34, 0:34])
            pe.transpose(ps[:, 0, 128:240], shift_rows[:, :], ident[0:112, 0:112]).then_inc(s_par, 1)

        def act_rwkv_setup(act):
            act.wait_ge(s_par, 1)
            act.activation(par[:, :], ps[:, 0, 0:34], ACT.Copy)
            act.activation(shift[:, :], ps[:, 0, 128:240], ACT.Copy).then_inc(s_par, 1)

        def dve_rwkv_setup(dve):
            dve.wait_ge(s_rwc, 16 * 13)
            dve.wait_ge(s_par, 2)
            dve.memset(state[0][:, :], 0.0)

        mu, p_kk, p_ka, p_rk, p_lng, p_lnb = (par[:, a:b] for a, b in
                                              ((0, 14), (14, 18), (18, 22), (22, 26), (26, 30), (30, 34)))

        def levels(streams):
            return range(2, 5 if streams else 7)

        def dve_rwkv_tile(dve, tile, streams):
            D, A, E, L = tile_counts(tile, streams)
            did = ticker(RW_DVE, streams)

            def step(ins, name):
                ins.then_inc(s_rwd, did(name))

            def own(name):
                dve.wait_ge(s_rwd, D(name))

            dve.wait_ge(s_rwa, tile_start(RW_ACT, tile, streams))
            dve.wait_ge(s_rwe, tile_start(RW_PE, tile, streams))
            if streams:
                cur = rw[:, :, 1 + SEQ:1 + TOK].rearrange("p i (s t) -> p i s t", t=NEW)
                mix4 = xm[:, :, :].rearrange("p i (s t) -> p i s t", t=NEW)
                step(dve.tensor_tensor(mix4[:, :, :, 1:NEW], cur[:, :, :, 0:NEW - 1], cur[:, :, :, 1:NEW],
                                       ALU.subtract), "diff")
                step(dve.tensor_tensor(mix4[:, :, :, 0], shift[:, :].rearrange("p (s i) -> p i s", s=NSEQ),
                                       cur[:, :, :, 0], ALU.subtract), "diff0")
                own("diff0")
                now = rw[:, :, 1 + SEQ:1 + TOK]
            else:
                now = rw[:, :, bass.ds(tile * P + 1, P)]
                step(dve.tensor_tensor(xm[:, :, :], rw[:, :, bass.ds(tile * P, P)], now, ALU.subtract), "diff")
                own("diff")
            step(dve.tensor_tensor(xm[:, :, :], xm[:, :, :], stretch(mu, 14, P), ALU.mult), "mix")
            own("mix")
            step(dve.tensor_tensor(xm[:, :, :], xm[:, :, :], now, ALU.add), "xm")
            own("xm")
            if streams:
                step(dve.memset(state_raw[:, :, :], 0.0), "clear")
            step(dve.tensor_tensor(F4(t6), xm[:, 4:8, :], stretch(p_kk, 4, P), ALU.mult), "kkr")
            dve.wait_ge(s_rwa, A("tanh_g"))
            step(dve.tensor_scalar(sig_g[:, :], sig_g[:, :], 0.5, 0.5, ALU.mult, ALU.add), "sig_g")
            dve.wait_ge(s_rwa, A("sig_w"))
            step(dve.tensor_scalar(t0, t0, DECAY, DECAY, ALU.mult, ALU.add), "e")
            own("e")
            step(dve.tensor_tensor_scan(t1, reset_s if streams else reset_p, t0, 0.0, ALU.mult, ALU.add), "scan")
            own("scan")
            step(dve.tensor_tensor(t0, t1, t0, ALU.subtract), "eex")
            dve.wait_ge(s_rwa, A("sig_a"))
            step(dve.tensor_scalar(t5, t5, 0.5, 0.5, ALU.mult, ALU.add), "a")
            own("a")
            step(dve.scalar_tensor_tensor(out=F4(t8), in0=F4(t5), scalar=-1.0, in1=stretch(p_ka, 4, P),
                                          op0=ALU.add, op1=ALU.mult), "ka")
            own("ka")
            step(dve.scalar_tensor_tensor(out=F4(t8), in0=F4(t8), scalar=1.0, in1=xm[:, 4:8, :],
                                          op0=ALU.add, op1=ALU.mult), "kmod")
            own("kmod")
            step(dve.tensor_tensor(F4(t9), xm[:, 0:4, :], F4(t8), ALU.mult), "rk")
            own("rk")
            step(dve.tensor_tensor(F4(t9), F4(t9), stretch(p_rk, 4, P), ALU.mult), "rkr")
            dve.wait_ge(s_rwa, A("root"))
            step(dve.tensor_scalar(t7, t7, 1e-12, None, ALU.max), "floor")
            own("floor")
            step(dve.reciprocal(t7, t7), "inverse")
            own("inverse")
            step(dve.tensor_tensor(t6, t6, t7, ALU.mult), "kk")
            own("kk")
            step(dve.scalar_tensor_tensor(out=ar[:, :, 0, :], in0=F4(t6), scalar=-1.0, in1=F4(t4),
                                          op0=ALU.mult, op1=ALU.mult), "abar")
            step(dve.tensor_tensor(t6, t6, t5, ALU.mult), "kka")
            step(dve.tensor_tensor(ar[:, :, 1, :], xm[:, 0:4, :], F4(t2), ALU.mult), "rbar")
            step(dve.tensor_tensor(kT, t8, t3, ALU.mult), "khat")
            own("kka")
            step(dve.tensor_tensor(bT, t6, t3, ALU.mult), "bhat")
            dve.wait_ge(s_rwe, E("bonus"))
            step(dve.tensor_tensor(F4(bonus), F4(ps[:, 4, :]), xm[:, 8:12, :], ALU.mult), "bonus")
            if streams:
                step(dve.tensor_copy(p_end[:, :].rearrange("p (k s) -> p k s", k=4),
                                     F4(t2).rearrange("p k (s t) -> p k s t", t=NEW)[:, :, :, NEW - 1]), "p_end")
            else:
                for c in range(2):
                    step(dve.tensor_tensor(F4(decay_mask[c][:, :]), same(two_heads, 4),
                                           F4(t2)[:, :, 64 * c + 63:64 * c + 64].broadcast_to([P, 4, P]),
                                           ALU.mult), f"p_end{c}")
            own("p_end" if streams else "p_end1")
            for h in range(8):
                dve.wait_ge(s_rwe, E(f"gram{h}"))
                step(dve.tensor_tensor(gram[:, h, :].rearrange("p (a c) -> p a c", a=2),
                                       ps[:, h, :].rearrange("p (a c) -> p a c", a=2),
                                       same(tril_s if streams else tril_p, 2), ALU.mult), f"gram{h}")
            own("gram7")
            step(dve.tensor_tensor(H8(q_inv), gram[:, :, 0:P], same(level_mask(1), 8), ALU.mult), "q_first")
            own("q_first")
            step(dve.tensor_tensor(H8(q_inv), H8(q_inv), same(ident[:, :], 8), ALU.add), "q_unit")
            last = levels(streams)[-1]
            for lv in levels(streams):
                if lv < last:
                    dve.wait_ge(s_rwe, E(f"tn{lv}"))
                    step(dve.tensor_tensor(t_inv, t_inv, flat[:, 4 * 512:6 * 512], ALU.add), f"tn{lv}")
                dve.wait_ge(s_rwe, E(f"qn{lv}"))
                step(dve.tensor_tensor(q_inv, q_inv, flat[:, 6 * 512:8 * 512], ALU.add), f"qn{lv}")
            if streams:
                for h in range(2):
                    rows = slice(64 * h, 64 * h + 64)
                    dve.wait_ge(s_rwe, E("y"))
                    dve.wait_ge(s_rwa, A("y0"))
                    step(dve.tensor_tensor(
                        F4(y_t[rows, :]), F4(y0_t[rows, :]),
                        flat[rows, 5 * 512:7 * 512].rearrange("p (k h c) -> p k h c", k=4, h=2)[:, :, h, :],
                        ALU.add), f"yt{h}")
            else:
                dve.wait_ge(s_rwe, E("s0"))
                step(dve.tensor_tensor(state[1][:, :], state[0][:, :], ps[:, 2, :], ALU.add), "sadd0")
                own("sadd0")
                step(dve.tensor_tensor(state[1][:, :], state[1][:, :], decay_mask[0][:, :], ALU.mult), "s0")
                dve.wait_ge(s_rwe, E("s1"))
                step(dve.tensor_tensor(state[0][:, :], state[1][:, :], ps[:, 2, :], ALU.add), "sadd1")
                own("sadd1")
                step(dve.tensor_tensor(state[0][:, :], state[0][:, :], decay_mask[1][:, :], ALU.mult), "s1")
            dve.wait_ge(s_rwe, E("mean"))
            step(dve.scalar_tensor_tensor(out=yc[:, :], in0=ps[:, 7, :], scalar=-1 / HEAD, in1=y_t[:, :],
                                          op0=ALU.mult, op1=ALU.add), "yc")
            dve.wait_ge(s_rwa, A("y_root"))
            step(dve.reciprocal(ysq[:, :], ysq[:, :]), "y_inverse")
            own("y_inverse")
            step(dve.tensor_tensor(yc[:, :], yc[:, :], ysq[:, :], ALU.mult), "yn")
            own("yn")
            step(dve.tensor_tensor(F4(yc[:, :]), F4(yc[:, :]), stretch(p_lng, 4, P), ALU.mult), "y_gain")
            own("y_gain")
            step(dve.tensor_tensor(F4(yc[:, :]), F4(yc[:, :]), stretch(p_lnb, 4, P), ALU.add), "y_shift")
            own("y_shift")
            step(dve.tensor_tensor(yc[:, :], yc[:, :], bonus, ALU.add), "y_bonus")
            own("y_bonus")
            step(dve.tensor_tensor(yc[:, :], yc[:, :], gate[:, :], ALU.mult), "y_gate")
            own("y_gate")
            dve.wait_ge(s_rwa, A("hi"))
            cols = slice(SEQ, TOK) if streams else bass.ds(tile * P, P)
            step(dve.tensor_tensor(act_lo[:, 4:8, cols], F4(yc[:, :]), act_hi[:, 4:8, cols].bitcast(F32),
                                   ALU.subtract), "lo")
            if streams:
                for h in range(8):
                    rows = slice(64 * (h % 2), 64 * (h % 2) + 64)
                    part = streams_state[rows, :, h // 2, 64 * (h % 2):64 * (h % 2) + 64]
                    dve.wait_ge(s_rwe, E(f"s{h}"))
                    step(dve.tensor_tensor(part, part, ps[rows, h % 2, :].rearrange("p (s v) -> p s v", s=NSEQ),
                                           ALU.add), f"sadd{h}")
                    own(f"sadd{h}")
                    step(dve.tensor_tensor(
                        part, part, p_end[rows, :].rearrange("p (k s o) -> p k s o", k=4, o=1)[:, h // 2]
                        .broadcast_to([64, NSEQ, 64]), ALU.mult), f"s{h}")

        def act_rwkv_tile(act, tile, streams):
            D, A, E, L = tile_counts(tile, streams)
            did = ticker(RW_ACT, streams)

            def step(ins, name):
                ins.then_inc(s_rwa, did(name))

            if streams:
                act.wait_ge(s_rwe, E("prompt_state"))
                step(act.activation(prompt_state[:, :], ps[:, 7, :], ACT.Copy), "prompt_state")
            act.wait_ge(s_rwd, D("xm"))
            act.wait_ge(s_rwe, tile_start(RW_PE, tile, streams))
            step(act.activation(tanh_w[0:64, :], xm[0:64, 12, :], ACT.Tanh), "tanh_w")
            step(act.activation(sig_g[:, :], xm[:, 13, :], ACT.Tanh, scale=0.5), "tanh_g")
            act.wait_ge(s_rwe, E("lora"))
            step(act.activation(t0, ps[:, 0, :], ACT.Tanh, scale=0.5), "sig_w")
            step(act.activation(t5, ps[:, 1, :], ACT.Tanh, scale=0.5), "sig_a")
            step(act.activation(gate[:, :], ps[:, 2, :], ACT.Copy), "gate")
            act.wait_ge(s_rwd, D("kkr"))
            step(act.activation(t7, t6, ACT.Square), "kk_sq")
            act.wait_ge(s_rwd, D("eex"))
            step(act.activation(t2, t1, ACT.Exp, scale=-1.0), "p")
            step(act.activation(t3, t1, ACT.Exp), "p_inv")
            step(act.activation(t4, t0, ACT.Exp, scale=-1.0), "p_ex")
            act.wait_ge(s_rwe, E("norm"))
            step(act.activation(t7, ps[:, 3, :], ACT.Sqrt), "root")
            act.wait_ge(s_rwe, E("turn"))
            step(act.activation(b_tok, ps[:, 5, :], ACT.Copy), "b_tok")
            step(act.activation(k_tok, ps[:, 6, :], ACT.Copy), "k_tok")
            step(act.activation(v_tok, ps[:, 7, :], ACT.Copy), "v_tok")
            act.wait_ge(s_rwe, E("q_turn"))
            step(act.activation(t_inv, flat[:, 0:1024], ACT.Copy), "t_first")
            for lv in levels(streams):
                act.wait_ge(s_rwe, E(f"y1_{lv}"))
                step(act.activation(y1, flat[:, 2 * 512:4 * 512], ACT.Copy), f"y1_{lv}")
            if streams:
                for q in range(NSEQ):
                    act.wait_ge(s_rwe, E(f"turn{q}"))
                    step(act.activation(streams_state[:, q, :, :], F4(ps[:, q, :]), ACT.Copy), f"turn{q}")
                act.wait_ge(s_rwe, E("ra"))
                both = flat[:, 0:1024].rearrange("p (k a c) -> p k a c", k=4, a=2)
                step(act.activation(F4(r1t), both[:, :, 0, :], ACT.Copy), "r1t")
                step(act.activation(F4(y0_t[:, :]), both[:, :, 1, :], ACT.Copy), "y0")
                act.wait_ge(s_rwe, E("r"))
                step(act.activation(r1, ps[:, 2, :], ACT.Copy), "r")
                act.wait_ge(s_rwe, E("u"))
                step(act.activation(u_tok, ps[:, 4, :], ACT.Copy), "u")
            else:
                for c in range(2):
                    act.wait_ge(s_rwe, E(f"r{c}"))
                    rows = slice(64 * c, P)
                    step(act.activation(r1[rows, :], ps[rows, 0, :], ACT.Copy), f"r{c}")
                    act.wait_ge(s_rwe, E(f"u{c}"))
                    rows = slice(64 * c, 64 * c + 64)
                    step(act.activation(u_tok[rows, :], ps[rows, 1, :], ACT.Copy), f"u{c}")
                act.wait_ge(s_rwe, E("y"))
                for h in range(2):
                    rows = slice(64 * h, 64 * h + 64)
                    step(act.activation(
                        F4(y_t[rows, :]),
                        flat[rows, 3 * 512:5 * 512].rearrange("p (k h c) -> p k h c", k=4, h=2)[:, :, h, :],
                        ACT.Copy), f"yt{h}")
            act.wait_ge(s_rwd, D("yc"))
            step(act.activation(ysq[:, :], yc[:, :], ACT.Square), "y_sq")
            act.wait_ge(s_rwe, E("var"))
            step(act.activation(ysq[:, :], ps[:, 0, :], ACT.Sqrt, bias=eps[:, 2:3], scale=1 / HEAD), "y_root")
            act.wait_ge(s_rwd, D("y_gate"))
            cols = slice(SEQ, TOK) if streams else bass.ds(tile * P, P)
            step(act.activation(act_hi[:, 4:8, cols], F4(yc[:, :]), ACT.Copy), "hi")
            if streams:
                for q in range(NSEQ):
                    act.wait_ge(s_rwe, E(f"out{q}"))
                    step(act.activation(state_raw[:, 4 * q:4 * q + 4, :], F4(ps[:, q, :]), ACT.Copy), f"out{q}")

        def pool_rwkv_tile(pool, tile, streams):
            D, A, E, L = tile_counts(tile, streams)
            did = ticker(RW_POOL, streams)
            for lv in levels(streams):
                pool.wait_ge(s_rwd, D("gram7"))
                if lv > 2:
                    pool.wait_ge(s_rwe, E(f"y1_{lv - 1}"))
                pool.tensor_tensor(H8(lt_m), gram[:, :, 0:P], same(level_mask(lv), 8), ALU.mult)\
                    .then_inc(s_rwp, did(f"lt{lv}"))
            if streams:
                for h in range(8):
                    pool.wait_ge(s_rwa, A("u"))
                    pool.wait_ge(s_rwe, E("y") if h < 2 else E(f"s{h - 2}"))
                    mask = stream_rows.rearrange("p (s o) -> p s o", o=1).broadcast_to([P, NSEQ, HEAD])
                    for i, src in enumerate((u_tok, v_tok)):
                        pool.tensor_tensor(spread[h % 2][i], same(src[:, HEAD * h:HEAD * h + HEAD], NSEQ), mask,
                                           ALU.mult).then_inc(s_rwp, did(f"spread{h}_{i}"))

        def pe_rwkv_tile(pe, tile, streams):
            D, A, E, L = tile_counts(tile, streams)
            did = ticker(RW_PE, streams)

            def step(ins, name):
                ins.then_inc(s_rwe, did(name))

            pe.wait_ge(s_rwa, tile_start(RW_ACT, tile, streams))
            pe.wait_ge(s_rwd, tile_start(RW_DVE, tile, streams))
            if streams:
                for p in range(4):
                    mm = pe.transpose(ps[:, 7, p * P:(p + 1) * P], state[0][:, p * P:(p + 1) * P], ident[:, :])
                step(mm, "prompt_state")
            pe.wait_ge(s_rwa, A("tanh_w"))
            pe.wait_ge(s_rwd, D("sig_g"))
            for p in range(4):
                c = slice(p * P, (p + 1) * P)
                pe.matmul(ps[:, 0, c], lora_wa[0:64, c], tanh_w[0:64, :], start=True, stop=False)
                pe.matmul(ps[:, 0, c], bias_rows[0:1, c], ones[0:1, :], start=False, stop=True)
                pe.matmul(ps[:, 1, c], lora_wa[64:128, c], xm[64:128, 12, :], start=True, stop=False)
                pe.matmul(ps[:, 1, c], bias_rows[32:33, c], ones[32:33, :], start=False, stop=True)
                mm = pe.matmul(ps[:, 2, c], lora_g[:, c], sig_g[:, :], start=True, stop=True)
            step(mm, "lora")
            pe.wait_ge(s_rwa, A("kk_sq"))
            step(pe.matmul(ps[:, 3, :], two_heads, t7, start=True, stop=True), "norm")
            pe.wait_ge(s_rwd, D("rkr"))
            step(pe.matmul(ps[:, 4, :], two_heads, t9, start=True, stop=True), "bonus")
            pe.wait_ge(s_rwd, D("bhat"))
            for bank, src in ((5, F4(bT)), (6, F4(kT)), (7, xm[:, 8:12, :])):
                if streams and bank == 7:
                    pe.wait_ge(s_rwa, A("prompt_state"))
                for p in range(4):
                    mm = pe.transpose(ps[:, bank, p * P:(p + 1) * P], src[:, p, :], ident[:, :])
            step(mm, "turn")
            for h in range(8):
                rows = slice(64 * (h % 2), 64 * (h % 2) + 64)
                if h == 3:
                    pe.wait_ge(s_rwa, A("root"))
                if h == 4:
                    pe.wait_ge(s_rwd, D("bonus"))
                if h == 5:
                    pe.wait_ge(s_rwa, A("v_tok"))
                both = ar[rows, h // 2, :, :].rearrange("p a c -> p (a c)")
                pe.matmul(ps[:, h, 0:256], F4(bT)[rows, h // 2, :], both, start=True, stop=True)
                step(pe.matmul(ps[:, h, 256:512], F4(kT)[rows, h // 2, :], both, start=True, stop=True), f"gram{h}")
            pe.wait_ge(s_rwd, D("q_unit"))
            for h in range(8):
                mm = pe.transpose(flat[:, h * P:(h + 1) * P], H8(q_inv)[:, h, :], ident[:, :])
            step(mm, "q_turn")
            last = levels(streams)[-1]
            for lv in levels(streams):
                pe.wait_ge(s_rwp, L(f"lt{lv}"))
                if lv == 2:
                    pe.wait_ge(s_rwa, A("t_first"))
                else:
                    pe.wait_ge(s_rwd, D(f"tn{lv - 1}"))
                for h in range(8):
                    mm = pe.matmul(flat[:, 1024 + h * P:1024 + (h + 1) * P], H8(lt_m)[:, h, :], H8(t_inv)[:, h, :],
                                   start=True, stop=True)
                step(mm, f"y1_{lv}")
                pe.wait_ge(s_rwa, A(f"y1_{lv}"))
                if lv > 2:
                    pe.wait_ge(s_rwd, D(f"qn{lv - 1}"))
                if lv < last:
                    for h in range(8):
                        mm = pe.matmul(flat[:, 2048 + h * P:2048 + (h + 1) * P], H8(q_inv)[:, h, :],
                                       H8(y1)[:, h, :], start=True, stop=True)
                    step(mm, f"tn{lv}")
                for h in range(8):
                    mm = pe.matmul(flat[:, 3072 + h * P:3072 + (h + 1) * P], H8(y1)[:, h, :],
                                   H8(q_inv)[:, h, :], start=True, stop=True)
                step(mm, f"qn{lv}")
            pe.wait_ge(s_rwd, D(f"qn{last}"))

            def y_terms(bank, sources):
                for h in range(8):
                    c = (h // 2 % 2) * 256 + h % 2 * P
                    out = ps[:, bank + h // 4, c:c + P]
                    pair = slice(h // 2 * P, h // 2 * P + P)
                    pe.matmul(out, u_tok[:, pair], gram[:, h, P:2 * P], start=True, stop=False)
                    mm = pe.matmul(out, v_tok[:, pair], gram[:, h, 3 * P:4 * P], start=False, stop=not sources)
                    for n, s in enumerate(sources):
                        mm = pe.matmul(out[:, 64 * n:64 * n + 64], s[:, pair], ar[:, h // 2, 1, 64 * n:64 * n + 64],
                                       start=False, stop=(n == 1))
                return mm

            if streams:
                pe.wait_ge(s_st, 32)
                for q in range(NSEQ):
                    for p in range(4):
                        mm = pe.transpose(ps[:, q, p * P:(p + 1) * P], state_raw[:, 4 * q + p, :], ident[:, :])
                    step(mm, f"turn{q}")
                for q in range(NSEQ):
                    pe.wait_ge(s_rwa, A(f"turn{max(q, 1)}"))
                    for p in range(4):
                        for a in range(2):
                            c = p % 2 * 256 + a * P + NEW * q
                            mm = pe.matmul(ps[:, p // 2, c:c + NEW], streams_state[:, q, p, :],
                                           ar[:, p, a, NEW * q:NEW * q + NEW], start=True, stop=True)
                step(mm, "ra")
                pe.wait_ge(s_rwa, A("r1t"))
                for h in range(8):
                    if h % 2 == 0:
                        pair = slice(h * HEAD, h * HEAD + P)
                        pe.matmul(ps[:, 2, pair], F4(r1t)[:, h // 2, :], ident[:, :], start=True, stop=False)
                    mm = pe.matmul(ps[:, 2, h * HEAD:(h + 1) * HEAD], gram[:, h, 256:384],
                                   v_tok[:, h * HEAD:(h + 1) * HEAD], start=False, stop=(h % 2 == 1))
                step(mm, "r")
                pe.wait_ge(s_rwa, A("r"))
                for h in range(8):
                    mm = pe.matmul(ps[:, 4, h * HEAD:(h + 1) * HEAD], H8(q_inv)[:, h, :],
                                   r1[:, h * HEAD:(h + 1) * HEAD], start=True, stop=True)
                step(mm, "u")
                pe.wait_ge(s_rwa, A("u"))
                step(y_terms(5, ()), "y")
                pe.wait_ge(s_rwd, D("yt1"))
            else:
                for c in range(2):
                    if c:
                        pe.wait_ge(s_rwd, D("s0"))
                    for h in range(8):
                        if h % 2 == 0:
                            pair = slice(h * HEAD, h * HEAD + P)
                            pe.matmul(ps[:, 0, pair], ar[:, h // 2, 0, :], state[c][:, pair], start=True, stop=False)
                        mm = pe.matmul(ps[:, 0, h * HEAD:(h + 1) * HEAD], gram[:, h, 256:384],
                                       v_tok[:, h * HEAD:(h + 1) * HEAD], start=False, stop=(h % 2 == 1))
                    step(mm, f"r{c}")
                    pe.wait_ge(s_rwa, A(f"r{c}"))
                    for h in range(8):
                        mm = pe.matmul(ps[:, 1, h * HEAD:(h + 1) * HEAD], H8(q_inv)[:, h, :],
                                       r1[:, h * HEAD:(h + 1) * HEAD], start=True, stop=True)
                    step(mm, f"u{c}")
                    pe.wait_ge(s_rwa, A(f"u{c}"))
                    if c:
                        step(y_terms(3, state), "y")
                    rows = slice(64 * c, 64 * c + 64)
                    for p in range(4):
                        pair = slice(p * P, (p + 1) * P)
                        pe.matmul(ps[:, 2, pair], b_tok[rows, pair], u_tok[rows, pair], start=True, stop=False)
                        mm = pe.matmul(ps[:, 2, pair], k_tok[rows, pair], v_tok[rows, pair], start=False, stop=True)
                    step(mm, f"s{c}")
                pe.wait_ge(s_rwa, A("yt1"))
            step(pe.matmul(ps[:, 7, :], two_heads, y_t[:, :], start=True, stop=True), "mean")
            pe.wait_ge(s_rwa, A("y_sq"))
            step(pe.matmul(ps[:, 0, :], two_heads, ysq[:, :], start=True, stop=True), "var")
            if streams:
                pe.wait_ge(s_rwa, A("y_root"))
                for h in range(8):
                    pe.wait_ge(s_rwp, L(f"spread{h}_1"))
                    if h >= 2:
                        pe.wait_ge(s_rwd, D(f"sadd{h - 2}"))
                    pair = slice(h // 2 * P, h // 2 * P + P)
                    for i, w in enumerate((b_tok, k_tok)):
                        mm = pe.matmul(ps[:, h % 2, :], w[:, pair], spread[h % 2][i].rearrange("p s v -> p (s v)"),
                                       start=(i == 0), stop=(i == 1))
                    step(mm, f"s{h}")
                pe.wait_ge(s_rwd, D("s7"))
                for q in range(NSEQ):
                    for p in range(4):
                        mm = pe.transpose(ps[:, q, p * P:(p + 1) * P], streams_state[:, q, p, :], ident[:, :])
                    step(mm, f"out{q}")

        def rwkv(eng, setup, tile):
            setup(eng)
            with eng.Fori(0, 4) as t:
                tile(eng, t, False)
            tile(eng, None, True)

        def sp_mixer_out(sp, stage, w):
            r0 = before(stage, 1)
            for i in range(OUT_N * KD):
                n, k = i // KD, i % KD
                sp_row(sp, i, r0, r0 // 2, w[k * P:(k + 1) * P, n * 512:(n + 1) * 512])

        def pe_mixer_out(pe, stage):
            pe_rows(pe, KD, OUT_N, before(stage, 1), before(stage, 2), act_hi, act_lo, lambda k: None)

        def act_mixer_out(act, stage):
            r0 = before(stage, 1)
            for i in range(OUT_N * KD):
                act_split_row(act, i, r0, r0 // 2)

        def dve_mixer_out(dve, stage):
            r0, g0 = before(stage, 1), before(stage, 2)

            def evict(g, t):
                wait_output(dve, g, t, KD, r0, g0)
                bank = (ODD_BANKS if g % 2 else EVEN_BANKS)[t]
                dve.tensor_copy(y[:, t, g * 512:(g + 1) * 512], ps[:, bank, :]).then_inc(s_evict, 1)

            splits_and_outputs(KD, OUT_N, lambda i: dve_split_row(dve, i, r0), evict)

        N_GPAIR = STAGES["gm_in"][0]
        GROUPS = D // P
        spatial_loads = 4 + 2 * NSEQ
        gm_in = io["gm_w_in"][0]

        def sp_gmlp(sp):
            n0, r0, g0 = (before("gm_in", i) for i in range(3))
            sp.wait_ge(s_evict, g0 * TT + 1)
            sp.dma_start(ws[:, :, :], io["gm_w_s"][0].rearrange("g t s -> t g s")).then_inc(s_gm, 16)
            sp.wait_ge(s_ws0, 1)
            for b in range(NSEQ):
                at = slice(NEW * b, NEW * b + NEW)
                sp.dma_start(ws_new[at, :, at], io["gm_w_s"][0, :, 0:NEW, 0:NEW].rearrange("g t s -> t g s"))\
                  .then_inc(s_gm, 16)
                sp.dma_start(bs_new[:, :, at], io["gm_b_s"][0:1, :, 0:NEW]).then_inc(s_gm, 16)
            sp.dma_start(bs[:, :, :], io["gm_b_s"][0:1]).then_inc(s_gm, 16)
            sp.dma_start(ln_g[:, :], io["gm_ln_g"].broadcast_to([P, D])).then_inc(s_gm, 16)
            sp.dma_start(ln_b[:, :], io["gm_ln_b"].broadcast_to([P, D])).then_inc(s_gm, 16)
            w = gm_in.rearrange("(k p) n -> p k n", p=P)
            with sp.Fori(0, N_GPAIR) as j:
                sp_pair(sp, n0 + j, lambda c: w[:, :, bass.ds(j * 256 + c * P, P)])
            for i in range(OUT_N * KD):
                n, k = i // KD, i % KD
                sp_row(sp, i, r0, r0 // 2, gm_in[k * P:(k + 1) * P, D + n * 512:D + (n + 1) * 512])

        def pe_gmlp(pe):
            n0, r0, g0 = (before("gm_in", i) for i in range(3))
            with pe.Fori(0, N_GPAIR) as j:
                pe.wait_ge(s_evict, g0 * TT + 1)
                pe_pair(pe, n0 + j)
            pe.wait_ge(s_gm, 16 * spatial_loads)
            for g in range(GROUPS):
                pe.transpose(ps[:, 4 + g // 4, g % 4 * P:(g % 4 + 1) * P], ws[:, g, :], ident[:, :])
                mm = pe.transpose(ps[:, 6 + g // 4, g % 4 * P:(g % 4 + 1) * P], ws_new[:, g, :], ident[:, :])
            mm.then_inc(s_wt, 1)
            for h in range(2):
                pe.wait_ge(s_pair_read[h], n0 + N_GPAIR + 1)
            pe.wait_ge(s_wt_read, 4)
            pe_rows(pe, KD, OUT_N, r0, g0, act_hi, act_lo, lambda k: None)
            pe.wait_ge(s_evict, (g0 + OUT_N) * TT + 1)
            for t in range(TT):
                w, b = (ws_t, bs) if t < TT - 1 else (ws_new_t, bs_new)
                pe.wait_ge(s_v, t + 1)
                if t >= 4:
                    pe.wait_ge(s_gated, t - 3)
                for g in range(GROUPS):
                    bank = t % 4 * 2 + g // 4
                    if g % 4 == 0:
                        pe.matmul(ps[:, bank, :], ones[0:1, :], b[0:1, g:g + 4, :].rearrange("o g t -> o (g t)"),
                                  start=True, stop=False)
                    mm = pe.matmul(ps[:, bank, g % 4 * P:(g % 4 + 1) * P], y[:, t, g * P:(g + 1) * P], w[:, g, :],
                                   start=False, stop=(g % 4 == 3))
                mm.then_inc(s_spatial, 1)

        def act_gmlp(act):
            n0, r0, g0 = (before("gm_in", i) for i in range(3))

            def tile(j, last):
                for c in range(2):
                    act.wait_ge(s_pair_mm[c], n0 + j + 2)
                    act.activation(halves(u_cols, 2 * j + c), wide(2 * c), ACT.Gelu).then_inc(s_pair_read[c], 1)
                    if not last:
                        act_split_pair(act, c, n0 + j + 1)

            act_split_pair(act, 0, n0)
            act_split_pair(act, 1, n0)
            with act.Fori(0, N_GPAIR - 1) as j:
                tile(j, False)
            act_split_row(act, 0, r0, r0 // 2)
            act_split_row(act, 1, r0, r0 // 2)
            tile(N_GPAIR - 1, True)

            def split(i):
                if i > 1:
                    act_split_row(act, i, r0, r0 // 2)

            def evict(g, t):
                wait_output(act, g, t, KD, r0, g0)
                act.activation(y[:, t, g * 512:(g + 1) * 512], ps[:, (ODD_BANKS if g % 2 else EVEN_BANKS)[t], :],
                               ACT.Gelu, accum_out=ln_stat[:, g, t:t + 1]).then_inc(s_evict, 1)

            splits_and_outputs(KD, OUT_N, split, evict)
            act.wait_ge(s_sq[0], 5 * 4)
            for t in range(TT):
                act.wait_ge(s_mean, t + 1)
                if t:
                    act.wait_ge(s_vsq, t)
                act.activation(squares[0], y[:, t, :], ACT.Square, bias=ln_stat[:, 2, t:t + 1],
                               accum_out=ln_stat[:, 3, t:t + 1]).then_inc(s_vsq, 1)
            act.wait_ge(s_vsq, TT)
            act.activation(ln_stat[:, 4, :], ln_stat[:, 3, :], ACT.Sqrt, bias=eps[:, 3:4], scale=1 / D)\
               .then_inc(s_vroot, 1)
            for t in range(TT):
                act.wait_ge(s_gated, t + 1)
                act.activation(act_hi[:, :, t * P:(t + 1) * P], gated[t % 2], ACT.Copy).then_inc(s_ghi, 1)

        def dve_gmlp(dve):
            n0, r0, g0 = (before("gm_in", i) for i in range(3))
            dve_split_pair(dve, 0, n0)
            dve_split_pair(dve, 1, n0)
            with dve.Fori(0, N_GPAIR - 1) as j:
                dve_split_pair(dve, 0, n0 + j + 1)
                dve_split_pair(dve, 1, n0 + j + 1)
            dve_split_row(dve, 0, r0)
            dve_split_row(dve, 1, r0)
            dve.memset(ws_t[64:P, :, 0:64], 0.0).then_inc(s_wt_read, 1)
            dve.wait_ge(s_wt, 1)
            chunk = ps[:, 4:6, :].rearrange("p a (g t) -> p (a g) t", g=4)
            dve.tensor_copy(ws_t[0:64, :, :], chunk[0:64, :, :]).then_inc(s_wt_read, 1)
            dve.tensor_copy(ws_t[64:P, :, 64:P], chunk[64:P, :, 64:P]).then_inc(s_wt_read, 1)
            dve.tensor_copy(ws_new_t[:, :, :], ps[:, 6:8, :].rearrange("p a (g t) -> p (a g) t", g=4))\
               .then_inc(s_wt_read, 1)
            for i in range(2, OUT_N * KD):
                dve_split_row(dve, i, r0)
            for t in range(TT):
                dve.wait_ge(s_evict, (g0 + 1) * TT + t + 2)
                dve.tensor_scalar(ln_stat[:, 2, t:t + 1], ln_stat[:, 0, t:t + 1], ln_stat[:, 1, t:t + 1], -1 / D,
                                  ALU.add, ALU.mult).then_inc(s_mean, 1)
            dve.wait_ge(s_vroot, 1)
            dve.wait_ge(s_mean, TT)
            dve.reciprocal(ln_stat[:, 5, :], ln_stat[:, 4, :]).then_inc(s_vinv, 1)
            dve.wait_ge(s_gm, 16 * spatial_loads)
            dve.wait_ge(s_vinv, 1)
            for s in range(TT + 2):
                if s < TT:
                    v = y[:, s, :]
                    dve.scalar_tensor_tensor(out=v, in0=v, scalar=ln_stat[:, 2, s:s + 1], in1=ln_g[:, :],
                                             op0=ALU.add, op1=ALU.mult).then_inc(s_vgain, 1)
                    dve.wait_ge(s_vgain, s + 1)
                    dve.scalar_tensor_tensor(out=v, in0=v, scalar=ln_stat[:, 5, s:s + 1], in1=ln_b[:, :],
                                             op0=ALU.mult, op1=ALU.add).then_inc(s_v, 1)
                if 0 <= s - 1 < TT:
                    t = s - 1
                    dve.wait_ge(s_spatial, t + 1)
                    if t >= 2:
                        dve.wait_ge(s_glo, t - 1)
                    dve.tensor_tensor(gated[t % 2], u_cols[:, :, t * P:(t + 1) * P],
                                      flat[:, t % 4 * 1024:t % 4 * 1024 + 1024].rearrange("p (g t) -> p g t", g=GROUPS),
                                      ALU.mult).then_inc(s_gated, 1)
                if 0 <= s - 2 < TT:
                    t = s - 2
                    dve.wait_ge(s_ghi, t + 1)
                    cols = slice(t * P, (t + 1) * P)
                    dve.tensor_tensor(act_lo[:, :, cols], gated[t % 2], act_hi[:, :, cols].bitcast(F32),
                                      ALU.subtract).then_inc(s_glo, 1)
            dve.wait_ge(s_glo, TT)
            dve.wait_ge(s_new_v, 16)

        def store(sp, dst, src):
            sp.dma_start(dst, src).then_inc(s_store, 16)
            stores.append(16)

        stores = []

        @block.sync
        def _(sp):
            sp.dma_start(x[:, 0:4, :], io["x_prompt"][0].rearrange("(t p) d -> p t d", p=P)).then_inc(s_x, 16)
            sp.dma_start(x[:, 4, :], io["x_sample"].rearrange("s t d -> (s t) d")).then_inc(s_x, 16)
            sp_norm_gains(sp, 0)
            sp_ffn(sp, 0)
            sp_norm_gains(sp, 1)
            sp.wait_ge(s_xn, 10)
            sp_even_in(sp)
            sp_even_outputs(sp)
            sp_streams(sp)
            sp_rwkv(sp)
            sp_norm_gains(sp, 2)
            sp_mixer_out(sp, "even_out", io["even_w_out"][0])
            sp.wait_ge(s_store, sum(stores))
            sp_ffn(sp, 1)
            sp_norm_gains(sp, 3)
            sp_ffn(sp, 2)
            sp_norm_gains(sp, 4)
            sp_gmlp(sp)
            sp.wait_ge(s_v, TT)
            sp.dma_start(io["gv_s"][0].rearrange("s t d -> (s t) d"), y[:, TT - 1, :]).then_inc(s_new_v, 16)
            sp_mixer_out(sp, "gm_out", io["gm_w_out"][0])
            sp_norm_gains(sp, 5)
            sp_ffn(sp, 3)
            sp_norm_gains(sp, 6)
            for t in range(TT):
                sp.wait_ge(s_xnew, 5 * (NORMS - 1) + t + 1)
                if t < TT - 1:
                    store(sp, io["y_prompt"][0, t * P:(t + 1) * P, :], x[:, t, :])
                else:
                    store(sp, io["y_sample"].rearrange("s t d -> (s t) d"), x[:, t, :])
            sp.wait_ge(s_store, sum(stores))

        @block.gpsimd
        def _(pool):
            pool.memset(ident[:, :], 0.0).then_inc(s_const, 1)
            pool.memset(eps[:, 0:1], RMS_EPS).then_inc(s_const, 1)
            pool.memset(eps[:, 2:3], GN_EPS)
            pool.memset(eps[:, 3:4], LN_EPS)
            pool.memset(ones[:, :], 1.0)
            pool.memset(eps[:, 1:2], 4 * RMS_EPS).then_inc(s_const, 1)
            pool.wait_ge(s_const, 3)
            pool.affine_select(out=ident[:, :], in_=ident[:, :], compare_op=ALU.not_equal, fill=1.0,
                               base=0, pattern=[[-1, P]], channel_multiplier=1).then_inc(s_const, 1)
            pool.sem_inc(s_rwp, 1)
            pool.sem_inc(s_pm, 2)
            pool.sem_inc(s_pm2, 2)
            pool_norm(pool, 0)
            pool_norm(pool, 1)
            pool_prompt(pool)
            pool_streams(pool)
            rwkv(pool, lambda e: None, pool_rwkv_tile)
            for m in (2, 3, 4):
                pool_norm(pool, m)
            pool.memset(ws_new[:, :, :], 0.0).then_inc(s_ws0, 1)
            pool_norm(pool, 5)
            pool_norm(pool, 6)

        @block.scalar
        def _(act):
            act.sem_inc(s_pair_read[0], 1)
            act.sem_inc(s_rwa, 1)
            for s in (s_ex, s_ptr, s_oh, s_kta, s_cs, s_q2, s_ex2, s_ptr2, s_oh2):
                act.sem_inc(s, 2)
            act_norm(act, 0, 1, 0)
            act_ffn(act, 0)
            act_norm(act, 1, 0.5, 4)
            act_even_in(act)
            act_prompt(act)
            act_streams(act)
            rwkv(act, act_rwkv_setup, act_rwkv_tile)
            act_mixer_out(act, "even_out")
            act_norm(act, 2, 1, before("ffn1", 2))
            act_ffn(act, 1)
            act_norm(act, 3, 0.5, before("ffn2", 2))
            act_ffn(act, 2)
            act_norm(act, 4, 0.5, before("gm_in", 2))
            act_gmlp(act)
            act_mixer_out(act, "gm_out")
            act_norm(act, 5, 1, before("ffn3", 2))
            act_ffn(act, 3)
            act_norm(act, 6, 0.5, before("end", 2))

        @block.vector
        def _(dve):
            dve.sem_inc(s_rwd, 1)
            dve.sem_inc(s_pair_lo[0], 1)
            dve.sem_inc(s_pair_lo[1], 1)
            dve.sem_inc(s_pair_read[1], 1)
            dve.sem_inc(s_hid_lo, 1)
            dve.sem_inc(s_row_lo, 2)
            dve.sem_inc(s_evict, 1)
            for s in (s_nm, s_ol, s_ktd, s_nm2, s_ol2):
                dve.sem_inc(s, 2)
            dve_norm(dve, 0)
            dve_ffn(dve, 0)
            dve_norm(dve, 1)
            dve_even_in(dve)
            dve_even_outputs(dve)
            dve_prompt_c(dve)
            dve_prompt(dve)
            dve_streams(dve)
            rwkv(dve, dve_rwkv_setup, dve_rwkv_tile)
            dve.wait_ge(s_rwd, tile_counts(0, True)[0]("s7"))
            dve_mixer_out(dve, "even_out")
            dve_norm(dve, 2)
            dve_ffn(dve, 1)
            dve_norm(dve, 3)
            dve_ffn(dve, 2)
            dve_norm(dve, 4)
            dve_gmlp(dve)
            dve_mixer_out(dve, "gm_out")
            dve_norm(dve, 5)
            dve_ffn(dve, 3)
            dve_norm(dve, 6)

        @block.tensor
        def _(pe):
            pe.sem_inc(s_rwe, 1)
            pe.sem_inc(s_pair_mm[0], 1)
            pe.sem_inc(s_pair_mm[1], 1)
            pe.sem_inc(s_row_mm, 2)
            for s in (s_sc, s_pt, s_o, s_tk, s_c2, s_sc2, s_pt2, s_o2):
                pe.sem_inc(s, 2)
            pe_norm(pe, 0, 0)
            pe.wait_ge(s_alo, 5)
            pe_ffn(pe, 0)
            pe_norm(pe, 1, 4)
            pe.wait_ge(s_alo, 10)
            pe_even_in(pe)
            pe.wait_ge(s_last, 2)
            pe_even_outputs(pe)
            pe_prompt_c(pe)
            pe_prompt(pe)
            pe_streams(pe)
            rwkv(pe, pe_rwkv_setup, pe_rwkv_tile)
            pe.wait_ge(s_rwa, tile_counts(0, True)[1]("out7"))
            pe.wait_ge(s_rwd, tile_counts(0, True)[0]("s7"))
            pe_mixer_out(pe, "even_out")
            pe_norm(pe, 2, before("ffn1", 2))
            pe.wait_ge(s_alo, 15)
            pe_ffn(pe, 1)
            pe_norm(pe, 3, before("ffn2", 2))
            pe.wait_ge(s_alo, 20)
            pe_ffn(pe, 2)
            pe_norm(pe, 4, before("gm_in", 2))
            pe.wait_ge(s_alo, 25)
            pe_gmlp(pe)
            pe.wait_ge(s_glo, TT)
            pe_mixer_out(pe, "gm_out")
            pe_norm(pe, 5, before("ffn3", 2))
            pe.wait_ge(s_alo, 30)
            pe_ffn(pe, 3)


OUTS = {"y_prompt": (1, SEQ, D), "y_sample": (NSEQ, NEW, D), "fk_p": (1, 1, SEQ, FOXH, HEAD),
        "fv_p": (1, 1, SEQ, FOXH, HEAD), "fl_p": (1, 1, SEQ, FOXH), "rs_p": (1, 1, FOXH, HEAD, HEAD),
        "rsh_p": (1, 1, 1, 14 * P), "fk_s": (1, NSEQ, NEW, FOXH, HEAD), "fv_s": (1, NSEQ, NEW, FOXH, HEAD),
        "fl_s": (1, NSEQ, NEW, FOXH), "rs_s": (1, NSEQ, FOXH, HEAD, HEAD), "rsh_s": (1, NSEQ, 1, 14 * P),
        "gv_s": (1, NSEQ, NEW, D)}


def att_constants():
    import numpy as np

    s, t = np.arange(P)[:, None], np.arange(P)[None, :]
    c = np.zeros((P, ATT_N), np.float32)
    c[:, ATT_AT["tri_ones"]] = np.concatenate([s <= t, np.ones((P, 512 - P), bool)], 1)
    c[:, ATT_AT["tri_streams"]] = (s // NEW == t // NEW) & (s <= t)
    c[:, ATT_AT["causal"]] = np.where(t <= s, 0, -1e30)
    c[0:FOXH, ATT_AT["sel8"]] = np.eye(FOXH)
    c[:, ATT_AT["minus_ones"]] = -1
    c[0:FOXH, ATT_AT["minus_heads"]] = np.where(np.arange(FOXH)[:, None] == t // NEW, -1, 0)
    new = [np.where((t // NEW == b) & (t % NEW <= s % NEW), 0, -1e30) for b in range(NSEQ)]
    return c, np.concatenate(new, 1).astype(np.float32)


def rw_constants():
    import numpy as np

    s, t = np.arange(P)[:, None], np.arange(P)[None, :]
    c = np.zeros((P, RWC_N), np.float32)
    for name, chunk in (("tril_p", 64), ("tril_s", NEW)):
        block = s // chunk == t // chunk
        c[:, RWC_AT[name]] = np.concatenate([block & (s < t), block & (s <= t)], 1)
    c[:, RWC_AT["levels"]] = np.concatenate(
        [(s >> lv == t >> lv) & (s >> (lv - 1) & 1 == 0) & (t >> (lv - 1) & 1 == 1) for lv in range(1, 7)], 1)
    c[:, RWC_AT["two_heads"]] = s // HEAD == t // HEAD
    for name, chunk in (("reset_p", 64), ("reset_s", NEW)):
        c[:, RWC_AT[name]] = np.arange(512) % chunk != 0
    c[:, RWC_AT["stream_rows"]] = s // NEW == np.arange(NSEQ)
    return c


_INS = ["x_prompt", "x_sample", "cache_fox_k", "cache_fox_v", "cache_fox_logf", "state_rwkv", "state_rwkv_shift",
        "norm_g", "ffn_w_in", "ffn_w_out", "even_w_in", "fox_bf", "rw_mu", "rw_w0", "rw_w2", "rw_a0", "rw_a2",
        "rw_g2", "rw_kk", "rw_ka", "rw_rk", "rw_ln_g", "rw_ln_b", "even_w_out", "gm_w_in", "gm_ln_g", "gm_ln_b",
        "gm_w_s", "gm_b_s", "gm_w_out"]


def kernel(**inputs):
    import numpy as _np
    import concourse.bacc as _bacc
    from concourse import mybir as _mybir
    from concourse.bass_utils import run_bass_kernel_spmd as _run

    nc = _bacc.Bacc("TRN2", target_bir_lowering=False, num_devices=1, dynamic_dma_scratch_size=1024)
    given = {name: _np.ascontiguousarray(inputs[name]) for name in _INS}
    given["att_const"], given["new_mask"] = att_constants()
    given["rw_const"] = rw_constants()
    arrays, io = {}, {}
    for name, a in given.items():
        arrays[f"in_{name}_dram"] = a
        io[name] = nc.dram_tensor(f"in_{name}_dram", a.shape, _mybir.dt.from_np(a.dtype), kind="ExternalInput").ap()
    for i, (name, shape) in enumerate(OUTS.items()):
        io[name] = nc.dram_tensor(f"out_{i}_dram", shape, _mybir.dt.float32, kind="ExternalOutput").ap()
    build(nc, io)
    r = _run(nc, [arrays], core_ids=[0])
    return tuple(r.results[0][f"out_{i}_dram"] for i in range(len(OUTS)))
```

```python
import math
from contextlib import ExitStack

import concourse.bass as bass
from concourse import mybir

F32 = mybir.dt.float32
F32R = mybir.dt.float32r
ALU = mybir.AluOpType
ACT = mybir.ActivationFunctionType
AX = mybir.AxisListType.X

P = 128
D = 1024
KD = D // P
SEQ = 512
NSEQ, NEW = 8, 16
TT = SEQ // P + NSEQ * NEW // P
TOK = TT * P
HALF = TOK // 2
D_FF = 2816
FF_CHUNKS = 2
FF_K = D_FF // P // FF_CHUNKS
OUT_N = D // 512
FOXH, HEAD = 8, 64
FOXW = FOXH * HEAD
FOXC = 3 * FOXW + FOXH
RMS_EPS = 1e-6
LN_EPS = 1e-5
GN_EPS = 64e-5

EVEN_BANKS = (4, 5, 6, 7, 0)
ODD_BANKS = (1, 2, 3, 4, 5)
NORM_BANKS = (6, 4)

FFN = (FF_CHUNKS * FF_K, FF_CHUNKS * OUT_N * FF_K, FF_CHUNKS * OUT_N)
STAGES = {"ffn0": FFN, "even_in": (11, KD, 1), "even_out": (0, OUT_N * KD, OUT_N), "ffn1": FFN, "ffn2": FFN,
          "gm_in": (KD // 2, OUT_N * KD, OUT_N), "gm_out": (0, OUT_N * KD, OUT_N), "ffn3": FFN, "end": (0, 0, 0)}

ATT = {"tri_ones": 512, "tri_streams": P, "causal": P, "sel8": FOXH, "minus_ones": P,
       "minus_heads": P}


def columns(table):
    at, out = 0, {}
    for name, n in table.items():
        out[name] = slice(at, at + n)
        at += n
    return out, at


ATT_AT, ATT_N = columns(ATT)


RW_DVE = {
    "prompt": """
        bonus p_end0 p_end1 gram0 gram1 gram2 gram3 gram4 gram5 gram6 gram7 q_first q_unit tn2 qn2
        tn3 qn3 tn4 qn4 tn5 qn5 qn6 xm+ sadd0 s0 sig_g+ sadd1 s1 yc kkr+ e+ scan+ eex+ floor+ a+ ka+
        kmod+ rk+ rkr+ kk+ abar+ kka+ rbar+ khat+ bhat+ yn y_gain y_shift y_bonus y_gate lo
    """.split(),
    "streams": """
        clear bonus p_end gram0 gram1 gram2 gram3 gram4 gram5 gram6 gram7 q_first q_unit tn2 qn2 tn3
        qn3 qn4 yt0 yt1 yc yn y_gain y_shift y_bonus y_gate lo sadd0 s0 sadd1 s1 sadd2 s2 sadd3 s3
        sadd4 s4 sadd5 s5 sadd6 s6 sadd7 s7
    """.split(),
}
RW_ACT = {
    "prompt": """
        b_tok k_tok v_tok t_first y1a_2 y1b_2 y1a_3 y1b_3 y1a_4 y1b_4 y1a_5 y1b_5 y1a_6 y1b_6 r0 u0
        tanh_w+ tanh_g+ r1 u1 yt0 yt1 sig_w+ sig_a+ y_sq kk_sq+ log+ y_log p+ p_inv+ p_ex+ inverse+
        y_inverse hi gate+
    """.split(),
    "streams": """
        prompt_state b_tok k_tok v_tok t_first y1a_2 y1b_2 y1a_3 y1b_3 y1a_4 y1b_4 turn0 turn1 turn2
        turn3 turn4 turn5 turn6 turn7 r1t y0 r u y_sq y_log y_inverse hi out0 out1 out2 out3 out4
        out5 out6 out7
    """.split(),
}
RW_PE = {
    "prompt": """
        bonus turn gram0 gram1 gram2 gram3 gram4 gram5 gram6 gram7 q_turn y1a_2 y1b_2 tn2 qn2 y1a_3
        y1b_3 tn3 qn3 y1a_4 y1b_4 tn4 qn4 y1a_5 y1b_5 tn5 qn5 y1a_6 y1b_6 qn6 r0 u0 s0 r1 u1 y s1
        mean lora+ var norm+
    """.split(),
    "streams": """
        prompt_state bonus turn gram0 gram1 gram2 gram3 gram4 gram5 gram6 gram7 q_turn y1a_2 y1b_2
        tn2 qn2 y1a_3 y1b_3 tn3 qn3 y1a_4 y1b_4 qn4 turn0 turn1 turn2 turn3 turn4 turn5 turn6 turn7
        ra r u y mean var s0 s1 s2 s3 s4 s5 s6 s7 out0 out1 out2 out3 out4 out5 out6 out7
    """.split(),
}
RW_POOL = {
    "prompt": """
        lt2 lt3 lt4 lt5 lt6 diff+ mix+
    """.split(),
    "streams": """
        lt2 lt3 lt4 spread0_0 spread0_1 spread1_0 spread1_1 spread2_0 spread2_1 spread3_0 spread3_1
        spread4_0 spread4_1 spread5_0 spread5_1 spread6_0 spread6_1 spread7_0 spread7_1
    """.split(),
}

RWC = {"tril_p": 2 * P, "tril_s": 2 * P, "levels": 6 * P, "two_heads": P, "reset_p": 512, "reset_s": 512,
       "stream_rows": NSEQ}
RWC_AT, RWC_N = columns(RWC)


def before(stage, what):
    total = 0
    for name, counts in STAGES.items():
        if name == stage:
            return total
        total += counts[what]
    raise KeyError(stage)


def build(nc, io):
    ctx = ExitStack()
    with ctx:
        def sb(name, shape, dt=F32):
            return ctx.enter_context(nc.sbuf_tensor(name, shape, dt))

        def sem(name):
            return ctx.enter_context(nc.semaphore(name))

        x = sb("x", [P, TT, D])
        y = sb("y", [P, TT, D])
        act_hi = sb("act_hi", [P, KD, TOK], F32R)
        act_lo = sb("act_lo", [P, KD, TOK], F32R)
        pair_raw = [sb(f"pair_raw{i}", [P, KD, P]) for i in range(2)]
        pair_hi = [sb(f"pair_hi{i}", [P, KD, P], F32R) for i in range(2)]
        pair_lo = [sb(f"pair_lo{i}", [P, KD, P], F32R) for i in range(2)]
        row_raw = [sb(f"row_raw{i}", [P, 512]) for i in range(2)]
        row_hi = [sb(f"row_hi{i}", [P, 512], F32R) for i in range(2)]
        row_lo = [sb(f"row_lo{i}", [P, 512], F32R) for i in range(2)]
        norm_buf = sb("norm_buf", [P, 4 * D])
        g_post, g_pre = norm_buf[:, 0:D], norm_buf[:, D:2 * D]
        squares = [norm_buf[:, 2 * D:3 * D], norm_buf[:, 3 * D:4 * D]]
        xn_buf = sb("xn_buf", [P, 2 * D])
        xn = [xn_buf[:, 0:D], xn_buf[:, D:2 * D]]
        stat = sb("stat", [P, 8, TT])
        ident = sb("ident", [P, P])
        ones = sb("ones", [P, P])
        warm = sb("warm", [P, 1])
        eps = sb("eps", [P, 4])
        with ExitStack() as ffn:
            hid_hi = ffn.enter_context(nc.sbuf_tensor("hid_hi", [P, FF_K, TOK], F32R))
            hid_lo = ffn.enter_context(nc.sbuf_tensor("hid_lo", [P, FF_K, TOK], F32R))
            silu = ffn.enter_context(nc.sbuf_tensor("silu", [P, 2, HALF], F32))
            hid = ffn.enter_context(nc.sbuf_tensor("hid", [P, 2, HALF], F32))
        with ExitStack() as even:
            def eb(name, shape, dt=F32):
                return even.enter_context(nc.sbuf_tensor(name, shape, dt))

            rw = eb("rw", [P, 14, 1 + TOK])
            last_cols = eb("last_cols", [P, 14, 9])
            logf = eb("logf", [P, TT, FOXH])
            with ExitStack() as fox:
                def fb(name, shape, dt=F32):
                    return fox.enter_context(nc.sbuf_tensor(name, shape, dt))

                qk = fb("qk", [P, 8, TOK])
                vtok = fb("vtok", [P, TT, FOXW])
                att_const = fb("att_const", [P, ATT_N])
                rmax, nmax = fb("rmax", [P, 8]), fb("nmax", [P, 8])
                esum, rsum = fb("esum", [P, 8]), fb("rsum", [P, 8])
                f_raw = fb("f_raw", [P, KD, FOXH])
                f_hi = fb("f_hi", [P, KD, FOXH], F32R)
                f_lo = fb("f_lo", [P, KD, FOXH], F32R)
                f_tmp = fb("f_tmp", [P, TT, FOXH])
                bf_all = fb("bf_all", [P, FOXH])
                pair_cols = fb("pair_cols", [P, 8, P])
                v_pair = pair_cols[:, 0:4, :]
                k_pair = pair_cols[:, 4:8, :].rearrange("p (o k) c -> p o (k c)", o=1)
                qk_new = pair_cols
                f_cache = [fb(f"f_cache{i}", [P, 4, FOXH]) for i in range(2)]
                q_rows = fb("q_rows", [P, 656])
            with ExitStack() as wkv:
                def wb(name, shape, dt=F32):
                    return wkv.enter_context(nc.sbuf_tensor(name, shape, dt))

                rw_const = wb("rw_const", [P, RWC_N])
                par = wb("par", [P, 34])
                shift = wb("shift", [P, NSEQ * 14])
                lora_wa, lora_g = wb("lora_wa", [P, 512]), wb("lora_g", [P, 512])
                bias_rows = wb("bias_rows", [33, 512])
                rows_raw = wb("rows_raw", [P, 2 * P])
                xm = wb("xm", [P, 14, P])
                tanh_w, sig_g = wb("tanh_w", [P, P]), wb("sig_g", [P, P])
                gate, bonus_buf = wb("gate", [P, 512]), wb("bonus", [P, 512])
                state = [wb(f"state{i}", [P, 512]) for i in range(2)]
                decay_mask = [wb(f"decay_mask{i}", [P, 512]) for i in range(2)]
                yc, ysq = wb("yc", [P, 512]), wb("ysq", [P, 512])
                prompt_state = wb("prompt_state", [P, 512])
                p_end = wb("p_end", [P, 4 * NSEQ])
        with ExitStack() as odd:
            def ob(name, shape):
                return odd.enter_context(nc.sbuf_tensor(name, shape, F32))

            u_cols = ob("u_cols", [P, KD, TOK])
            ws, ws_t = ob("ws", [P, KD, P]), ob("ws_t", [P, KD, P])
            ws_new, ws_new_t = ob("ws_new", [P, KD, P]), ob("ws_new_t", [P, KD, P])
            ln_g, ln_b = ob("ln_g", [P, D]), ob("ln_b", [P, D])
            bs, bs_new = ob("bs", [1, KD, P]), ob("bs_new", [1, KD, P])
            ln_stat = ob("ln_stat", [P, 6, TT])
        gated = [xn[i].rearrange("p (g t) -> p g t", t=P) for i in range(2)]
        f_rows = q_rows[0:FOXH, 0:TOK]
        att = {n: att_const[:, ATT_AT[n]] for n in ATT}
        tri_ones, tri_streams, causal, sel8 = (att[n] for n in ("tri_ones", "tri_streams", "causal", "sel8"))
        sel8 = sel8[0:FOXH]
        minus_ones, minus_heads = att["minus_ones"], att["minus_heads"][0:FOXH]
        yflat = y[:, :, :].rearrange("p t d -> p (t d)")
        ktok = yflat[:, 0:TT * FOXW].rearrange("p (t c) -> p t c", c=FOXW)
        last_rows = yflat[0:9, 2560:2560 + 14 * P]
        q_pair = yflat[:, 4352:4864]
        c_heads = norm_buf[0:FOXH, :].rearrange("p (h c) -> p h c", c=SEQ)
        prob = [xn_buf[:, 1024 * i:1024 * i + 512] for i in range(2)]
        prob_t = [xn_buf[:, 1024 * i + 512:1024 * i + 1024] for i in range(2)]
        v_cache = [yflat[:, 2048 * i:2048 * i + 2048].rearrange("p (a c) -> p a c", c=FOXW) for i in range(2)]
        k_cache = [norm_buf[:, 2048 * i:2048 * i + 2048].rearrange("p (a c) -> p a c", c=FOXW) for i in range(2)]
        new_mask = yflat[:, 4096:5120].rearrange("p (b c) -> p b c", c=P)
        kt_cache = [pair_raw[i][:, :, :].rearrange("p (a k) c -> p a (k c)", a=2) for i in range(2)]
        prob2, prob_t2 = xn_buf[:, 0:TOK], xn_buf[:, TOK:2 * TOK]
        c_stream = xn_buf[0:FOXH, 2 * TOK:3 * TOK]

        rwc = {n: rw_const[:, RWC_AT[n]] for n in RWC}
        tril_p, tril_s, two_heads, reset_p, reset_s, stream_rows = (rwc[n] for n in (
            "tril_p", "tril_s", "two_heads", "reset_p", "reset_s", "stream_rows"))

        def level_mask(lv):
            return rwc["levels"][:, (lv - 1) * P:lv * P]

        par_rows, shift_rows = rows_raw[0:34, 0:P], rows_raw[0:NSEQ * 14, P:2 * P]
        t0, t1, t2, t3, t4, t5, t6, t7, t8, t9 = (yflat[:, 512 * i:512 * i + 512] for i in range(10))
        gram = yflat[:, 0:4096].rearrange("p (h c) -> p h c", h=8)
        t_inv = yflat[:, 4096:5120]
        q_inv, y1, lt_m = (norm_buf[:, D * i:D * i + D] for i in range(3))
        ar = norm_buf[:, 3 * D:4 * D].rearrange("p (k a c) -> p k a c", k=4, a=2)
        bT, kT, b_tok, k_tok = (xn_buf[:, 512 * i:512 * i + 512] for i in range(4))
        raw0, raw1 = (pair_raw[i][:, :, :].rearrange("p k c -> p (k c)") for i in range(2))
        r1, u_tok, v_tok, y_t = raw0[:, 0:512], raw0[:, 512:1024], raw1[:, 0:512], raw1[:, 512:1024]
        r1t, y0_t = decay_mask[0][:, :], decay_mask[1][:, :]
        bonus = bonus_buf[:, :]
        rwflat = rw[:, :, :].rearrange("p i c -> p (i c)")
        streams_state = rwflat[:, 0:4096].rearrange("p (s k c) -> p s k c", s=NSEQ, k=4)
        state_raw = rwflat[:, 4096:8192].rearrange("p (n c) -> p n c", c=P)
        spread = [[yflat[:, 512 * (2 * j + i):512 * (2 * j + i) + 512].rearrange("p (s v) -> p s v", s=NSEQ)
                   for i in range(2)] for j in range(2)]

        ps = ctx.enter_context(nc.psum_tensor("ps", [P, 8, 512], F32))

        s_x = [sem(f"x{t}_loaded") for t in range(TT)]
        s_const = sem("constants_set")
        s_pair_raw = [sem("gate_raw"), sem("up_raw")]
        s_pair_hi = [sem("gate_hi"), sem("up_hi")]
        s_pair_lo = [sem("gate_lo"), sem("up_lo")]
        s_pair_mm = [sem("gate_products"), sem("up_products")]
        s_pair_read = [sem("gate_read"), sem("up_read")]
        s_hid_hi = sem("hid_hi_written")
        s_hid_lo = sem("hid_lo_written")
        s_row_raw = [sem("row_raw0"), sem("row_raw1")]
        s_row_hi = sem("row_hi_written")
        s_row_lo = sem("row_lo_written")
        s_row_mm = sem("row_products")
        s_out = sem("outputs_summed")
        s_evict = sem("outputs_read")
        s_y0 = sem("y_cleared")
        s_gpost = sem("g_post_loaded")
        s_gpre = sem("g_pre_loaded")
        s_sq = [sem("post_squares"), sem("pre_squares")]
        s_rt = [sem("post_root"), sem("pre_root")]
        s_rc = [sem("post_reciprocal"), sem("pre_reciprocal")]
        s_yg, s_bias = sem("y_times_gain"), sem("root_bias")
        s_xnew = sem("x_updated")
        s_xn = sem("xn_written")
        s_tr = sem("xn_transposed")
        s_ahi = sem("act_hi_written")
        s_alo = sem("act_lo_written")
        s_store = sem("y_stored")
        s_f_raw, s_f_hi, s_f_split, s_f_mm = (sem(n) for n in ("f_raw_loaded", "f_hi_written", "f_split", "f_products"))
        s_att_const, s_z, s_fa, s_logf = (sem(n) for n in ("att_const_loaded", "f_logits", "f_functions", "logf_done"))
        s_rw0, s_last, s_kt, s_kt_read = (sem(n) for n in ("rw_zeroed", "last_cols_copied", "k_turned", "k_read"))
        s_c, s_ch, s_qrow0 = sem("c_summed"), sem("c_by_head"), sem("q_rows_cleared")
        s_qp, s_vp, s_mx, s_rs = (sem(n) for n in ("q_pair_set", "v_pair_set", "row_max", "row_sum_inverse"))
        s_sc, s_nm, s_ex, s_pm = (sem(n) for n in ("scores", "minus_max", "exponentials", "probabilities"))
        s_pt, s_ptr, s_o, s_oh, s_ol = (sem(n) for n in ("prob_turned", "prob_t_read", "fox_out", "fox_hi", "fox_lo"))
        s_rwc, s_par, s_st = sem("rw_loaded"), sem("rw_parameters"), sem("states_loaded")
        s_rwd, s_rwa, s_rwe, s_rwp = (sem(f"rw_{n}_steps") for n in ("dve", "act", "pe", "pool"))
        s_gm, s_ws0, s_wt, s_wt_read = (sem(n) for n in (
            "spatial_loaded", "ws_new_cleared", "spatial_turned", "spatial_read"))
        s_mean, s_vsq, s_vroot, s_vinv, s_vgain, s_v, s_new_v = (sem(n) for n in (
            "v_mean", "v_squares", "v_root", "v_inverse", "v_times_gain", "v_normalised", "new_v_stored"))
        s_spatial, s_gated, s_ghi, s_glo = (sem(n) for n in ("spatial_products", "gated", "gated_hi", "gated_lo"))
        s_qkn, s_f_read = sem("qk_new_copied"), sem("f_rows_copied")
        s_kc = [sem(f"k_cache{i}_loaded") for i in range(2)]
        s_vc = [sem(f"v_cache{i}_loaded") for i in range(2)]
        s_fc = [sem(f"f_cache{i}_loaded") for i in range(2)]
        s_mx2, s_rs2 = sem("row_max2"), sem("row_sum_inverse2")
        s_tk, s_c2, s_kta, s_ktd, s_cs, s_q2 = (sem(n) for n in (
            "cache_turned", "c2_summed", "kt01_read", "kt23_read", "c2_read", "q_rows_set"))
        s_sc2, s_nm2, s_ex2, s_pm2, s_pt2, s_ptr2, s_o2, s_oh2, s_ol2 = (sem(n + "2") for n in (
            "scores", "minus_max", "exponentials", "probabilities", "prob_turned", "prob_t_read", "fox_out", "fox_hi",
            "fox_lo"))
        block = ctx.enter_context(nc.Block())

        def wide(b):
            return ps[:, b:b + 2, 0:HALF]

        def halves(buf, k):
            if isinstance(k, int):
                return buf[:, k, :].rearrange("p (a b) -> p a b", a=2)
            return buf[:, bass.ds(k, 1), :].rearrange("p o (a b) -> p (o a) b", a=2)


        def sp_pair(sp, n, src_of):
            for c in range(2):
                sp.wait_ge(s_pair_lo[c], n + 1)
                sp.dma_start(pair_raw[c][:, :, :], src_of(c)).then_inc(s_pair_raw[c], 16)

        def sp_row(sp, i, base, half_base, src):
            sp.wait_ge(s_row_lo, base + i + 1)
            sp.dma_start(row_raw[i % 2][:, :], src).then_inc(s_row_raw[i % 2], 16)

        def act_split_pair(act, c, n):
            act.wait_ge(s_pair_raw[c], (n + 1) * 16)
            act.wait_ge(s_pair_mm[c], n + 1)
            act.activation(pair_hi[c][:, :, :], pair_raw[c][:, :, :], ACT.Copy).then_inc(s_pair_hi[c], 1)

        def dve_split_pair(dve, c, n):
            dve.wait_ge(s_pair_hi[c], n + 1)
            dve.tensor_tensor(pair_lo[c][:, :, :], pair_raw[c][:, :, :], pair_hi[c][:, :, :].bitcast(F32),
                              ALU.subtract).then_inc(s_pair_lo[c], 1)

        def act_split_row(act, i, base, half_base):
            act.wait_ge(s_row_raw[i % 2], (half_base + i // 2 + 1) * 16)
            act.wait_ge(s_row_mm, base + i + 1)
            act.activation(row_hi[i % 2][:, :], row_raw[i % 2][:, :], ACT.Copy).then_inc(s_row_hi, 1)

        def dve_split_row(dve, i, base):
            dve.wait_ge(s_row_hi, base + i + 1)
            dve.tensor_tensor(row_lo[i % 2][:, :], row_raw[i % 2][:, :], row_hi[i % 2][:, :].bitcast(F32),
                              ALU.subtract).then_inc(s_row_lo, 1)

        def pe_pair(pe, n):
            for c in range(2):
                pe.wait_ge(s_pair_lo[c], n + 2)
                pe.wait_ge(s_pair_read[c], n + 1)
                for k in range(KD):
                    for w, a in ((pair_hi, act_hi), (pair_hi, act_lo), (pair_lo, act_hi)):
                        for h in range(2):
                            mm = pe.matmul(ps[:, 2 * c + h, 0:HALF], w[c][:, k, :],
                                           a[:, k, h * HALF:(h + 1) * HALF],
                                           start=(k == 0 and w is pair_hi and a is act_hi),
                                           stop=(k == KD - 1 and w is pair_lo))
                mm.then_inc(s_pair_mm[c], 1)

        def pe_first_pair(pe, n, normed):
            for c in range(2):
                pe.wait_ge(s_pair_lo[c], n + 2)
                pe.wait_ge(s_pair_read[c], n + 1)
            for h in range(2):
                pe.wait_ge(s_alo, normed - 2 * (1 - h))
                for c in range(2):
                    for k in range(KD):
                        for w, a in ((pair_hi, act_hi), (pair_hi, act_lo), (pair_lo, act_hi)):
                            mm = pe.matmul(ps[:, 2 * c + h, 0:HALF], w[c][:, k, :],
                                           a[:, k, h * HALF:(h + 1) * HALF],
                                           start=(k == 0 and w is pair_hi and a is act_hi),
                                           stop=(k == KD - 1 and w is pair_lo))
                    if h:
                        mm.then_inc(s_pair_mm[c], 1)

        def split_ahead(eng, split, n):
            for c in range(2):
                split(eng, c, n)

        def pe_rows(pe, kt, groups, base, group_base, left_hi, left_lo, left_ready):
            for g in range(groups):
                banks = ODD_BANKS if g % 2 else EVEN_BANKS
                for k in range(kt):
                    i = g * kt + k
                    pe.wait_ge(s_row_lo, base + i + 3)
                    if g == 0:
                        left_ready(k)
                    for t in range(TT):
                        if k == 0 and g % 2 == 0 and t == 0:
                            pe.wait_ge(s_evict, (group_base + g) * TT + 1)
                        if k == 0 and g % 2 == 1 and t == 3:
                            pe.wait_ge(s_evict, (group_base + g - 1) * TT + 3)
                        for w, a in ((row_hi, left_hi), (row_hi, left_lo), (row_lo, left_hi)):
                            mm = pe.matmul(ps[:, banks[t], :], a[:, k, t * P:(t + 1) * P],
                                           w[i % 2][:, :],
                                           start=(k == 0 and w is row_hi and a is left_hi),
                                           stop=(k == kt - 1 and w is row_lo))
                        if t == TT - 1:
                            mm.then_inc(s_row_mm, 1)
                        elif k == kt - 1:
                            mm.then_inc(s_out, 1)

        def wait_output(eng, g, t, kt, base, group_base):
            if t < TT - 1:
                eng.wait_ge(s_out, (group_base + g) * (TT - 1) + t + 1)
            else:
                eng.wait_ge(s_row_mm, base + (g + 1) * kt + 2)

        def splits_and_outputs(kt, groups, split, evict):
            done = 0
            for g in range(groups):
                until = min((g + 1) * kt + 2, groups * kt)
                for i in range(done, until):
                    split(i)
                done = until
                for t in range(TT):
                    evict(g, t)

        def ffn_counts(stage, c):
            return (before(stage, 0) + c * FF_K, before(stage, 1) + c * (OUT_N * FF_K),
                    before(stage, 1) // 2 + c * (OUT_N * FF_K // 2), before(stage, 2) + c * OUT_N)

        LOAD_AHEAD, SPLIT_AHEAD = 8, 4

        def first_pair_of(stage, c=0):
            n = before(stage, 0) + c * FF_K
            if stage == "even_in":
                src = lambda half: ew_in[:, :, half * P:(half + 1) * P]
            elif stage == "gm_in":
                src = lambda half: gm_in.rearrange("(k p) n -> p k n", p=P)[:, :, half * P:(half + 1) * P]
            else:
                f = int(stage[-1])
                w_in = io["ffn_w_in"][f // 2, f % 2].rearrange("(k p) n -> p k n", p=P)
                src = lambda half: w_in[:, :, c * FF_K * P + half * D_FF:c * FF_K * P + half * D_FF + P]
            return lambda sp: sp_pair(sp, n, src)

        def sp_ffn(sp, f, load_next):
            w_in = io["ffn_w_in"][f // 2, f % 2].rearrange("(k p) n -> p k n", p=P)
            w_out = io["ffn_w_out"][f // 2, f % 2]
            for c in range(FF_CHUNKS):
                n0, r0, h0, _ = ffn_counts(f"ffn{f}", c)
                with sp.Fori(1, FF_K) as j:
                    sp_pair(sp, n0 + j, lambda half: w_in[:, :, bass.ds((c * FF_K + j) * P + half * D_FF, P)])
                for i in range(OUT_N * FF_K):
                    n, k = i // FF_K, i % FF_K
                    if i == OUT_N * FF_K - LOAD_AHEAD:
                        (first_pair_of(f"ffn{f}", c + 1) if c + 1 < FF_CHUNKS else load_next)(sp)
                    sp_row(sp, i, r0, h0, w_out[(c * FF_K + k) * P:(c * FF_K + k + 1) * P, n * 512:(n + 1) * 512])

        def pe_ffn(pe, f, normed):
            with pe.Fori(0, FF_CHUNKS) as c:
                n0, r0, _, g0 = ffn_counts(f"ffn{f}", c)
                pe.wait_ge(s_evict, g0 * TT + 1)
                pe_first_pair(pe, n0, normed)
                with pe.Fori(1, FF_K) as j:
                    pe_pair(pe, n0 + j)
                for h in range(2):
                    pe.wait_ge(s_pair_read[h], n0 + FF_K + 1)

                def hidden_ready(k):
                    pe.wait_ge(s_hid_lo, hid_base(f, c) + k + 2)

                pe_rows(pe, FF_K, OUT_N, r0, g0, hid_hi, hid_lo, hidden_ready)

        def hid_base(f, c):
            return (f * FF_CHUNKS + c) * FF_K

        def act_ffn(act, f):
            with act.Fori(0, FF_CHUNKS) as c:
                n0, r0, h0, _ = ffn_counts(f"ffn{f}", c)
                hb = hid_base(f, c)

                def tile(j, last):
                    act.wait_ge(s_pair_mm[0], n0 + j + 2)
                    act.wait_ge(s_pair_read[1], n0 + j + 1)
                    act.activation(silu[:, :, :], wide(0), ACT.Silu).then_inc(s_pair_read[0], 1)
                    if not last:
                        act_split_pair(act, 0, n0 + j + 1)
                    act.wait_ge(s_pair_read[1], n0 + j + 2)
                    act.activation(halves(hid_hi, j), hid[:, :, :], ACT.Copy).then_inc(s_hid_hi, 1)
                    if not last:
                        act_split_pair(act, 1, n0 + j + 1)

                if f == 3:
                    split_ahead(act, act_split_pair, n0)
                with act.Fori(0, FF_K - 1) as j:
                    tile(j, False)
                act_split_row(act, 0, r0, h0)
                act_split_row(act, 1, r0, h0)
                tile(FF_K - 1, True)
                for i in range(2, OUT_N * FF_K):
                    act_split_row(act, i, r0, h0)
                    if i == OUT_N * FF_K - SPLIT_AHEAD and f < 3:
                        split_ahead(act, act_split_pair, n0 + FF_K)

        def dve_ffn(dve, f):
            with dve.Fori(0, FF_CHUNKS) as c:
                n0, r0, h0, g0 = ffn_counts(f"ffn{f}", c)
                hb = hid_base(f, c)

                def tile(j, last):
                    if not last:
                        dve_split_pair(dve, 0, n0 + j + 1)
                    dve.wait_ge(s_pair_mm[1], n0 + j + 2)
                    dve.wait_ge(s_pair_read[0], n0 + j + 2)
                    dve.wait_ge(s_hid_lo, hb + j + 1)
                    dve.tensor_tensor(hid[:, :, :], silu[:, :, :], wide(2), ALU.mult).then_inc(s_pair_read[1], 1)
                    dve.wait_ge(s_hid_hi, hb + j + 1)
                    dve.tensor_tensor(halves(hid_lo, j), hid[:, :, :], halves(hid_hi, j).bitcast(F32),
                                      ALU.subtract).then_inc(s_hid_lo, 1)
                    if not last:
                        dve_split_pair(dve, 1, n0 + j + 1)

                if f == 3:
                    split_ahead(dve, dve_split_pair, n0)
                with dve.Fori(0, FF_K - 1) as j:
                    tile(j, False)
                dve_split_row(dve, 0, r0)
                dve_split_row(dve, 1, r0)
                tile(FF_K - 1, True)

                def split(i):
                    if i > 1:
                        dve_split_row(dve, i, r0)
                    if i == OUT_N * FF_K - SPLIT_AHEAD and f < 3:
                        split_ahead(dve, dve_split_pair, n0 + FF_K)

                def evict(g, t):
                    wait_output(dve, g, t, FF_K, r0, g0)
                    bank = (ODD_BANKS if g % 2 else EVEN_BANKS)[t]
                    dve.wait_ge(s_evict, g0 * TT + 1)
                    dve.wait_ge(s_y0, f + 1)
                    dst = y[:, t, g * 512:(g + 1) * 512]
                    dve.tensor_tensor(dst, dst, ps[:, bank, :], ALU.add).then_inc(s_evict, 1)

                splits_and_outputs(FF_K, OUT_N, split, evict)

        NORMS = 6

        def act_norm(act, m, scale, groups):
            if m == 0:
                act.wait_ge(s_const, 4)
            act.activation(warm[:, :], eps[:, 0:1], ACT.Sqrt)
            first = 10 * (m - 1)
            for t in range(TT if m else 0):
                act.wait_ge(s_evict, (groups - 2) * TT + t + 2)
                if first + t:
                    act.wait_ge(s_sq[0], first + t)
                act.activation(squares[0][:, 0:512], y[:, t, 0:512], ACT.Square,
                               accum_out=stat[:, 0, t:t + 1]).then_inc(s_sq[0], 1)
            for s in range(TT + 2):
                if m and s < TT:
                    n = first + TT + s
                    act.wait_ge(s_evict, groups * TT - TT + s + 2)
                    act.wait_ge(s_sq[0], n)
                    act.activation(squares[0][:, 512:D], y[:, s, 512:D], ACT.Square,
                                   accum_out=stat[:, 6, s:s + 1]).then_inc(s_sq[0], 1)
                    act.wait_ge(s_sq[0], n + 1)
                    act.wait_ge(s_bias, m)
                    act.activation(stat[:, 1, s:s + 1], stat[:, 6, s:s + 1], ACT.Sqrt, bias=stat[:, 7, s:s + 1],
                                   scale=1 / D / scale ** 2).then_inc(s_rt[0], 1)
                if 0 <= s - 1 < TT and m < NORMS:
                    t = s - 1
                    if m:
                        act.wait_ge(s_xnew, 5 * (m - 1) + t + 1)
                    else:
                        act.wait_ge(s_x[t], 16)
                    n = 5 * m + t
                    if n:
                        act.wait_ge(s_sq[1], n)
                    act.activation(squares[1][:, :], x[:, t, :], ACT.Square,
                                   accum_out=stat[:, 3, t:t + 1]).then_inc(s_sq[1], 1)
                    act.wait_ge(s_sq[1], n + 1)
                    act.activation(stat[:, 4, t:t + 1], stat[:, 3, t:t + 1], ACT.Sqrt, bias=eps[:, 0:1],
                                   scale=1 / D).then_inc(s_rt[1], 1)
                if 0 <= s - 2 < TT and m < NORMS:
                    t = s - 2
                    act.wait_ge(s_tr, 5 * m + t + 1)
                    b = NORM_BANKS[t % 2]
                    act.activation(act_hi[:, :, t * P:(t + 1) * P],
                                   ps[:, b:b + 2, :].rearrange("p a (k c) -> p (a k) c", c=P),
                                   ACT.Copy).then_inc(s_ahi, 1)

        def dve_norm(dve, m, scale=1):
            if m:
                dve.wait_ge(s_sq[0], 10 * (m - 1) + TT)
                dve.tensor_scalar(stat[:, 7, :], stat[:, 0, :], 1 / D / scale ** 2, RMS_EPS / scale ** 2,
                                  ALU.mult, ALU.add).then_inc(s_bias, 1)
            for s in range(TT + 2):
                if m and s < TT:
                    n = 5 * (m - 1) + s
                    dve.wait_ge(s_rt[0], n + 1)
                    dve.reciprocal(stat[:, 2, s:s + 1], stat[:, 1, s:s + 1]).then_inc(s_rc[0], 1)
                    dve.wait_ge(s_rc[0], n + 1)
                    dve.wait_ge(s_yg, 10 * (m - 1) + 2 * (s + 1))
                    dve.scalar_tensor_tensor(out=x[:, s, :], in0=y[:, s, :], scalar=stat[:, 2, s:s + 1],
                                             in1=x[:, s, :], op0=ALU.mult, op1=ALU.add).then_inc(s_xnew, 1)
                if 0 <= s - 1 < TT and m < NORMS:
                    t, n = s - 1, 5 * m + s - 1
                    dve.wait_ge(s_rt[1], n + 1)
                    dve.reciprocal(stat[:, 5, t:t + 1], stat[:, 4, t:t + 1]).then_inc(s_rc[1], 1)
                    dve.wait_ge(s_rc[1], n + 1)
                    dve.wait_ge(s_gpre, 16 * (m + 1))
                    if n >= 2:
                        dve.wait_ge(s_tr, n - 1)
                    dve.scalar_tensor_tensor(out=xn[t % 2][:, :], in0=x[:, t, :], scalar=stat[:, 5, t:t + 1],
                                             in1=g_pre[:, :], op0=ALU.mult, op1=ALU.mult).then_inc(s_xn, 1)
                if 0 <= s - 2 < TT and m < NORMS:
                    t = s - 2
                    dve.wait_ge(s_ahi, 5 * m + t + 1)
                    b = NORM_BANKS[t % 2]
                    cols = slice(t * P, (t + 1) * P)
                    dve.tensor_tensor(act_lo[:, :, cols],
                                      ps[:, b:b + 2, :].rearrange("p a (k c) -> p (a k) c", c=P),
                                      act_hi[:, :, cols].bitcast(F32), ALU.subtract).then_inc(s_alo, 1)

        CLEARING = (0, 2, 3, 5)

        def pool_norm(pool, m):
            for t in range(TT if m else 0):
                for half in range(2):
                    n = 10 * (m - 1) + TT * half + t
                    pool.wait_ge(s_sq[0], n + 1)
                    pool.wait_ge(s_gpost, 16 * m)
                    part = slice(512 * half, 512 * half + 512)
                    pool.tensor_tensor(y[:, t, part], y[:, t, part], g_post[:, part], ALU.mult).then_inc(s_yg, 1)
            if m in CLEARING:
                if m:
                    pool.wait_ge(s_xnew, 5 * m)
                pool.memset(y[:, :, :], 0.0).then_inc(s_y0, 1)

        def pe_norm(pe, m, groups):
            if m == 0:
                pe.wait_ge(s_const, 4)
            else:
                pe.wait_ge(s_evict, groups * TT + 1)
            for t in range(TT):
                n = 5 * m + t
                pe.wait_ge(s_xn, n + 1)
                if n >= 2:
                    pe.wait_ge(s_alo, n - 1)
                b = NORM_BANKS[t % 2]
                for k in range(KD):
                    mm = pe.transpose(ps[:, b + k // 4, k % 4 * P:(k % 4 + 1) * P],
                                      xn[t % 2][:, k * P:(k + 1) * P], ident[:, :])
                mm.then_inc(s_tr, 1)

        def sp_norm_gains(sp, m):
            layer, i = divmod(m, 3)
            if m:
                pl, pi = divmod(m - 1, 3)
                if m > 1:
                    sp.wait_ge(s_yg, 10 * (m - 1))
                sp.dma_start(g_post[:, :], io["norm_g"][pl, 2 * pi + 1:2 * pi + 2, :].broadcast_to([P, D]))\
                  .then_inc(s_gpost, 16)
            if m < NORMS:
                if m:
                    sp.wait_ge(s_xn, 5 * m)
                sp.dma_start(g_pre[:, :], io["norm_g"][layer, 2 * i:2 * i + 1, :].broadcast_to([P, D]))\
                  .then_inc(s_gpre, 16)

        NQK, NRW = 4, 7
        ew_in = io["even_w_in"][0].rearrange("(k p) n -> p k n", p=P)

        def sp_even_in(sp):
            n0, r0, h0 = before("even_in", 0), before("even_in", 1), before("even_in", 1) // 2
            sp.wait_ge(s_xn, 10)
            sp.dma_start(f_raw[:, :, :], ew_in[:, :, 3 * FOXW:3 * FOXW + FOXH]).then_inc(s_f_raw, 16)
            sp.dma_start(bf_all[:, :], io["fox_bf"].broadcast_to([P, FOXH])).then_inc(s_f_raw, 16)
            sp.dma_start(att_const[:, :], io["att_const"]).then_inc(s_att_const, 16)
            with sp.Fori(1, NQK) as j:
                sp_pair(sp, n0 + j, lambda c: ew_in[:, :, bass.ds(j * 256 + c * P, P)])
            with sp.Fori(0, NRW) as j:
                sp_pair(sp, n0 + NQK + j, lambda c: ew_in[:, :, bass.ds(j * 256 + c * P + FOXC, P)])
            for k in range(KD):
                sp_row(sp, k, r0, h0, io["even_w_in"][0, k * P:(k + 1) * P, 2 * FOXW:3 * FOXW])

        def pe_even_in(pe):
            n0, r0, g0 = (before("even_in", i) for i in range(3))
            pe_first_pair(pe, n0, 2 * TT)
            with pe.Fori(1, NQK + NRW) as j:
                pe_pair(pe, n0 + j)
            pe.wait_ge(s_f_split, 1)
            for h in range(2):
                cols = slice(h * HALF, (h + 1) * HALF)
                for k in range(KD):
                    for w, a in ((f_hi, act_hi), (f_hi, act_lo), (f_lo, act_hi)):
                        mm = pe.matmul(ps[0:FOXH, 6 + h, 0:HALF], w[:, k, :], a[:, k, cols],
                                       start=(k == 0 and w is f_hi and a is act_hi),
                                       stop=(k == KD - 1 and w is f_lo))
            mm.then_inc(s_f_mm, 1)
            for h in range(2):
                pe.wait_ge(s_pair_read[h], n0 + NQK + NRW + 1)
            pe.wait_ge(s_f_read, 1)
            for t in range(TT):
                mm = pe.transpose(ps[:, 1, t * FOXH:(t + 1) * FOXH], f_rows[:, t * P:(t + 1) * P],
                                  ident[0:FOXH, 0:FOXH])
            mm.then_inc(s_f_mm, 1)
            pe_rows(pe, KD, 1, r0, g0, act_hi, act_lo, lambda k: None)

        def rw_cols(i):
            return rw[:, bass.ds(i, 1), 1:1 + TOK].rearrange("p o (a b) -> p (o a) b", a=2)

        def act_even_in(act):
            n0, r0, h0 = before("even_in", 0), before("even_in", 1), before("even_in", 1) // 2
            act.wait_ge(s_f_raw, 32)
            act.activation(f_hi[:, :, :], f_raw[:, :, :], ACT.Copy).then_inc(s_f_hi, 1)

            def tile(n, dst, last):
                act.wait_ge(s_pair_mm[0], n + 2)
                act.activation(dst, wide(0), ACT.Copy).then_inc(s_pair_read[0], 1)
                if not last:
                    act_split_pair(act, 0, n + 1)
                    act_split_pair(act, 1, n + 1)

            with act.Fori(0, NQK) as j:
                tile(n0 + j, halves(qk, 2 * j), False)
            with act.Fori(0, NRW - 1) as j:
                tile(n0 + NQK + j, rw_cols(2 * j), False)
            act_split_row(act, 0, r0, h0)
            act_split_row(act, 1, r0, h0)
            tile(n0 + NQK + NRW - 1, rw_cols(2 * NRW - 2), True)
            for k in range(2, KD):
                act_split_row(act, k, r0, h0)
            act.wait_ge(s_z, 1)
            act.activation(f_tmp[:, :, :], logf[:, :, :], ACT.Abs).then_inc(s_fa, 1)
            act.wait_ge(s_fa, 1)
            act.activation(f_tmp[:, :, :], f_tmp[:, :, :], ACT.Exp, scale=-1.0).then_inc(s_fa, 1)
            act.wait_ge(s_fa, 2)
            act.activation(f_tmp[:, :, :], f_tmp[:, :, :], ACT.Ln, bias=1.0).then_inc(s_fa, 1)

        def dve_even_in(dve):
            n0, r0, g0 = (before("even_in", i) for i in range(3))
            dve.wait_ge(s_f_hi, 1)
            dve.tensor_tensor(f_lo[:, :, :], f_raw[:, :, :], f_hi[:, :, :].bitcast(F32), ALU.subtract)\
               .then_inc(s_f_split, 1)
            dve.memset(rw[:, :, 0:1], 0.0).then_inc(s_rw0, 1)

            def tile(n, dst, last):
                if not last:
                    dve_split_pair(dve, 0, n + 1)
                dve.wait_ge(s_pair_mm[1], n + 2)
                dve.tensor_copy(dst, wide(2)).then_inc(s_pair_read[1], 1)
                if not last:
                    dve_split_pair(dve, 1, n + 1)

            with dve.Fori(0, NQK) as j:
                tile(n0 + j, halves(qk, 2 * j + 1), False)
            with dve.Fori(0, NRW - 1) as j:
                tile(n0 + NQK + j, rw_cols(2 * j + 1), False)
            dve_split_row(dve, 0, r0)
            dve_split_row(dve, 1, r0)
            tile(n0 + NQK + NRW - 1, rw_cols(2 * NRW - 1), True)
            dve.wait_ge(s_f_mm, 1)
            dve.tensor_copy(f_rows.rearrange("p (a b) -> p a b", a=2), ps[0:FOXH, 6:8, 0:HALF]).then_inc(s_f_read, 1)
            dve.wait_ge(s_f_mm, 2)
            dve.tensor_tensor(logf[:, :, :], ps[:, 1, 0:TT * FOXH].rearrange("p (t h) -> p t h", h=FOXH),
                              bf_all[:, :].rearrange("p (o h) -> p o h", o=1).broadcast_to([P, TT, FOXH]),
                              ALU.add).then_inc(s_z, 1)
            for k in range(2, KD):
                dve_split_row(dve, k, r0)
            for t in range(TT):
                wait_output(dve, 0, t, KD, r0, g0)
                dve.tensor_copy(vtok[:, t, :], ps[:, EVEN_BANKS[t], :]).then_inc(s_evict, 1)
            dve.wait_ge(s_fa, 3)
            dve.wait_ge(s_z, 1)
            dve.scalar_tensor_tensor(out=logf[:, :, :], in0=logf[:, :, :], scalar=0.0, in1=f_tmp[:, :, :],
                                     op0=ALU.min, op1=ALU.subtract).then_inc(s_logf, 1)

        def pe_even_outputs(pe):
            e0 = before("even_in", 2)
            pe.wait_ge(s_evict, (e0 + 1) * TT + 1)
            pe.wait_ge(s_z, 1)
            for t in range(TT):
                for p in range(4):
                    mm = pe.transpose(ps[:, t, p * P:(p + 1) * P], qk[:, 4 + p, t * P:(t + 1) * P], ident[:, :])
                mm.then_inc(s_kt, 1)
            for i in range(2 * NRW):
                if i == 12:
                    pe.wait_ge(s_kt_read, 1)
                mm = pe.transpose(ps[0:9, (5, 6, 7, 0)[i // 4], i % 4 * P:(i % 4 + 1) * P],
                                  last_cols[:, i, :], ident[:, :])
            mm.then_inc(s_kt, 1)

        def dve_even_outputs(dve):
            dve.wait_ge(s_pair_read[0], before("even_in", 0) + NQK + NRW + 1)
            dve.wait_ge(s_pair_read[1], before("even_in", 0) + NQK + NRW + 1)
            dve.tensor_copy(last_cols[:, :, 0:1], rw[:, :, SEQ:SEQ + 1]).then_inc(s_last, 1)
            dve.tensor_copy(last_cols[:, :, 1:9],
                            rw[:, :, 1 + SEQ:1 + TOK].rearrange("p i (s t) -> p i s t", t=NEW)[:, :, :, NEW - 1])\
               .then_inc(s_last, 1)
            for t in range(TT):
                dve.wait_ge(s_kt, t + 1)
                dve.tensor_copy(ktok[:, t, :], ps[:, t, :]).then_inc(s_kt_read, 1)
            dve.wait_ge(s_kt, TT + 1)
            dve.tensor_copy(last_rows[:, 0:12 * P].rearrange("p (b c) -> p b c", b=3), ps[0:9, 5:8, :])\
               .then_inc(s_kt_read, 1)
            dve.tensor_copy(last_rows[:, 12 * P:14 * P], ps[0:9, 0, 0:2 * P]).then_inc(s_kt_read, 1)

        def sp_even_outputs(sp):
            sp.wait_ge(s_evict, (before("even_in", 2) + 1) * TT + 1)
            store(sp, io["fv_p"][0, 0].rearrange("(t p) h d -> p t (h d)", p=P), vtok[:, 0:4, :])
            store(sp, io["fv_s"][0].rearrange("s t h d -> (s t) (h d)"), vtok[:, 4, :])
            sp.wait_ge(s_kt_read, TT)
            store(sp, io["fk_p"][0, 0].rearrange("(t p) h d -> p t (h d)", p=P), ktok[:, 0:4, :])
            store(sp, io["fk_s"][0].rearrange("s t h d -> (s t) (h d)"), ktok[:, 4, :])
            sp.wait_ge(s_kt_read, TT + 2)
            store(sp, io["rsh_p"][0, 0], last_rows[0:1, :])
            store(sp, io["rsh_s"][0].rearrange("s o c -> (s o) c"), last_rows[1:9, :])
            sp.wait_ge(s_logf, 1)
            store(sp, io["fl_p"][0, 0].rearrange("(t p) h -> p t h", p=P), logf[:, 0:4, :])
            store(sp, io["fl_s"][0].rearrange("s t h -> (s t) h"), logf[:, 4, :])

        def pe_prompt_c(pe):
            pe.wait_ge(s_att_const, 16)
            pe.wait_ge(s_logf, 1)
            pe.wait_ge(s_kt_read, TT + 2)
            for t in range(4):
                mm = pe.matmul(ps[0:FOXH, 1, t * P:SEQ], logf[:, t, :], tri_ones[:, 0:SEQ - t * P],
                               start=(t == 0), stop=(t == 3))
            mm.then_inc(s_c, 1)

        def dve_prompt_c(dve):
            dve.wait_ge(s_c, 1)
            dve.tensor_tensor(c_heads[:, :, :],
                              ps[0:FOXH, 1:2, :].broadcast_to([FOXH, FOXH, SEQ]),
                              sel8.rearrange("p (h o) -> p h o", o=1).broadcast_to([FOXH, FOXH, SEQ]),
                              ALU.mult).then_inc(s_ch, 1)

        UNITS = 8

        def unit(u):
            h, qt = u // 4, u % 4
            return h, qt, (qt + 1) * P, slice(64 * h, 64 * h + 64)

        def after(n, lag=0):
            return n + (3 - lag)

        def act_prompt(act):
            act.wait_ge(s_kt_read, TT + 2)
            with act.Fori(0, 4) as p:
                act.wait_ge(s_sc, UNITS * p + 2)
                act.activation(q_pair[:, :].rearrange("p (o c) -> p o c", o=1), qk[:, bass.ds(p, 1), 0:SEQ],
                               ACT.Copy, scale=HEAD ** -0.5).then_inc(s_qp, 1)
                for s in range(UNITS + 2):
                    if s < UNITS:
                        u, n = s, UNITS * p + s
                        kl = unit(u)[2]
                        act.wait_ge(s_nm, after(n))
                        act.wait_ge(s_pt, after(n, 2))
                        act.activation(prob[u % 2][:, 0:kl], ps[:, u % 2, 0:kl], ACT.Exp, bias=nmax[:, u:u + 1],
                                       accum_out=esum[:, u:u + 1]).then_inc(s_ex, 1)
                    if 0 <= s - 1 < UNITS:
                        u, n = s - 1, UNITS * p + (s - 1)
                        kl = unit(u)[2]
                        act.wait_ge(s_pt, after(n))
                        act.wait_ge(s_o, after(n, 2))
                        act.activation(prob_t[u % 2][:, 0:kl], ps[:, 2 + u % 2, 0:kl], ACT.Copy).then_inc(s_ptr, 1)
                    if 0 <= s - 2 < UNITS:
                        u, n = s - 2, UNITS * p + (s - 2)
                        _, qt, _, rows = unit(u)
                        act.wait_ge(s_o, after(n))
                        act.activation(act_hi[rows, bass.ds(p, 1), qt * P:(qt + 1) * P],
                                       ps[rows, 4 + u % 2, 0:P].rearrange("p (o c) -> p o c", o=1),
                                       ACT.Copy).then_inc(s_oh, 1)

        def dve_prompt(dve):
            with dve.Fori(0, 4) as p:
                for s in range(UNITS + 2):
                    if s < UNITS:
                        u, n = s, UNITS * p + s
                        kl = unit(u)[2]
                        dve.wait_ge(s_sc, after(n))
                        dve.tensor_reduce(rmax[:, u:u + 1], ps[:, u % 2, 0:kl], AX, ALU.max).then_inc(s_mx, 1)
                        dve.wait_ge(s_mx, n + 1)
                        dve.tensor_scalar(nmax[:, u:u + 1], rmax[:, u:u + 1], -1.0, None, ALU.mult)\
                           .then_inc(s_nm, 1)
                        dve.wait_ge(s_ex, after(n))
                        dve.wait_ge(s_pm, after(n, 2))
                        dve.reciprocal(rsum[:, u:u + 1], esum[:, u:u + 1]).then_inc(s_rs, 1)
                    if 0 <= s - 2 < UNITS:
                        u, n = s - 2, UNITS * p + (s - 2)
                        _, qt, _, rows = unit(u)
                        dve.wait_ge(s_oh, after(n))
                        cols = slice(qt * P, (qt + 1) * P)
                        dve.tensor_tensor(act_lo[rows, bass.ds(p, 1), cols],
                                          ps[rows, 4 + u % 2, 0:P].rearrange("p (o c) -> p o c", o=1),
                                          act_hi[rows, bass.ds(p, 1), cols].bitcast(F32),
                                          ALU.subtract).then_inc(s_ol, 1)

        def pool_prompt(pool):
            pool.wait_ge(s_kt_read, TT + 2)
            with pool.Fori(0, 4) as p:
                pool.wait_ge(s_o, UNITS * p + 2)
                pool.tensor_copy(k_pair[:, :, :], qk[:, bass.ds(p + 4, 1), 0:SEQ])
                pool.tensor_copy(v_pair[:, :, :], vtok[:, 0:4, bass.ds(p * P, P)]).then_inc(s_vp, 1)
                for u in range(UNITS):
                    n = UNITS * p + u
                    kl = unit(u)[2]
                    pool.wait_ge(s_rs, n + 1)
                    pool.tensor_tensor(prob[u % 2][:, 0:kl], prob[u % 2][:, 0:kl],
                                       rsum[:, u:u + 1].broadcast_to([P, kl]), ALU.mult).then_inc(s_pm, 1)

        def pe_prompt(pe):
            def scores(p, u):
                h, qt, kl, rows = unit(u)
                pe.wait_ge(s_ex, after(UNITS * p + u, 2))
                out = ps[:, u % 2, 0:kl]
                pe.matmul(out, q_pair[rows, qt * P:(qt + 1) * P],
                          k_pair[rows, 0, 0:kl], start=True, stop=False)
                pe.matmul(out, minus_ones[0:FOXH, :],
                          c_heads[:, bass.ds(2 * p + h, 1), 0:kl].rearrange("p o c -> p (o c)"),
                          start=False, stop=False)
                pe.matmul(ps[:, u % 2, qt * P:kl], ident[:, :], causal, start=False, stop=True)\
                  .then_inc(s_sc, 1)

            def turn(p, u):
                n = UNITS * p + u
                pe.wait_ge(s_pm, after(n))
                pe.wait_ge(s_ptr, after(n, 2))
                for k in range(unit(u)[1] + 1):
                    mm = pe.transpose(ps[:, 2 + u % 2, k * P:(k + 1) * P],
                                      prob[u % 2][:, k * P:(k + 1) * P], ident[:, :])
                mm.then_inc(s_pt, 1)

            def outputs(p, u):
                n, qt = UNITS * p + u, unit(u)[1]
                pe.wait_ge(s_ptr, after(n))
                pe.wait_ge(s_ol, after(n, 2))
                for k in range(qt + 1):
                    mm = pe.matmul(ps[:, 4 + u % 2, 0:P], v_pair[:, k, :], prob_t[u % 2][:, k * P:(k + 1) * P],
                                   start=(k == 0), stop=(k == qt))
                mm.then_inc(s_o, 1)

            pe.wait_ge(s_ch, 1)
            with pe.Fori(0, 4) as p:
                pe.wait_ge(s_qp, p + 1)
                pe.wait_ge(s_vp, p + 1)
                scores(p, 0)
                for u in range(UNITS + 1):
                    if u + 1 < UNITS:
                        scores(p, u + 1)
                    if u > 0:
                        outputs(p, u - 1)
                    if u < UNITS:
                        turn(p, u)

        flat = ps[:, :, :].rearrange("p b c -> p (b c)")

        def sp_streams(sp):
            sp.wait_ge(s_store, sum(stores))
            sp.wait_ge(s_ol, UNITS * 4 + 2)
            sp.dma_start(new_mask, io["new_mask"].rearrange("p (b c) -> p b c", c=P)).then_inc(s_att_const, 16)
            with sp.Fori(0, NSEQ // 2) as i:
                for slot in range(2):
                    b = 2 * i + slot
                    one = lambda a: a[0, bass.ds(b, 1)]
                    sp.wait_ge(s_tk, after(b, 2))
                    sp.dma_start(k_cache[slot][:, :, :],
                                 one(io["cache_fox_k"]).rearrange("o (t p) h d -> p (o t) (h d)", p=P))\
                      .then_inc(s_kc[slot], 16)
                    sp.wait_ge(s_c2, after(b, 2))
                    sp.dma_start(f_cache[slot][:, :, :],
                                 one(io["cache_fox_logf"]).rearrange("o (t p) h -> p (o t) h", p=P))\
                      .then_inc(s_fc[slot], 16)
                    sp.wait_ge(s_o2, after(b, 2))
                    sp.dma_start(v_cache[slot][:, :, :],
                                 one(io["cache_fox_v"]).rearrange("o (t p) h d -> p (o t) (h d)", p=P))\
                      .then_inc(s_vc[slot], 16)

        def pe_streams(pe):
            def keys(i, slot):
                b = 2 * i + slot
                pe.wait_ge(s_kc[slot], 16 * i + 16)
                pe.wait_ge(s_kta, after(b, 1))
                pe.wait_ge(s_ktd, after(b, 1))
                for p in (1, 2, 3, 0):
                    if p == 0:
                        pe.wait_ge(s_ol2, after(b, 2))
                    for k in range(4):
                        mm = pe.transpose(ps[:, p, k * P:(k + 1) * P], k_cache[slot][:, k, p * P:(p + 1) * P],
                                          ident[:, :])
                mm.then_inc(s_tk, 1)
                pe.wait_ge(s_fc[slot], 16 * i + 16)
                pe.wait_ge(s_ptr2, after(b, 2))
                for k in range(4):
                    pe.matmul(ps[0:FOXH, 6, k * P:SEQ], f_cache[slot][:, k, :], tri_ones[:, 0:SEQ - k * P],
                              start=(k == 0), stop=(k == 3))
                for k in range(4):
                    pe.matmul(ps[0:FOXH, 7, 0:P], f_cache[slot][:, k, :], tri_ones[:, P:2 * P],
                              start=(k == 0), stop=False)
                pe.matmul(ps[0:FOXH, 7, 0:P], logf[:, 4, :], tri_streams, start=False, stop=True)\
                  .then_inc(s_c2, 1)

            def scores(b):
                pe.wait_ge(s_kta, after(b))
                pe.wait_ge(s_ktd, after(b))
                pe.wait_ge(s_q2, after(b))
                pe.wait_ge(s_ex2, after(b, 1))
                for p in range(4):
                    pe.matmul(ps[:, 4, :], q_rows[:, p * P:(p + 1) * P], kt_cache[p // 2][:, p % 2, :], start=(p == 0), stop=False)
                pe.matmul(ps[:, 4, :], minus_heads, c_stream[0:FOXH, 0:SEQ], start=False, stop=True)
                for p in range(4):
                    pe.matmul(ps[:, 5, 0:P], q_rows[:, p * P:(p + 1) * P], qk_new[:, 4 + p, :],
                              start=(p == 0), stop=False)
                pe.matmul(ps[:, 5, 0:P], minus_heads, c_stream[0:FOXH, SEQ:TOK], start=False, stop=False)
                pe.matmul(ps[:, 5, 0:P], ident[:, :], new_mask[:, bass.ds(b, 1), :].rearrange("p o c -> p (o c)"),
                          start=False, stop=True).then_inc(s_sc2, 1)

            def turn(b, last=False):
                pe.wait_ge(s_pm2, after(b))
                pe.wait_ge(s_cs, after(b, 0 if last else -1))
                for k in range(5):
                    mm = pe.transpose(flat[:, 6 * 512 + k * P:6 * 512 + (k + 1) * P], prob2[:, k * P:(k + 1) * P],
                                      ident[:, :])
                mm.then_inc(s_pt2, 1)

            def products(i, slot):
                b = 2 * i + slot
                pe.wait_ge(s_ptr2, after(b))
                pe.wait_ge(s_vc[slot], 16 * i + 16)
                pe.wait_ge(s_ol2, after(b, 1))
                for p in range(4):
                    for k in range(5):
                        v = v_cache[slot][:, k, p * P:(p + 1) * P] if k < 4 else vtok[:, 4, p * P:(p + 1) * P]
                        mm = pe.matmul(ps[:, 0, p * 32:p * 32 + 32], v, prob_t2[:, k * P + p * 32:k * P + p * 32 + 32],
                                       start=(k == 0), stop=(k == 4))
                mm.then_inc(s_o2, 1)

            pe.wait_ge(s_ol, UNITS * 4 + 2)
            pe.wait_ge(s_att_const, 32)
            keys(0, 0)
            scores(0)

            def step(i, slot):
                keys(i + slot, 1 - slot)
                turn(2 * i + slot)
                scores(2 * i + slot + 1)
                products(i, slot)

            with pe.Fori(0, NSEQ // 2 - 1) as i:
                step(i, 0)
                step(i, 1)
            step(NSEQ // 2 - 1, 0)
            turn(NSEQ - 1, True)
            products(NSEQ // 2 - 1, 1)

        def diagonal(buf, h, b):
            return buf[64 * h:64 * h + 64, 0:4, bass.ds(SEQ + NEW * b, NEW)]

        def products(h):
            return ps[64 * h:64 * h + 64, 0, 0:P].rearrange("p (a c) -> p a c", c=32)[:, :, NEW * h:NEW * h + NEW]

        def act_streams(act):
            def keys(b):
                act.wait_ge(s_sc2, after(b, 1))
                act.wait_ge(s_tk, after(b))
                act.activation(kt_cache[0], ps[:, 0:2, :], ACT.Copy).then_inc(s_kta, 1)
                act.wait_ge(s_c2, after(b))
                act.activation(c_stream[0:FOXH, :], flat[0:FOXH, 6 * 512:6 * 512 + TOK], ACT.Copy).then_inc(s_cs, 1)
                for h in range(2):
                    rows = slice(64 * h, 64 * h + 64)
                    ins = act.activation(
                        q_rows[rows, NEW * h:NEW * h + 640].rearrange("p (a c) -> p a c", c=160)[:, :, 0:NEW],
                        qk_new[rows, 0:4, bass.ds(NEW * b, NEW)], ACT.Copy, scale=HEAD ** -0.5)
                ins.then_inc(s_q2, 1)

            def soft(b):
                act.wait_ge(s_nm2, after(b))
                act.wait_ge(s_pt2, after(b, 1))
                act.activation(prob2[:, :], flat[:, 4 * 512:4 * 512 + TOK], ACT.Exp, bias=nmax[:, 0:1],
                               accum_out=esum[:, 0:1]).then_inc(s_ex2, 1)

            def turned(b):
                act.wait_ge(s_pt2, after(b))
                act.wait_ge(s_o2, after(b, 1))
                act.activation(prob_t2[:, :], flat[:, 6 * 512:6 * 512 + TOK], ACT.Copy).then_inc(s_ptr2, 1)

            def outputs(b):
                act.wait_ge(s_o2, after(b))
                act.activation(diagonal(act_hi, 0, b), products(0), ACT.Copy)
                act.activation(diagonal(act_hi, 1, b), products(1), ACT.Copy).then_inc(s_oh2, 1)

            act.wait_ge(s_qrow0, 1)
            act.wait_ge(s_ol, UNITS * 4 + 2)
            act.activation(qk_new[:, :, :], qk[:, :, SEQ:TOK], ACT.Copy).then_inc(s_qkn, 1)
            act.wait_ge(s_qkn, 1)
            keys(0)
            soft(0)
            with act.Fori(0, NSEQ - 1) as b:
                keys(b + 1)
                turned(b)
                soft(b + 1)
                outputs(b)
            turned(NSEQ - 1)
            outputs(NSEQ - 1)

        def dve_streams(dve):
            def keys(b):
                dve.wait_ge(s_sc2, after(b, 1))
                dve.wait_ge(s_tk, after(b))
                dve.tensor_copy(kt_cache[1], ps[:, 2:4, :]).then_inc(s_ktd, 1)

            def soft(b):
                dve.wait_ge(s_sc2, after(b))
                dve.tensor_reduce(rmax[:, 0:1], flat[:, 4 * 512:4 * 512 + TOK], AX, ALU.max).then_inc(s_mx2, 1)
                dve.wait_ge(s_mx2, b + 1)
                dve.tensor_scalar(nmax[:, 0:1], rmax[:, 0:1], -1.0, None, ALU.mult).then_inc(s_nm2, 1)

            def total(b):
                dve.wait_ge(s_ex2, after(b))
                dve.wait_ge(s_pm2, after(b, 1))
                dve.reciprocal(rsum[:, 0:1], esum[:, 0:1]).then_inc(s_rs2, 1)

            def outputs(b):
                dve.wait_ge(s_oh2, after(b))
                for h in range(2):
                    ins = dve.tensor_tensor(diagonal(act_lo, h, b), products(h), diagonal(act_hi, h, b).bitcast(F32),
                                            ALU.subtract)
                ins.then_inc(s_ol2, 1)

            dve.memset(q_rows[:, :], 0.0).then_inc(s_qrow0, 1)
            keys(0)
            soft(0)
            total(0)
            with dve.Fori(0, NSEQ - 1) as b:
                keys(b + 1)
                soft(b + 1)
                total(b + 1)
                outputs(b)
            outputs(NSEQ - 1)

        def pool_streams(pool):
            with pool.Fori(0, NSEQ) as b:
                pool.wait_ge(s_rs2, b + 1)
                pool.tensor_tensor(prob2[:, :], prob2[:, :], rsum[:, 0:1].broadcast_to([P, TOK]), ALU.mult)\
                    .then_inc(s_pm2, 1)

        F4 = lambda a: a.rearrange("p (k c) -> p k c", k=4)
        H8 = lambda a: a.rearrange("p (h c) -> p h c", h=8)

        def stretch(v, n, c):
            return v.rearrange("p (k o) -> p k o", o=1).broadcast_to([P, n, c])

        def same(v, n):
            return v.rearrange("p (o c) -> p o c", o=1).broadcast_to([P, n, v.shape[-1]])

        def tile_counts(tile, streams):
            def of(steps):
                n = len(steps["prompt"])

                def at(name):
                    if name + "+" in steps["prompt"]:
                        done = (4 if streams else tile) * n + (steps["prompt"].index(name + "+") + 2)
                    elif streams:
                        done = 5 * n + steps["streams"].index(name) + 2
                    else:
                        done = tile * n + (n + steps["prompt"].index(name) + 2)
                    return done
                return at
            return of(RW_DVE), of(RW_ACT), of(RW_PE), of(RW_POOL)

        def stepper(eng, signal, steps, kind):
            names = steps["streams" if kind == "streams" else "prompt"]
            at = [0]

            def to(place):
                if kind == "ahead" and place > at[0]:
                    eng.wait_ge(signal, at[0] + 1)
                    eng.sem_inc(signal, place - at[0])
                    at[0] = place

            def step(ins, name):
                assert names[at[0]] == name, (names[at[0]], name)
                ins.then_inc(signal, 1)
                at[0] += 1
            return step, lambda name: to(names.index(name)), lambda: to(len(names))

        DECAY = 0.5 * math.exp(-0.5)

        def sp_rwkv(sp):
            sp.wait_ge(s_qkn, 1)
            sp.dma_start(rw_const[:, :], io["rw_const"]).then_inc(s_rwc, 16)
            sp.dma_start(par_rows[0:14, :], io["rw_mu"][0].rearrange("(i c) -> i c", c=P)).then_inc(s_rwc, 16)
            for n, name in enumerate(("rw_kk", "rw_ka", "rw_rk", "rw_ln_g", "rw_ln_b")):
                src = io[name][0]
                if name == "rw_rk":
                    src = src.rearrange("h d -> (h d)")
                sp.dma_start(par_rows[14 + 4 * n:18 + 4 * n, :], src.rearrange("(i c) -> i c", c=P))\
                  .then_inc(s_rwc, 16)
            sp.dma_start(shift_rows[:, :], io["state_rwkv_shift"][0].rearrange("s o (i c) -> (s o i) c", c=P))\
              .then_inc(s_rwc, 16)
            sp.dma_start(lora_wa[0:64, :], io["rw_w2"][0]).then_inc(s_rwc, 16)
            sp.dma_start(lora_wa[64:128, :], io["rw_a2"][0]).then_inc(s_rwc, 16)
            sp.dma_start(lora_g[:, :], io["rw_g2"][0]).then_inc(s_rwc, 16)
            sp.dma_start(bias_rows[0:1, :], io["rw_w0"]).then_inc(s_rwc, 16)
            sp.dma_start(bias_rows[32:33, :], io["rw_a0"]).then_inc(s_rwc, 16)
            at = tile_counts(0, True)
            sp.wait_ge(s_rwd, at[0]("clear"))
            for h in range(2):
                sp.dma_start(state_raw[64 * h:64 * h + 64, :, 64 * h:64 * h + 64],
                             io["state_rwkv"][0].rearrange("s (p h) v k -> h v (s p) k", h=2)[h]).then_inc(s_st, 16)
            sp.wait_ge(s_rwa, at[1]("prompt_state"))
            for h in range(2):
                store(sp, io["rs_p"][0, 0].rearrange("(p h) v k -> h v p k", h=2)[h],
                      F4(prompt_state[64 * h:64 * h + 64, :])[:, :, 64 * h:64 * h + 64])
            sp.wait_ge(s_rwa, at[1]("out7"))
            sp.wait_ge(s_rwd, at[0]("s7"))
            for h in range(2):
                store(sp, io["rs_s"][0].rearrange("s (p h) v k -> h v (s p) k", h=2)[h],
                      state_raw[64 * h:64 * h + 64, :, 64 * h:64 * h + 64])

        def pe_rwkv_setup(pe):
            pe.wait_ge(s_rwc, 16 * 13)
            pe.wait_ge(s_ol2, NSEQ + 2)
            pe.transpose(ps[:, 0, 0:34], par_rows[0:34, :], ident[0:34, 0:34])
            pe.transpose(ps[:, 0, 128:240], shift_rows[:, :], ident[0:112, 0:112]).then_inc(s_par, 1)

        def act_rwkv_setup(act):
            act.wait_ge(s_par, 1)
            act.activation(par[:, :], ps[:, 0, 0:34], ACT.Copy)
            act.activation(shift[:, :], ps[:, 0, 128:240], ACT.Copy).then_inc(s_par, 1)

        def dve_rwkv_setup(dve):
            dve.wait_ge(s_rwc, 16 * 13)
            dve.wait_ge(s_par, 2)
            dve.memset(state[0][:, :], 0.0)

        mu, p_kk, p_ka, p_rk, p_lng, p_lnb = (par[:, a:b] for a, b in
                                              ((0, 14), (14, 18), (18, 22), (22, 26), (26, 30), (30, 34)))

        def levels(streams):
            return range(2, 5 if streams else 7)

        def pool_mix_ahead(pool, N, step, tile, streams):
            L = N[3]
            if streams:
                cur = rw[:, :, 1 + SEQ:1 + TOK].rearrange("p i (s t) -> p i s t", t=NEW)
                mix4 = xm[:, :, :].rearrange("p i (s t) -> p i s t", t=NEW)
                pool.tensor_tensor(mix4[:, :, :, 1:NEW], cur[:, :, :, 0:NEW - 1], cur[:, :, :, 1:NEW],
                                   ALU.subtract)
                step(pool.tensor_tensor(mix4[:, :, :, 0], shift[:, :].rearrange("p (s i) -> p i s", s=NSEQ),
                                        cur[:, :, :, 0], ALU.subtract), "diff+")
                now = rw[:, :, 1 + SEQ:1 + TOK]
            else:
                now = rw[:, :, bass.ds(tile * P + 1, P)]
                step(pool.tensor_tensor(xm[:, :, :], rw[:, :, bass.ds(tile * P, P)], now, ALU.subtract), "diff+")
            pool.wait_ge(s_rwp, L("diff"))
            step(pool.tensor_tensor(xm[:, :, :], xm[:, :, :], stretch(mu, 14, P), ALU.mult), "mix+")

        def dve_mix_ahead(dve, N, step, tile, streams):
            now = rw[:, :, 1 + SEQ:1 + TOK] if streams else rw[:, :, bass.ds(tile * P + 1, P)]
            dve.wait_ge(s_rwp, N[3]("mix"))
            step(dve.tensor_tensor(xm[:, :, :], xm[:, :, :], now, ALU.add), "xm+")

        def act_tanh_ahead(act, N, step):
            act.wait_ge(s_rwd, N[0]("xm"))
            step(act.activation(tanh_w[0:64, :], xm[0:64, 12, :], ACT.Tanh), "tanh_w+")
            step(act.activation(sig_g[:, :], xm[:, 13, :], ACT.Tanh, scale=0.5), "tanh_g+")

        def dve_gate_ahead(dve, N, step):
            dve.wait_ge(s_rwa, N[1]("tanh_g"))
            step(dve.tensor_scalar(sig_g[:, :], sig_g[:, :], 0.5, 0.5, ALU.mult, ALU.add), "sig_g+")

        def pe_lora_ahead(pe, N, step):
            pe.wait_ge(s_rwa, N[1]("tanh_w"))
            pe.wait_ge(s_rwd, N[0]("sig_g"))
            for p in range(4):
                c = slice(p * P, (p + 1) * P)
                pe.matmul(ps[:, 0, c], lora_wa[0:64, c], tanh_w[0:64, :], start=True, stop=False)
                pe.matmul(ps[:, 0, c], bias_rows[0:1, c], ones[0:1, :], start=False, stop=True)
                pe.matmul(ps[:, 1, c], lora_wa[64:128, c], xm[64:128, 12, :], start=True, stop=False)
                pe.matmul(ps[:, 1, c], bias_rows[32:33, c], ones[32:33, :], start=False, stop=True)
                mm = pe.matmul(ps[:, 2, c], lora_g[:, c], sig_g[:, :], start=True, stop=True)
            step(mm, "lora+")

        def pe_norm_ahead(pe, N, step):
            pe.wait_ge(s_rwa, N[1]("kk_sq"))
            step(pe.matmul(ps[:, 3, :], two_heads, t7, start=True, stop=True), "norm+")

        def act_sigmoids_ahead(act, N, step):
            act.wait_ge(s_rwe, N[2]("lora"))
            step(act.activation(t0, ps[:, 0, :], ACT.Tanh, scale=0.5), "sig_w+")
            step(act.activation(t5, ps[:, 1, :], ACT.Tanh, scale=0.5), "sig_a+")

        def dve_decay_ahead(dve, N, step, streams):
            D, A, E, L = N
            dve.wait_ge(s_rwd, D("xm"))
            dve.wait_ge(s_rwa, A("sig_w"))
            step(dve.tensor_tensor(F4(t6), xm[:, 4:8, :], stretch(p_kk, 4, P), ALU.mult), "kkr+")
            step(dve.tensor_scalar(t0, t0, DECAY, DECAY, ALU.mult, ALU.add), "e+")
            dve.wait_ge(s_rwd, D("e"))
            step(dve.tensor_tensor_scan(t1, reset_s if streams else reset_p, t0, 0.0, ALU.mult, ALU.add), "scan+")
            dve.wait_ge(s_rwd, D("scan"))
            step(dve.tensor_tensor(t0, t1, t0, ALU.subtract), "eex+")
            dve.wait_ge(s_rwe, E("norm"))
            step(dve.tensor_scalar(t7, ps[:, 3, :], 1e-24, None, ALU.max), "floor+")
            dve.wait_ge(s_rwa, A("sig_a"))
            step(dve.tensor_scalar(t5, t5, 0.5, 0.5, ALU.mult, ALU.add), "a+")
            dve.wait_ge(s_rwd, D("a"))
            step(dve.scalar_tensor_tensor(out=F4(t8), in0=F4(t5), scalar=-1.0, in1=stretch(p_ka, 4, P),
                                          op0=ALU.add, op1=ALU.mult), "ka+")
            dve.wait_ge(s_rwd, D("ka"))
            step(dve.scalar_tensor_tensor(out=F4(t8), in0=F4(t8), scalar=1.0, in1=xm[:, 4:8, :],
                                          op0=ALU.add, op1=ALU.mult), "kmod+")
            dve.wait_ge(s_rwd, D("kmod"))
            step(dve.tensor_tensor(F4(t9), xm[:, 0:4, :], F4(t8), ALU.mult), "rk+")
            dve.wait_ge(s_rwd, D("rk"))
            step(dve.tensor_tensor(F4(t9), F4(t9), stretch(p_rk, 4, P), ALU.mult), "rkr+")
            dve.wait_ge(s_rwa, A("inverse"))
            step(dve.tensor_tensor(t6, t6, t7, ALU.mult), "kk+")
            dve.wait_ge(s_rwd, D("kk"))
            step(dve.scalar_tensor_tensor(out=ar[:, :, 0, :], in0=F4(t6), scalar=-1.0, in1=F4(t4),
                                          op0=ALU.mult, op1=ALU.mult), "abar+")
            step(dve.tensor_tensor(t6, t6, t5, ALU.mult), "kka+")
            step(dve.tensor_tensor(ar[:, :, 1, :], xm[:, 0:4, :], F4(t2), ALU.mult), "rbar+")
            step(dve.tensor_tensor(kT, t8, t3, ALU.mult), "khat+")
            dve.wait_ge(s_rwd, D("kka"))
            step(dve.tensor_tensor(bT, t6, t3, ALU.mult), "bhat+")

        def act_square_ahead(act, N, step):
            act.wait_ge(s_rwd, N[0]("kkr"))
            step(act.activation(t7, t6, ACT.Square), "kk_sq+")
            act.wait_ge(s_rwd, N[0]("floor"))
            step(act.activation(t7, t7, ACT.Ln), "log+")

        def act_decay_ahead(act, N, step):
            act.wait_ge(s_rwd, N[0]("eex"))
            step(act.activation(t2, t1, ACT.Exp, scale=-1.0), "p+")
            step(act.activation(t3, t1, ACT.Exp), "p_inv+")
            step(act.activation(t4, t0, ACT.Exp, scale=-1.0), "p_ex+")
            act.wait_ge(s_rwa, N[1]("log"))
            step(act.activation(t7, t7, ACT.Exp, scale=-0.5), "inverse+")

        def act_gate_ahead(act, step):
            step(act.activation(gate[:, :], ps[:, 2, :], ACT.Copy), "gate+")

        def pool_rwkv_first(pool):
            step, skip_to, skip_rest = stepper(pool, s_rwp, RW_POOL, "ahead")
            pool.wait_ge(s_par, 2)
            skip_to("diff+")
            pool_mix_ahead(pool, tile_counts(0, False), step, 0, False)
            skip_rest()

        def act_rwkv_first(act):
            N = tile_counts(0, False)
            step, skip_to, skip_rest = stepper(act, s_rwa, RW_ACT, "ahead")
            skip_to("tanh_w+")
            act_tanh_ahead(act, N, step)
            skip_to("sig_w+")
            act_sigmoids_ahead(act, N, step)
            skip_to("kk_sq+")
            act_square_ahead(act, N, step)
            skip_to("p+")
            act_decay_ahead(act, N, step)
            skip_to("gate+")
            act_gate_ahead(act, step)
            skip_rest()

        def dve_rwkv_first(dve):
            N = tile_counts(0, False)
            step, skip_to, skip_rest = stepper(dve, s_rwd, RW_DVE, "ahead")
            skip_to("xm+")
            dve_mix_ahead(dve, N, step, 0, False)
            skip_to("sig_g+")
            dve_gate_ahead(dve, N, step)
            skip_to("kkr+")
            dve_decay_ahead(dve, N, step, False)
            skip_rest()

        def pe_rwkv_first(pe):
            step, skip_to, skip_rest = stepper(pe, s_rwe, RW_PE, "ahead")
            skip_to("lora+")
            pe_lora_ahead(pe, tile_counts(0, False), step)
            skip_to("norm+")
            pe_norm_ahead(pe, tile_counts(0, False), step)
            skip_rest()

        def dve_rwkv_tile(dve, tile, streams, to_streams):
            D, A, E, L = tile_counts(tile, streams)
            N = None if streams else tile_counts(tile + 1, to_streams)
            step = stepper(dve, s_rwd, RW_DVE, "streams" if streams else "prompt")[0]

            def own(name):
                dve.wait_ge(s_rwd, D(name))

            if streams:
                own("xm")
                step(dve.memset(state_raw[:, :, :], 0.0), "clear")
            dve.wait_ge(s_rwe, E("bonus"))
            step(dve.tensor_tensor(F4(bonus), F4(ps[:, 4, :]), xm[:, 8:12, :], ALU.mult), "bonus")
            if streams:
                step(dve.tensor_copy(p_end[:, :].rearrange("p (k s) -> p k s", k=4),
                                     F4(t2).rearrange("p k (s t) -> p k s t", t=NEW)[:, :, :, NEW - 1]), "p_end")
            else:
                for c in range(2):
                    step(dve.tensor_tensor(F4(decay_mask[c][:, :]), same(two_heads, 4),
                                           F4(t2)[:, :, 64 * c + 63:64 * c + 64].broadcast_to([P, 4, P]),
                                           ALU.mult), f"p_end{c}")
            own("p_end" if streams else "p_end1")
            for h in range(8):
                dve.wait_ge(s_rwe, E(f"gram{h}"))
                step(dve.tensor_tensor(gram[:, h, :].rearrange("p (a c) -> p a c", a=2),
                                       ps[:, h, :].rearrange("p (a c) -> p a c", a=2),
                                       same(tril_s if streams else tril_p, 2), ALU.mult), f"gram{h}")
            own("gram7")
            step(dve.tensor_tensor(H8(q_inv), gram[:, :, 0:P], same(level_mask(1), 8), ALU.mult), "q_first")
            own("q_first")
            step(dve.tensor_tensor(H8(q_inv), H8(q_inv), same(ident[:, :], 8), ALU.add), "q_unit")
            last = levels(streams)[-1]
            for lv in levels(streams):
                if lv < last:
                    dve.wait_ge(s_rwe, E(f"tn{lv}"))
                    step(dve.tensor_tensor(t_inv, t_inv, flat[:, 4 * 512:6 * 512], ALU.add), f"tn{lv}")
                dve.wait_ge(s_rwe, E(f"qn{lv}"))
                step(dve.tensor_tensor(q_inv, q_inv, flat[:, 6 * 512:8 * 512], ALU.add), f"qn{lv}")
            if not streams:
                dve_mix_ahead(dve, N, step, tile + 1, to_streams)
            if streams:
                for h in range(2):
                    rows = slice(64 * h, 64 * h + 64)
                    dve.wait_ge(s_rwe, E("y"))
                    dve.wait_ge(s_rwa, A("y0"))
                    step(dve.tensor_tensor(
                        F4(y_t[rows, :]), F4(y0_t[rows, :]),
                        flat[rows, 5 * 512:7 * 512].rearrange("p (k h c) -> p k h c", k=4, h=2)[:, :, h, :],
                        ALU.add), f"yt{h}")
            else:
                dve.wait_ge(s_rwe, E("s0"))
                step(dve.tensor_tensor(state[1][:, :], state[0][:, :], ps[:, 2, :], ALU.add), "sadd0")
                own("sadd0")
                step(dve.tensor_tensor(state[1][:, :], state[1][:, :], decay_mask[0][:, :], ALU.mult), "s0")
                dve_gate_ahead(dve, N, step)
                dve.wait_ge(s_rwe, E("s1"))
                step(dve.tensor_tensor(state[0][:, :], state[1][:, :], ps[:, 2, :], ALU.add), "sadd1")
                own("sadd1")
                step(dve.tensor_tensor(state[0][:, :], state[0][:, :], decay_mask[1][:, :], ALU.mult), "s1")
            dve.wait_ge(s_rwe, E("mean"))
            step(dve.scalar_tensor_tensor(out=yc[:, :], in0=ps[:, 7, :], scalar=-1 / HEAD, in1=y_t[:, :],
                                          op0=ALU.mult, op1=ALU.add), "yc")
            if not streams:
                dve_decay_ahead(dve, N, step, to_streams)
            dve.wait_ge(s_rwa, A("y_inverse"))
            step(dve.tensor_tensor(yc[:, :], yc[:, :], ysq[:, :], ALU.mult), "yn")
            own("yn")
            step(dve.tensor_tensor(F4(yc[:, :]), F4(yc[:, :]), stretch(p_lng, 4, P), ALU.mult), "y_gain")
            own("y_gain")
            step(dve.tensor_tensor(F4(yc[:, :]), F4(yc[:, :]), stretch(p_lnb, 4, P), ALU.add), "y_shift")
            own("y_shift")
            step(dve.tensor_tensor(yc[:, :], yc[:, :], bonus, ALU.add), "y_bonus")
            own("y_bonus")
            step(dve.tensor_tensor(yc[:, :], yc[:, :], gate[:, :], ALU.mult), "y_gate")
            own("y_gate")
            dve.wait_ge(s_rwa, A("hi"))
            cols = slice(SEQ, TOK) if streams else bass.ds(tile * P, P)
            step(dve.tensor_tensor(act_lo[:, 4:8, cols], F4(yc[:, :]), act_hi[:, 4:8, cols].bitcast(F32),
                                   ALU.subtract), "lo")
            if streams:
                for h in range(8):
                    rows = slice(64 * (h % 2), 64 * (h % 2) + 64)
                    part = streams_state[rows, :, h // 2, 64 * (h % 2):64 * (h % 2) + 64]
                    dve.wait_ge(s_rwe, E(f"s{h}"))
                    step(dve.tensor_tensor(part, part, ps[rows, h % 2, :].rearrange("p (s v) -> p s v", s=NSEQ),
                                           ALU.add), f"sadd{h}")
                    own(f"sadd{h}")
                    step(dve.tensor_tensor(
                        part, part, p_end[rows, :].rearrange("p (k s o) -> p k s o", k=4, o=1)[:, h // 2]
                        .broadcast_to([64, NSEQ, 64]), ALU.mult), f"s{h}")

        def act_rwkv_tile(act, tile, streams, to_streams):
            D, A, E, L = tile_counts(tile, streams)
            N = None if streams else tile_counts(tile + 1, to_streams)
            step = stepper(act, s_rwa, RW_ACT, "streams" if streams else "prompt")[0]

            if streams:
                act.wait_ge(s_rwe, E("prompt_state"))
                step(act.activation(prompt_state[:, :], ps[:, 7, :], ACT.Copy), "prompt_state")
            act.wait_ge(s_rwe, E("turn"))
            step(act.activation(b_tok, ps[:, 5, :], ACT.Copy), "b_tok")
            step(act.activation(k_tok, ps[:, 6, :], ACT.Copy), "k_tok")
            step(act.activation(v_tok, ps[:, 7, :], ACT.Copy), "v_tok")
            act.wait_ge(s_rwe, E("q_turn"))
            step(act.activation(t_inv, flat[:, 0:1024], ACT.Copy), "t_first")
            for lv in levels(streams):
                for i, part in enumerate("ab"):
                    act.wait_ge(s_rwe, E(f"y1{part}_{lv}"))
                    step(act.activation(y1[:, 512 * i:512 * i + 512], ps[:, 2 + i, :], ACT.Copy), f"y1{part}_{lv}")
            if streams:
                for q in range(NSEQ):
                    act.wait_ge(s_rwe, E(f"turn{q}"))
                    step(act.activation(streams_state[:, q, :, :], F4(ps[:, q, :]), ACT.Copy), f"turn{q}")
                act.wait_ge(s_rwe, E("ra"))
                both = flat[:, 0:1024].rearrange("p (k a c) -> p k a c", k=4, a=2)
                step(act.activation(F4(r1t), both[:, :, 0, :], ACT.Copy), "r1t")
                step(act.activation(F4(y0_t[:, :]), both[:, :, 1, :], ACT.Copy), "y0")
                act.wait_ge(s_rwe, E("r"))
                step(act.activation(r1, ps[:, 2, :], ACT.Copy), "r")
                act.wait_ge(s_rwe, E("u"))
                step(act.activation(u_tok, ps[:, 4, :], ACT.Copy), "u")
            else:
                for c in range(2):
                    act.wait_ge(s_rwe, E(f"r{c}"))
                    rows = slice(64 * c, P)
                    step(act.activation(r1[rows, :], ps[rows, 0, :], ACT.Copy), f"r{c}")
                    act.wait_ge(s_rwe, E(f"u{c}"))
                    rows = slice(64 * c, 64 * c + 64)
                    step(act.activation(u_tok[rows, :], ps[rows, 1, :], ACT.Copy), f"u{c}")
                    if c == 0:
                        act_tanh_ahead(act, N, step)
                act.wait_ge(s_rwe, E("y"))
                for h in range(2):
                    rows = slice(64 * h, 64 * h + 64)
                    step(act.activation(
                        F4(y_t[rows, :]),
                        flat[rows, 3 * 512:5 * 512].rearrange("p (k h c) -> p k h c", k=4, h=2)[:, :, h, :],
                        ACT.Copy), f"yt{h}")
                act_sigmoids_ahead(act, N, step)
            act.wait_ge(s_rwd, D("yc"))
            step(act.activation(ysq[:, :], yc[:, :], ACT.Square), "y_sq")
            if not streams:
                act_square_ahead(act, N, step)
            act.wait_ge(s_rwe, E("var"))
            step(act.activation(ysq[:, :], ps[:, 6, :], ACT.Ln, bias=eps[:, 2:3], scale=1 / HEAD), "y_log")
            if not streams:
                act_decay_ahead(act, N, step)
            act.wait_ge(s_rwa, A("y_log"))
            step(act.activation(ysq[:, :], ysq[:, :], ACT.Exp, scale=-0.5), "y_inverse")
            act.wait_ge(s_rwd, D("y_gate"))
            cols = slice(SEQ, TOK) if streams else bass.ds(tile * P, P)
            step(act.activation(act_hi[:, 4:8, cols], F4(yc[:, :]), ACT.Copy), "hi")
            if not streams:
                act_gate_ahead(act, step)
            if streams:
                for q in range(NSEQ):
                    act.wait_ge(s_rwe, E(f"out{q}"))
                    step(act.activation(state_raw[:, 4 * q:4 * q + 4, :], F4(ps[:, q, :]), ACT.Copy), f"out{q}")

        def pool_rwkv_tile(pool, tile, streams, to_streams):
            D, A, E, L = tile_counts(tile, streams)
            step = stepper(pool, s_rwp, RW_POOL, "streams" if streams else "prompt")[0]
            for lv in levels(streams):
                pool.wait_ge(s_rwd, D("gram7"))
                if lv > 2:
                    pool.wait_ge(s_rwe, E(f"y1b_{lv - 1}"))
                step(pool.tensor_tensor(H8(lt_m), gram[:, :, 0:P], same(level_mask(lv), 8), ALU.mult), f"lt{lv}")
            if not streams:
                pool_mix_ahead(pool, tile_counts(tile + 1, to_streams), step, tile + 1, to_streams)
            if streams:
                for h in range(8):
                    pool.wait_ge(s_rwa, A("u"))
                    pool.wait_ge(s_rwe, E("y") if h < 2 else E(f"s{h - 2}"))
                    mask = stream_rows.rearrange("p (s o) -> p s o", o=1).broadcast_to([P, NSEQ, HEAD])
                    for i, src in enumerate((u_tok, v_tok)):
                        step(pool.tensor_tensor(spread[h % 2][i], same(src[:, HEAD * h:HEAD * h + HEAD], NSEQ), mask,
                                                ALU.mult), f"spread{h}_{i}")

        def pe_rwkv_tile(pe, tile, streams, to_streams):
            D, A, E, L = tile_counts(tile, streams)
            N = None if streams else tile_counts(tile + 1, to_streams)
            step = stepper(pe, s_rwe, RW_PE, "streams" if streams else "prompt")[0]
            if streams:
                pe.wait_ge(s_rwd, tile_counts(3, False)[0]("lo"))
                for p in range(4):
                    mm = pe.transpose(ps[:, 7, p * P:(p + 1) * P], state[0][:, p * P:(p + 1) * P], ident[:, :])
                step(mm, "prompt_state")
            pe.wait_ge(s_rwd, D("rkr"))
            step(pe.matmul(ps[:, 4, :], two_heads, t9, start=True, stop=True), "bonus")
            pe.wait_ge(s_rwd, D("bhat"))
            for bank, src in ((5, F4(bT)), (6, F4(kT)), (7, xm[:, 8:12, :])):
                if streams and bank == 7:
                    pe.wait_ge(s_rwa, A("prompt_state"))
                for p in range(4):
                    mm = pe.transpose(ps[:, bank, p * P:(p + 1) * P], src[:, p, :], ident[:, :])
            step(mm, "turn")
            for h in range(8):
                rows = slice(64 * (h % 2), 64 * (h % 2) + 64)
                if h == 2:
                    pe.wait_ge(s_rwa, A("gate"))
                if h == 3:
                    pe.wait_ge(s_rwd, D("floor"))
                if h == 4:
                    pe.wait_ge(s_rwd, D("bonus"))
                if h == 5:
                    pe.wait_ge(s_rwa, A("v_tok"))
                both = ar[rows, h // 2, :, :].rearrange("p a c -> p (a c)")
                pe.matmul(ps[:, h, 0:256], F4(bT)[rows, h // 2, :], both, start=True, stop=True)
                step(pe.matmul(ps[:, h, 256:512], F4(kT)[rows, h // 2, :], both, start=True, stop=True), f"gram{h}")
            pe.wait_ge(s_rwd, D("q_unit"))
            for h in range(8):
                mm = pe.transpose(flat[:, h * P:(h + 1) * P], H8(q_inv)[:, h, :], ident[:, :])
            step(mm, "q_turn")
            last = levels(streams)[-1]
            for lv in levels(streams):
                pe.wait_ge(s_rwp, L(f"lt{lv}"))
                if lv == 2:
                    pe.wait_ge(s_rwa, A("t_first"))
                else:
                    pe.wait_ge(s_rwd, D(f"tn{lv - 1}"))
                for h in range(8):
                    mm = pe.matmul(flat[:, 1024 + h * P:1024 + (h + 1) * P], H8(lt_m)[:, h, :], H8(t_inv)[:, h, :],
                                   start=True, stop=True)
                    if h == 3:
                        step(mm, f"y1a_{lv}")
                step(mm, f"y1b_{lv}")
                if lv > 2:
                    pe.wait_ge(s_rwd, D(f"qn{lv - 1}"))
                for h in range(8 if lv < last else 0):
                    if h % 4 == 0:
                        pe.wait_ge(s_rwa, A(f"y1{'ab'[h // 4]}_{lv}"))
                    mm = pe.matmul(flat[:, 2048 + h * P:2048 + (h + 1) * P], H8(q_inv)[:, h, :],
                                   H8(y1)[:, h, :], start=True, stop=True)
                if lv < last:
                    step(mm, f"tn{lv}")
                for h in range(8):
                    if h % 4 == 0:
                        pe.wait_ge(s_rwa, A(f"y1{'ab'[h // 4]}_{lv}"))
                    mm = pe.matmul(flat[:, 3072 + h * P:3072 + (h + 1) * P], H8(y1)[:, h, :],
                                   H8(q_inv)[:, h, :], start=True, stop=True)
                step(mm, f"qn{lv}")
            pe.wait_ge(s_rwd, D(f"qn{last}"))

            def y_terms(bank, sources):
                for h in range(8):
                    c = (h // 2 % 2) * 256 + h % 2 * P
                    out = ps[:, bank + h // 4, c:c + P]
                    pair = slice(h // 2 * P, h // 2 * P + P)
                    pe.matmul(out, u_tok[:, pair], gram[:, h, P:2 * P], start=True, stop=False)
                    mm = pe.matmul(out, v_tok[:, pair], gram[:, h, 3 * P:4 * P], start=False, stop=not sources)
                    for n, s in enumerate(sources):
                        mm = pe.matmul(out[:, 64 * n:64 * n + 64], s[:, pair], ar[:, h // 2, 1, 64 * n:64 * n + 64],
                                       start=False, stop=(n == 1))
                return mm

            if streams:
                pe.wait_ge(s_st, 32)
                for q in range(NSEQ):
                    for p in range(4):
                        mm = pe.transpose(ps[:, q, p * P:(p + 1) * P], state_raw[:, 4 * q + p, :], ident[:, :])
                    step(mm, f"turn{q}")
                for q in range(NSEQ):
                    pe.wait_ge(s_rwa, A(f"turn{max(q, 1)}"))
                    for p in range(4):
                        for a in range(2):
                            c = p % 2 * 256 + a * P + NEW * q
                            mm = pe.matmul(ps[:, p // 2, c:c + NEW], streams_state[:, q, p, :],
                                           ar[:, p, a, NEW * q:NEW * q + NEW], start=True, stop=True)
                step(mm, "ra")
                pe.wait_ge(s_rwa, A("r1t"))
                for h in range(8):
                    if h % 2 == 0:
                        pair = slice(h * HEAD, h * HEAD + P)
                        pe.matmul(ps[:, 2, pair], F4(r1t)[:, h // 2, :], ident[:, :], start=True, stop=False)
                    mm = pe.matmul(ps[:, 2, h * HEAD:(h + 1) * HEAD], gram[:, h, 256:384],
                                   v_tok[:, h * HEAD:(h + 1) * HEAD], start=False, stop=(h % 2 == 1))
                step(mm, "r")
                pe.wait_ge(s_rwa, A("r"))
                for h in range(8):
                    mm = pe.matmul(ps[:, 4, h * HEAD:(h + 1) * HEAD], H8(q_inv)[:, h, :],
                                   r1[:, h * HEAD:(h + 1) * HEAD], start=True, stop=True)
                step(mm, "u")
                pe.wait_ge(s_rwa, A("u"))
                step(y_terms(5, ()), "y")
                pe.wait_ge(s_rwd, D("yt1"))
            else:
                for c in range(2):
                    if c:
                        pe.wait_ge(s_rwd, D("s0"))
                    for h in range(8):
                        if h % 2 == 0:
                            pair = slice(h * HEAD, h * HEAD + P)
                            pe.matmul(ps[:, 0, pair], ar[:, h // 2, 0, :], state[c][:, pair], start=True, stop=False)
                        mm = pe.matmul(ps[:, 0, h * HEAD:(h + 1) * HEAD], gram[:, h, 256:384],
                                       v_tok[:, h * HEAD:(h + 1) * HEAD], start=False, stop=(h % 2 == 1))
                    step(mm, f"r{c}")
                    pe.wait_ge(s_rwa, A(f"r{c}"))
                    for h in range(8):
                        mm = pe.matmul(ps[:, 1, h * HEAD:(h + 1) * HEAD], H8(q_inv)[:, h, :],
                                       r1[:, h * HEAD:(h + 1) * HEAD], start=True, stop=True)
                    step(mm, f"u{c}")
                    pe.wait_ge(s_rwa, A(f"u{c}"))
                    if c:
                        step(y_terms(3, state), "y")
                    rows = slice(64 * c, 64 * c + 64)
                    for p in range(4):
                        pair = slice(p * P, (p + 1) * P)
                        pe.matmul(ps[:, 2, pair], b_tok[rows, pair], u_tok[rows, pair], start=True, stop=False)
                        mm = pe.matmul(ps[:, 2, pair], k_tok[rows, pair], v_tok[rows, pair], start=False, stop=True)
                    step(mm, f"s{c}")
                pe.wait_ge(s_rwa, A("yt1"))
            step(pe.matmul(ps[:, 7, :], two_heads, y_t[:, :], start=True, stop=True), "mean")
            if not streams:
                pe.wait_ge(s_rwd, D("sadd1"))
                pe_lora_ahead(pe, N, step)
            pe.wait_ge(s_rwa, A("y_sq"))
            step(pe.matmul(ps[:, 6, :], two_heads, ysq[:, :], start=True, stop=True), "var")
            if not streams:
                pe_norm_ahead(pe, N, step)
            if streams:
                pe.wait_ge(s_rwa, A("y_inverse"))
                for h in range(8):
                    pe.wait_ge(s_rwp, L(f"spread{h}_1"))
                    if h >= 2:
                        pe.wait_ge(s_rwd, D(f"sadd{h - 2}"))
                    pair = slice(h // 2 * P, h // 2 * P + P)
                    for i, w in enumerate((b_tok, k_tok)):
                        mm = pe.matmul(ps[:, h % 2, :], w[:, pair], spread[h % 2][i].rearrange("p s v -> p (s v)"),
                                       start=(i == 0), stop=(i == 1))
                    step(mm, f"s{h}")
                pe.wait_ge(s_rwd, D("s7"))
                for q in range(NSEQ):
                    for p in range(4):
                        mm = pe.transpose(ps[:, q, p * P:(p + 1) * P], streams_state[:, q, p, :], ident[:, :])
                    step(mm, f"out{q}")

        def rwkv(eng, tile):
            with eng.Fori(0, 3) as t:
                tile(eng, t, False, False)
            tile(eng, 3, False, True)
            tile(eng, 4, True, False)

        def sp_mixer_out(sp, stage, w, load_next, first=0, last=OUT_N * KD):
            r0 = before(stage, 1)
            for i in range(first, last):
                n, k = i // KD, i % KD
                if i == OUT_N * KD - LOAD_AHEAD:
                    load_next(sp)
                sp_row(sp, i, r0, r0 // 2, w[k * P:(k + 1) * P, n * 512:(n + 1) * 512])

        def pe_mixer_out(pe, stage):
            pe_rows(pe, KD, OUT_N, before(stage, 1), before(stage, 2), act_hi, act_lo, lambda k: None)

        def act_mixer_out(act, stage):
            r0 = before(stage, 1)
            for i in range(OUT_N * KD):
                act_split_row(act, i, r0, r0 // 2)
                if i == OUT_N * KD - SPLIT_AHEAD and stage == "even_out":
                    split_ahead(act, act_split_pair, before(stage, 0))

        def dve_mixer_out(dve, stage):
            r0, g0 = before(stage, 1), before(stage, 2)

            def evict(g, t):
                wait_output(dve, g, t, KD, r0, g0)
                bank = (ODD_BANKS if g % 2 else EVEN_BANKS)[t]
                dve.tensor_copy(y[:, t, g * 512:(g + 1) * 512], ps[:, bank, :]).then_inc(s_evict, 1)

            def split(i):
                dve_split_row(dve, i, r0)
                if i == OUT_N * KD - SPLIT_AHEAD and stage == "even_out":
                    split_ahead(dve, dve_split_pair, before(stage, 0))

            splits_and_outputs(KD, OUT_N, split, evict)

        N_GPAIR = STAGES["gm_in"][0]
        GROUPS = D // P
        spatial_loads = 4 + 2 * NSEQ
        gm_in = io["gm_w_in"][0]

        def sp_gmlp(sp):
            n0, r0, g0 = (before("gm_in", i) for i in range(3))
            w = gm_in.rearrange("(k p) n -> p k n", p=P)
            sp.wait_ge(s_evict, g0 * TT + 1)
            sp.dma_start(ws[:, :, :], io["gm_w_s"][0].rearrange("g t s -> t g s")).then_inc(s_gm, 16)
            sp.wait_ge(s_ws0, 1)
            for b in range(NSEQ):
                at = slice(NEW * b, NEW * b + NEW)
                sp.dma_start(ws_new[at, :, at], io["gm_w_s"][0, :, 0:NEW, 0:NEW].rearrange("g t s -> t g s"))\
                  .then_inc(s_gm, 16)
                sp.dma_start(bs_new[:, :, at], io["gm_b_s"][0:1, :, 0:NEW]).then_inc(s_gm, 16)
            sp.dma_start(bs[:, :, :], io["gm_b_s"][0:1]).then_inc(s_gm, 16)
            sp.dma_start(ln_g[:, :], io["gm_ln_g"].broadcast_to([P, D])).then_inc(s_gm, 16)
            sp.dma_start(ln_b[:, :], io["gm_ln_b"].broadcast_to([P, D])).then_inc(s_gm, 16)
            with sp.Fori(1, N_GPAIR) as j:
                sp_pair(sp, n0 + j, lambda c: w[:, :, bass.ds(j * 256 + c * P, P)])
            for i in range(OUT_N * KD):
                n, k = i // KD, i % KD
                sp_row(sp, i, r0, r0 // 2, gm_in[k * P:(k + 1) * P, D + n * 512:D + (n + 1) * 512])

        def pe_gmlp(pe):
            n0, r0, g0 = (before("gm_in", i) for i in range(3))
            pe_first_pair(pe, n0, 5 * TT)
            with pe.Fori(1, N_GPAIR) as j:
                pe_pair(pe, n0 + j)
            pe.wait_ge(s_gm, 16 * spatial_loads)
            for g in range(GROUPS):
                pe.transpose(ps[:, 4 + g // 4, g % 4 * P:(g % 4 + 1) * P], ws[:, g, :], ident[:, :])
                mm = pe.transpose(ps[:, 6 + g // 4, g % 4 * P:(g % 4 + 1) * P], ws_new[:, g, :], ident[:, :])
            mm.then_inc(s_wt, 1)
            for h in range(2):
                pe.wait_ge(s_pair_read[h], n0 + N_GPAIR + 1)
            pe.wait_ge(s_wt_read, 4)
            pe_rows(pe, KD, OUT_N, r0, g0, act_hi, act_lo, lambda k: None)
            pe.wait_ge(s_evict, (g0 + OUT_N) * TT + 1)
            for t in range(TT):
                w, b = (ws_t, bs) if t < TT - 1 else (ws_new_t, bs_new)
                pe.wait_ge(s_v, t + 1)
                if t >= 4:
                    pe.wait_ge(s_gated, t - 3)
                for g in range(GROUPS):
                    bank = t % 4 * 2 + g // 4
                    if g % 4 == 0:
                        pe.matmul(ps[:, bank, :], ones[0:1, :], b[0:1, g:g + 4, :].rearrange("o g t -> o (g t)"),
                                  start=True, stop=False)
                    mm = pe.matmul(ps[:, bank, g % 4 * P:(g % 4 + 1) * P], y[:, t, g * P:(g + 1) * P], w[:, g, :],
                                   start=False, stop=(g % 4 == 3))
                mm.then_inc(s_spatial, 1)

        def act_gmlp(act):
            n0, r0, g0 = (before("gm_in", i) for i in range(3))

            def tile(j, last):
                for c in range(2):
                    act.wait_ge(s_pair_mm[c], n0 + j + 2)
                    act.activation(halves(u_cols, 2 * j + c), wide(2 * c), ACT.Gelu).then_inc(s_pair_read[c], 1)
                    if not last:
                        act_split_pair(act, c, n0 + j + 1)

            with act.Fori(0, N_GPAIR - 1) as j:
                tile(j, False)
            act_split_row(act, 0, r0, r0 // 2)
            act_split_row(act, 1, r0, r0 // 2)
            tile(N_GPAIR - 1, True)

            def split(i):
                if i > 1:
                    act_split_row(act, i, r0, r0 // 2)

            def evict(g, t):
                wait_output(act, g, t, KD, r0, g0)
                act.activation(y[:, t, g * 512:(g + 1) * 512], ps[:, (ODD_BANKS if g % 2 else EVEN_BANKS)[t], :],
                               ACT.Gelu, accum_out=ln_stat[:, g, t:t + 1]).then_inc(s_evict, 1)

            splits_and_outputs(KD, OUT_N, split, evict)
            act.wait_ge(s_sq[0], 10 * 4)
            for t in range(TT):
                act.wait_ge(s_mean, t + 1)
                if t:
                    act.wait_ge(s_vsq, t)
                act.activation(squares[0], y[:, t, :], ACT.Square, bias=ln_stat[:, 2, t:t + 1],
                               accum_out=ln_stat[:, 3, t:t + 1]).then_inc(s_vsq, 1)
            act.wait_ge(s_vsq, TT)
            act.activation(ln_stat[:, 4, :], ln_stat[:, 3, :], ACT.Sqrt, bias=eps[:, 3:4], scale=1 / D)\
               .then_inc(s_vroot, 1)
            for t in range(TT):
                act.wait_ge(s_gated, t + 1)
                act.activation(act_hi[:, :, t * P:(t + 1) * P], gated[t % 2], ACT.Copy).then_inc(s_ghi, 1)

        def dve_gmlp(dve):
            n0, r0, g0 = (before("gm_in", i) for i in range(3))
            with dve.Fori(0, N_GPAIR - 1) as j:
                dve_split_pair(dve, 0, n0 + j + 1)
                dve_split_pair(dve, 1, n0 + j + 1)
            dve_split_row(dve, 0, r0)
            dve_split_row(dve, 1, r0)
            dve.memset(ws_t[64:P, :, 0:64], 0.0).then_inc(s_wt_read, 1)
            dve.wait_ge(s_wt, 1)
            chunk = ps[:, 4:6, :].rearrange("p a (g t) -> p (a g) t", g=4)
            dve.tensor_copy(ws_t[0:64, :, :], chunk[0:64, :, :]).then_inc(s_wt_read, 1)
            dve.tensor_copy(ws_t[64:P, :, 64:P], chunk[64:P, :, 64:P]).then_inc(s_wt_read, 1)
            dve.tensor_copy(ws_new_t[:, :, :], ps[:, 6:8, :].rearrange("p a (g t) -> p (a g) t", g=4))\
               .then_inc(s_wt_read, 1)
            for i in range(2, OUT_N * KD):
                dve_split_row(dve, i, r0)
            for t in range(TT):
                dve.wait_ge(s_evict, (g0 + 1) * TT + t + 2)
                dve.tensor_scalar(ln_stat[:, 2, t:t + 1], ln_stat[:, 0, t:t + 1], ln_stat[:, 1, t:t + 1], -1 / D,
                                  ALU.add, ALU.mult).then_inc(s_mean, 1)
            dve.wait_ge(s_vroot, 1)
            dve.wait_ge(s_mean, TT)
            dve.reciprocal(ln_stat[:, 5, :], ln_stat[:, 4, :]).then_inc(s_vinv, 1)
            dve.wait_ge(s_gm, 16 * spatial_loads)
            dve.wait_ge(s_vinv, 1)
            for s in range(TT + 2):
                if s < TT:
                    v = y[:, s, :]
                    dve.scalar_tensor_tensor(out=v, in0=v, scalar=ln_stat[:, 2, s:s + 1], in1=ln_g[:, :],
                                             op0=ALU.add, op1=ALU.mult).then_inc(s_vgain, 1)
                    dve.wait_ge(s_vgain, s + 1)
                    dve.scalar_tensor_tensor(out=v, in0=v, scalar=ln_stat[:, 5, s:s + 1], in1=ln_b[:, :],
                                             op0=ALU.mult, op1=ALU.add).then_inc(s_v, 1)
                if 0 <= s - 1 < TT:
                    t = s - 1
                    dve.wait_ge(s_spatial, t + 1)
                    if t >= 2:
                        dve.wait_ge(s_glo, t - 1)
                    dve.tensor_tensor(gated[t % 2], u_cols[:, :, t * P:(t + 1) * P],
                                      flat[:, t % 4 * 1024:t % 4 * 1024 + 1024].rearrange("p (g t) -> p g t", g=GROUPS),
                                      ALU.mult).then_inc(s_gated, 1)
                if 0 <= s - 2 < TT:
                    t = s - 2
                    dve.wait_ge(s_ghi, t + 1)
                    cols = slice(t * P, (t + 1) * P)
                    dve.tensor_tensor(act_lo[:, :, cols], gated[t % 2], act_hi[:, :, cols].bitcast(F32),
                                      ALU.subtract).then_inc(s_glo, 1)
            dve.wait_ge(s_glo, TT)
            dve.wait_ge(s_new_v, 16)

        def store(sp, dst, src):
            sp.dma_start(dst, src).then_inc(s_store, 16)
            stores.append(16)

        stores = []

        @block.sync
        def _(sp):
            sp_norm_gains(sp, 0)
            for t in range(TT - 1):
                sp.dma_start(x[:, t, :], io["x_prompt"][0, t * P:(t + 1) * P, :]).then_inc(s_x[t], 16)
            sp.dma_start(x[:, 4, :], io["x_sample"].rearrange("s t d -> (s t) d")).then_inc(s_x[TT - 1], 16)
            first_pair_of("ffn0")(sp)
            sp_ffn(sp, 0, first_pair_of("even_in"))
            sp_norm_gains(sp, 1)
            sp_even_in(sp)
            sp_even_outputs(sp)
            sp_streams(sp)
            sp_mixer_out(sp, "even_out", io["even_w_out"][0], None, 0, 2)
            sp_rwkv(sp)
            sp_mixer_out(sp, "even_out", io["even_w_out"][0], first_pair_of("ffn1"), 2)
            sp_norm_gains(sp, 2)
            sp.wait_ge(s_store, sum(stores))
            sp_ffn(sp, 1, first_pair_of("ffn2"))
            sp_norm_gains(sp, 3)
            sp_ffn(sp, 2, first_pair_of("gm_in"))
            sp_norm_gains(sp, 4)
            sp_gmlp(sp)
            sp.wait_ge(s_v, TT)
            sp.dma_start(io["gv_s"][0].rearrange("s t d -> (s t) d"), y[:, TT - 1, :]).then_inc(s_new_v, 16)
            sp_mixer_out(sp, "gm_out", io["gm_w_out"][0], first_pair_of("ffn3"))
            sp_norm_gains(sp, 5)
            sp_ffn(sp, 3, lambda sp: None)
            sp_norm_gains(sp, 6)
            for t in range(TT):
                sp.wait_ge(s_xnew, 5 * (NORMS - 1) + t + 1)
                if t < TT - 1:
                    store(sp, io["y_prompt"][0, t * P:(t + 1) * P, :], x[:, t, :])
                else:
                    store(sp, io["y_sample"].rearrange("s t d -> (s t) d"), x[:, t, :])
            sp.wait_ge(s_store, sum(stores))

        @block.gpsimd
        def _(pool):
            pool.memset(ident[:, :], 0.0).then_inc(s_const, 1)
            pool.memset(eps[:, 0:1], RMS_EPS).then_inc(s_const, 1)
            pool.memset(eps[:, 2:3], GN_EPS)
            pool.memset(eps[:, 3:4], LN_EPS)
            pool.memset(ones[:, :], 1.0)
            pool.memset(eps[:, 1:2], 0.0).then_inc(s_const, 1)
            pool.wait_ge(s_const, 3)
            pool.affine_select(out=ident[:, :], in_=ident[:, :], compare_op=ALU.not_equal, fill=1.0,
                               base=0, pattern=[[-1, P]], channel_multiplier=1).then_inc(s_const, 1)
            pool.sem_inc(s_rwp, 1)
            pool.sem_inc(s_pm, 2)
            pool.sem_inc(s_pm2, 2)
            pool_norm(pool, 0)
            pool_norm(pool, 1)
            pool_prompt(pool)
            pool_streams(pool)
            pool_rwkv_first(pool)
            rwkv(pool, pool_rwkv_tile)
            for m in (2, 3, 4):
                pool_norm(pool, m)
            pool.memset(ws_new[:, :, :], 0.0).then_inc(s_ws0, 1)
            pool_norm(pool, 5)
            pool_norm(pool, 6)

        @block.scalar
        def _(act):
            act.sem_inc(s_pair_read[0], 1)
            act.sem_inc(s_rwa, 1)
            for s in (s_ex, s_ptr, s_oh, s_kta, s_cs, s_q2, s_ex2, s_ptr2, s_oh2):
                act.sem_inc(s, 2)
            act_norm(act, 0, 1, 0)
            split_ahead(act, act_split_pair, 0)
            act_ffn(act, 0)
            act_norm(act, 1, 0.5, 4)
            act_even_in(act)
            act_prompt(act)
            act_streams(act)
            act_rwkv_setup(act)
            act_rwkv_first(act)
            rwkv(act, act_rwkv_tile)
            act_mixer_out(act, "even_out")
            act_norm(act, 2, 1, before("ffn1", 2))
            act_ffn(act, 1)
            act_norm(act, 3, 0.5, before("ffn2", 2))
            act_ffn(act, 2)
            act_norm(act, 4, 0.5, before("gm_in", 2))
            act_gmlp(act)
            act_mixer_out(act, "gm_out")
            act_norm(act, 5, 1, before("ffn3", 2))
            act_ffn(act, 3)
            act_norm(act, 6, 0.5, before("end", 2))

        @block.vector
        def _(dve):
            dve.sem_inc(s_rwd, 1)
            dve.sem_inc(s_pair_lo[0], 1)
            dve.sem_inc(s_pair_lo[1], 1)
            dve.sem_inc(s_pair_read[1], 1)
            dve.sem_inc(s_hid_lo, 1)
            dve.sem_inc(s_row_lo, 2)
            dve.sem_inc(s_evict, 1)
            for s in (s_nm, s_ol, s_ktd, s_nm2, s_ol2):
                dve.sem_inc(s, 2)
            dve_norm(dve, 0)
            split_ahead(dve, dve_split_pair, 0)
            dve_ffn(dve, 0)
            dve_norm(dve, 1, 0.5)
            dve_even_in(dve)
            dve_even_outputs(dve)
            dve_prompt_c(dve)
            dve_prompt(dve)
            dve_streams(dve)
            dve_rwkv_setup(dve)
            dve_rwkv_first(dve)
            rwkv(dve, dve_rwkv_tile)
            dve.wait_ge(s_rwd, tile_counts(0, True)[0]("s7"))
            dve_mixer_out(dve, "even_out")
            dve_norm(dve, 2)
            dve_ffn(dve, 1)
            dve_norm(dve, 3, 0.5)
            dve_ffn(dve, 2)
            dve_norm(dve, 4, 0.5)
            dve_gmlp(dve)
            dve_mixer_out(dve, "gm_out")
            dve_norm(dve, 5)
            dve_ffn(dve, 3)
            dve_norm(dve, 6, 0.5)

        @block.tensor
        def _(pe):
            pe.sem_inc(s_rwe, 1)
            pe.sem_inc(s_pair_mm[0], 1)
            pe.sem_inc(s_pair_mm[1], 1)
            pe.sem_inc(s_row_mm, 2)
            for s in (s_sc, s_pt, s_o, s_tk, s_c2, s_sc2, s_pt2, s_o2):
                pe.sem_inc(s, 2)
            pe_norm(pe, 0, 0)
            pe_ffn(pe, 0, 1 * TT)
            pe_norm(pe, 1, 4)
            pe_even_in(pe)
            pe.wait_ge(s_last, 2)
            pe_even_outputs(pe)
            pe_prompt_c(pe)
            pe_prompt(pe)
            pe_streams(pe)
            pe_rwkv_setup(pe)
            pe_rwkv_first(pe)
            rwkv(pe, pe_rwkv_tile)
            pe.wait_ge(s_rwa, tile_counts(0, True)[1]("out7"))
            pe.wait_ge(s_rwd, tile_counts(0, True)[0]("s7"))
            pe_mixer_out(pe, "even_out")
            pe_norm(pe, 2, before("ffn1", 2))
            pe_ffn(pe, 1, 3 * TT)
            pe_norm(pe, 3, before("ffn2", 2))
            pe_ffn(pe, 2, 4 * TT)
            pe_norm(pe, 4, before("gm_in", 2))
            pe_gmlp(pe)
            pe.wait_ge(s_glo, TT)
            pe_mixer_out(pe, "gm_out")
            pe_norm(pe, 5, before("ffn3", 2))
            pe_ffn(pe, 3, 6 * TT)


OUTS = {"y_prompt": (1, SEQ, D), "y_sample": (NSEQ, NEW, D), "fk_p": (1, 1, SEQ, FOXH, HEAD),
        "fv_p": (1, 1, SEQ, FOXH, HEAD), "fl_p": (1, 1, SEQ, FOXH), "rs_p": (1, 1, FOXH, HEAD, HEAD),
        "rsh_p": (1, 1, 1, 14 * P), "fk_s": (1, NSEQ, NEW, FOXH, HEAD), "fv_s": (1, NSEQ, NEW, FOXH, HEAD),
        "fl_s": (1, NSEQ, NEW, FOXH), "rs_s": (1, NSEQ, FOXH, HEAD, HEAD), "rsh_s": (1, NSEQ, 1, 14 * P),
        "gv_s": (1, NSEQ, NEW, D)}


def att_constants():
    import numpy as np

    s, t = np.arange(P)[:, None], np.arange(P)[None, :]
    c = np.zeros((P, ATT_N), np.float32)
    c[:, ATT_AT["tri_ones"]] = np.concatenate([s <= t, np.ones((P, 512 - P), bool)], 1)
    c[:, ATT_AT["tri_streams"]] = (s // NEW == t // NEW) & (s <= t)
    c[:, ATT_AT["causal"]] = np.where(t <= s, 0, -1e30)
    c[0:FOXH, ATT_AT["sel8"]] = np.eye(FOXH)
    c[:, ATT_AT["minus_ones"]] = -1
    c[0:FOXH, ATT_AT["minus_heads"]] = np.where(np.arange(FOXH)[:, None] == t // NEW, -1, 0)
    new = [np.where((t // NEW == b) & (t % NEW <= s % NEW), 0, -1e30) for b in range(NSEQ)]
    return c, np.concatenate(new, 1).astype(np.float32)


def rw_constants():
    import numpy as np

    s, t = np.arange(P)[:, None], np.arange(P)[None, :]
    c = np.zeros((P, RWC_N), np.float32)
    for name, chunk in (("tril_p", 64), ("tril_s", NEW)):
        block = s // chunk == t // chunk
        c[:, RWC_AT[name]] = np.concatenate([block & (s < t), block & (s <= t)], 1)
    c[:, RWC_AT["levels"]] = np.concatenate(
        [(s >> lv == t >> lv) & (s >> (lv - 1) & 1 == 0) & (t >> (lv - 1) & 1 == 1) for lv in range(1, 7)], 1)
    c[:, RWC_AT["two_heads"]] = s // HEAD == t // HEAD
    for name, chunk in (("reset_p", 64), ("reset_s", NEW)):
        c[:, RWC_AT[name]] = np.arange(512) % chunk != 0
    c[:, RWC_AT["stream_rows"]] = s // NEW == np.arange(NSEQ)
    return c


_INS = ["x_prompt", "x_sample", "cache_fox_k", "cache_fox_v", "cache_fox_logf", "state_rwkv", "state_rwkv_shift",
        "norm_g", "ffn_w_in", "ffn_w_out", "even_w_in", "fox_bf", "rw_mu", "rw_w0", "rw_w2", "rw_a0", "rw_a2",
        "rw_g2", "rw_kk", "rw_ka", "rw_rk", "rw_ln_g", "rw_ln_b", "even_w_out", "gm_w_in", "gm_ln_g", "gm_ln_b",
        "gm_w_s", "gm_b_s", "gm_w_out"]


def kernel(**inputs):
    import numpy as _np
    import concourse.bacc as _bacc
    from concourse import mybir as _mybir
    from concourse.bass_utils import run_bass_kernel_spmd as _run

    nc = _bacc.Bacc("TRN2", target_bir_lowering=False, num_devices=1, dynamic_dma_scratch_size=1024)
    given = {name: _np.ascontiguousarray(inputs[name]) for name in _INS}
    given["att_const"], given["new_mask"] = att_constants()
    given["rw_const"] = rw_constants()
    arrays, io = {}, {}
    for name, a in given.items():
        arrays[f"in_{name}_dram"] = a
        io[name] = nc.dram_tensor(f"in_{name}_dram", a.shape, _mybir.dt.from_np(a.dtype), kind="ExternalInput").ap()
    for i, (name, shape) in enumerate(OUTS.items()):
        io[name] = nc.dram_tensor(f"out_{i}_dram", shape, _mybir.dt.float32, kind="ExternalOutput").ap()
    build(nc, io)
    r = _run(nc, [arrays], core_ids=[0])
    return tuple(r.results[0][f"out_{i}_dram"] for i in range(len(OUTS)))
```
